# Optimizing a Trainium2 kernel written in Bass

```python
import math
import jax
import jax.numpy as jnp
from jax import lax
import numpy as np

D_MODEL = 1024
BATCH = 1
SEQ = 256
DEPTH = 2

N_MIXERS = 4
GRID_W = 64
CONV_K = 5
NORM_EPS = 1e-6

GDN_HEADS = 8
GDN_DK = 128
GDN_DV = 128
GDN_CHUNK = 64
GDN_QK = GDN_HEADS * GDN_DK
GDN_V = GDN_HEADS * GDN_DV
GDN_CONV_CH = 2 * GDN_QK + GDN_V
GDN_IN = GDN_CONV_CH + GDN_V + 4 * GDN_HEADS

SSD_INNER = 2 * D_MODEL
SSD_HEADDIM = 64
SSD_HEADS = SSD_INNER // SSD_HEADDIM
SSD_GROUPS = 4
SSD_STATE = 128
SSD_CHUNK = 64
SSD_BC = SSD_GROUPS * SSD_STATE
SSD_CONV_CH = SSD_INNER + 2 * SSD_BC
SSD_IN = SSD_INNER + SSD_CONV_CH + 2 * SSD_HEADS

SWA_HEADS = 16
SWA_KV_HEADS = 4
SWA_HEADDIM = 64
SWA_WINDOW = 128
SWA_IN = (SWA_HEADS + 2 * SWA_KV_HEADS) * SWA_HEADDIM
SWA_OUT = SWA_HEADS * SWA_HEADDIM
ROPE_THETA = 10000.0

NA_HEADS = 16
NA_HEADDIM = 64
NA_ROWS = 8
NA_COLS = 16
NA_WIDTH = NA_HEADS * NA_HEADDIM
NA_IN = 3 * NA_WIDTH

PEER_HEADS = 8
PEER_NKEYS = 128
PEER_EXPERTS = PEER_NKEYS * PEER_NKEYS
PEER_QDIM = 256
PEER_HALF = PEER_QDIM // 2
PEER_TOPK = 16
PEER_BLOCK = 128

kernel_name = "hybrid_gdn_ssd_swa_natten_peer_encoder"

def _rmsnorm(x, w):
    xf = x.astype(jnp.float32)
    y = xf * lax.rsqrt(jnp.mean(xf * xf, axis=-1, keepdims=True) + NORM_EPS)
    return (y * w.astype(jnp.float32)).astype(x.dtype)

def _l2norm(t):
    t = t.astype(jnp.float32)
    return t * lax.rsqrt(jnp.sum(t * t, axis=-1, keepdims=True) + NORM_EPS)

def _dwconv(x, w):
    ch = w.shape[1]
    return lax.conv_general_dilated(
        x, w[:, None, :].astype(x.dtype), window_strides=(1,),
        padding=[(CONV_K // 2, CONV_K // 2)],
        dimension_numbers=('NWC', 'WIO', 'NWC'), feature_group_count=ch)

def _flip(t):
    return jnp.flip(t, axis=1)

def _gated_delta_rule(q, k, v, g, beta):
    Bsz, T, H, DK = q.shape
    DV = v.shape[-1]
    C = GDN_CHUNK
    NC = T // C

    def chunks(a):
        a = a.astype(jnp.float32).reshape(Bsz, NC, C, H, *a.shape[3:])
        return jnp.moveaxis(a, (1, 3), (0, 2))

    q = chunks(q) * DK ** -0.5
    k, v, g, beta = chunks(k), chunks(v), chunks(g), chunks(beta)
    gc = jnp.cumsum(g, axis=-1)
    incl = jnp.tril(jnp.ones((C, C), bool))
    decay = jnp.exp(jnp.where(incl, gc[..., :, None] - gc[..., None, :], -jnp.inf))
    kb = k * beta[..., None]
    lower = jnp.tril(jnp.einsum('nbhid,nbhjd->nbhij', kb, k) * decay, -1)
    eye = jnp.eye(C, dtype=jnp.float32)
    rhs = jnp.concatenate([v * beta[..., None], kb * jnp.exp(gc)[..., None]], axis=-1)
    sol = lax.linalg.triangular_solve(jnp.broadcast_to(eye + lower, lower.shape), rhs,
                                      left_side=True, lower=True, unit_diagonal=True)
    u, w = sol[..., :DV], sol[..., DV:]
    qk = jnp.einsum('nbhid,nbhjd->nbhij', q, k) * decay

    def step(S, inp):
        q_c, k_c, u_c, w_c, qk_c, g_c = inp
        v_new = u_c - jnp.einsum('bhck,bhkv->bhcv', w_c, S)
        o = (jnp.einsum('bhck,bhkv->bhcv', q_c * jnp.exp(g_c)[..., None], S)
             + jnp.einsum('bhij,bhjv->bhiv', qk_c, v_new))
        g_last = g_c[..., -1:]
        S = (S * jnp.exp(g_last)[..., None]
             + jnp.einsum('bhck,bhcv->bhkv', k_c * jnp.exp(g_last - g_c)[..., None], v_new))
        return S, o

    S0 = jnp.zeros((Bsz, H, DK, DV), jnp.float32)
    _, o = lax.scan(step, S0, (q, k, u, w, qk, gc))
    return jnp.moveaxis(o, (0, 2), (1, 3)).reshape(Bsz, T, H, DV)

def _mixer_gdn(h, w_in, conv_w, a_log, dt_bias, norm_w, w_out):
    Bsz, T, _ = h.shape
    H = GDN_HEADS
    proj = h @ w_in
    qkv = jax.nn.silu(_dwconv(proj[..., :GDN_CONV_CH], conv_w))
    z = proj[..., GDN_CONV_CH:GDN_CONV_CH + GDN_V]
    gates = proj[..., GDN_CONV_CH + GDN_V:].astype(jnp.float32).reshape(Bsz, T, 2, 2, H)
    q = _l2norm(qkv[..., :GDN_QK].reshape(Bsz, T, H, GDN_DK))
    k = _l2norm(qkv[..., GDN_QK:2 * GDN_QK].reshape(Bsz, T, H, GDN_DK))
    v = qkv[..., 2 * GDN_QK:].reshape(Bsz, T, H, GDN_DV)
    g = -jnp.exp(a_log.astype(jnp.float32)) * jax.nn.softplus(gates[:, :, 0] + dt_bias)
    beta = jax.nn.sigmoid(gates[:, :, 1])
    o = (_gated_delta_rule(q, k, v, g[:, :, 0], beta[:, :, 0])
         + _flip(_gated_delta_rule(_flip(q), _flip(k), _flip(v), _flip(g[:, :, 1]), _flip(beta[:, :, 1]))))
    o = _rmsnorm(o, norm_w) * jax.nn.silu(z.astype(jnp.float32)).reshape(Bsz, T, H, GDN_DV)
    return o.reshape(Bsz, T, GDN_V).astype(h.dtype) @ w_out

def _ssd_scan(xs, dt, a, bm, cm):
    Bsz, T, G, R, P = xs.shape
    L = SSD_CHUNK
    NC = T // L
    da = (dt * a).reshape(Bsz, NC, L, G, R)
    X = (xs.astype(jnp.float32) * dt[..., None]).reshape(Bsz, NC, L, G, R, P)
    Bc = bm.astype(jnp.float32).reshape(Bsz, NC, L, G, -1)
    Cc = cm.astype(jnp.float32).reshape(Bsz, NC, L, G, -1)
    acum = jnp.cumsum(da, axis=2)
    incl = jnp.tril(jnp.ones((L, L), bool))[:, :, None, None]
    seg = jnp.exp(jnp.where(incl, acum[:, :, :, None] - acum[:, :, None, :], -jnp.inf))
    cb = jnp.einsum('bclgn,bcsgn->bclsg', Cc, Bc)
    y_diag = jnp.einsum('bclsgr,bcsgrp->bclgrp', cb[..., None] * seg, X)

    def step(S, inp):
        x_c, b_c, c_c, a_c = inp
        y_off = jnp.einsum('blgn,bgrpn,blgr->blgrp', c_c, S, jnp.exp(a_c))
        a_last = a_c[:, -1]
        S = (S * jnp.exp(a_last)[..., None, None]
             + jnp.einsum('blgn,blgr,blgrp->bgrpn', b_c, jnp.exp(a_last[:, None] - a_c), x_c))
        return S, y_off

    S0 = jnp.zeros((Bsz, G, R, P, Bc.shape[-1]), jnp.float32)
    sw = lambda t: jnp.swapaxes(t, 0, 1)
    _, y_off = lax.scan(step, S0, (sw(X), sw(Bc), sw(Cc), sw(acum)))
    return (y_diag + sw(y_off)).reshape(Bsz, T, G, R, P)

def _mixer_ssd(h, w_in, conv_w, conv_b, a_log, dt_bias, d_skip, norm_w, w_out):
    Bsz, T, _ = h.shape
    G, R, P, N = SSD_GROUPS, SSD_HEADS // SSD_GROUPS, SSD_HEADDIM, SSD_STATE
    proj = h @ w_in
    z = proj[..., :SSD_INNER]
    xbc = jax.nn.silu(_dwconv(proj[..., SSD_INNER:SSD_INNER + SSD_CONV_CH], conv_w) + conv_b)
    dt_raw = proj[..., SSD_INNER + SSD_CONV_CH:].astype(jnp.float32).reshape(Bsz, T, 2, G, R)
    xs = xbc[..., :SSD_INNER].reshape(Bsz, T, G, R, P)
    bm = xbc[..., SSD_INNER:SSD_INNER + SSD_BC].reshape(Bsz, T, G, N)
    cm = xbc[..., SSD_INNER + SSD_BC:].reshape(Bsz, T, G, N)
    dt = jax.nn.softplus(dt_raw + dt_bias.astype(jnp.float32).reshape(2, G, R))
    a = -jnp.exp(a_log.astype(jnp.float32)).reshape(2, G, R)
    y = (_ssd_scan(xs, dt[:, :, 0], a[0], bm, cm)
         + _flip(_ssd_scan(_flip(xs), _flip(dt[:, :, 1]), a[1], _flip(bm), _flip(cm))))
    y = y + d_skip.astype(jnp.float32).reshape(G, R, 1) * xs.astype(jnp.float32)
    y = y.reshape(Bsz, T, G, R * P) * jax.nn.silu(z.astype(jnp.float32)).reshape(Bsz, T, G, R * P)
    y = _rmsnorm(y, norm_w.reshape(G, R * P))
    return y.reshape(Bsz, T, SSD_INNER).astype(h.dtype) @ w_out

def _rope(t):
    Bsz, T, H, Dh = t.shape
    half = Dh // 2
    inv_freq = ROPE_THETA ** (-jnp.arange(half, dtype=jnp.float32) / half)
    ang = jnp.arange(T, dtype=jnp.float32)[:, None] * inv_freq[None, :]
    cos, sin = jnp.cos(ang)[:, None, :], jnp.sin(ang)[:, None, :]
    t1 = t[..., :half].astype(jnp.float32)
    t2 = t[..., half:].astype(jnp.float32)
    return jnp.concatenate([t1 * cos - t2 * sin, t2 * cos + t1 * sin], axis=-1).astype(t.dtype)

def _window_gqa(q, k, v, sink):
    Bsz, T, HQ, Dh = q.shape
    HKV = k.shape[2]
    rep = HQ // HKV
    W = SWA_WINDOW
    NB = T // W
    qb = q.reshape(Bsz, NB, W, HKV, rep, Dh)

    def band(t):
        tb = jnp.pad(t, ((0, 0), (W, W), (0, 0), (0, 0))).reshape(Bsz, NB + 2, W, HKV, Dh)
        return jnp.concatenate([tb[:, :-2], tb[:, 1:-1], tb[:, 2:]], axis=2)

    kw, vw = band(k), band(v)
    s = jnp.einsum('bnqgrd,bnkgd->bngrqk', qb, kw).astype(jnp.float32) * Dh ** -0.5
    qpos = jnp.arange(NB)[:, None, None] * W + jnp.arange(W)[None, :, None]
    kpos = jnp.arange(NB)[:, None, None] * W - W + jnp.arange(3 * W)[None, None, :]
    valid = (jnp.abs(qpos - kpos) <= W) & (kpos >= 0) & (kpos < T)
    s = jnp.where(valid[None, :, None, None], s, -jnp.inf)
    sk = sink.astype(jnp.float32).reshape(1, 1, HKV, rep, 1, 1)
    m = jnp.maximum(s.max(axis=-1, keepdims=True), sk)
    p = jnp.exp(s - m)
    p = p / (p.sum(axis=-1, keepdims=True) + jnp.exp(sk - m))
    o = jnp.einsum('bngrqk,bnkgd->bnqgrd', p.astype(vw.dtype), vw)
    return o.reshape(Bsz, T, HQ, Dh)

def _mixer_swa(h, w_in, sink, w_out):
    Bsz, T, _ = h.shape
    proj = h @ w_in
    qd, kd = SWA_HEADS * SWA_HEADDIM, SWA_KV_HEADS * SWA_HEADDIM
    q = _rope(proj[..., :qd].reshape(Bsz, T, SWA_HEADS, SWA_HEADDIM))
    k = _rope(proj[..., qd:qd + kd].reshape(Bsz, T, SWA_KV_HEADS, SWA_HEADDIM))
    v = proj[..., qd + kd:].reshape(Bsz, T, SWA_KV_HEADS, SWA_HEADDIM)
    o = _window_gqa(q, k, v, sink)
    return o.reshape(Bsz, T, SWA_OUT) @ w_out

def _neighbourhood_attn(q, k, v, rpb):
    Bsz, T, H, Dh = q.shape
    rows = T // GRID_W
    wr = min(NA_ROWS, rows)
    ncb = GRID_W // NA_COLS
    span = 2 * NA_COLS
    qcol = np.arange(GRID_W).reshape(ncb, NA_COLS)
    kcol = np.clip(np.arange(ncb) * NA_COLS - NA_COLS // 2, 0, GRID_W - span)[:, None] + np.arange(span)
    cstart = np.clip(qcol - NA_COLS // 2, 0, GRID_W - NA_COLS)
    col_valid = ((kcol[:, None, :] >= cstart[:, :, None])
                 & (kcol[:, None, :] < cstart[:, :, None] + NA_COLS))
    col_idx = np.clip(kcol[:, None, :] - qcol[:, :, None] + NA_COLS - 1, 0, 2 * NA_COLS - 2)
    qg = q.reshape(Bsz, rows, ncb, NA_COLS, H, Dh)
    kg = k.reshape(Bsz, rows, GRID_W, H, Dh)
    vg = v.reshape(Bsz, rows, GRID_W, H, Dh)
    rpb_cols = rpb.astype(jnp.float32)[:, :, col_idx]

    def row_block(r):
        rs = jnp.clip(r - wr // 2, 0, rows - wr)
        k_blk = lax.dynamic_slice_in_dim(kg, rs, wr, axis=1)[:, :, kcol]
        v_blk = lax.dynamic_slice_in_dim(vg, rs, wr, axis=1)[:, :, kcol]
        q_r = lax.dynamic_index_in_dim(qg, r, axis=1, keepdims=False)
        s = jnp.einsum('bmqhd,bwmkhd->bhmqwk', q_r, k_blk).astype(jnp.float32) * Dh ** -0.5
        bias = rpb_cols[:, rs + jnp.arange(wr) - r + NA_ROWS - 1]
        s = s + jnp.moveaxis(bias, 1, 3)[None]
        s = jnp.where(col_valid[None, None, :, :, None, :], s, -jnp.inf)
        p = jax.nn.softmax(s, axis=(-2, -1))
        o = jnp.einsum('bhmqwk,bwmkhd->bmqhd', p.astype(v_blk.dtype), v_blk)
        return o.reshape(Bsz, GRID_W, H, Dh)

    o = lax.map(row_block, jnp.arange(rows))
    return jnp.moveaxis(o, 0, 1).reshape(Bsz, T, H, Dh)

def _mixer_na(h, w_in, rpb, w_out):
    Bsz, T, _ = h.shape
    proj = h @ w_in
    q = proj[..., :NA_WIDTH].reshape(Bsz, T, NA_HEADS, NA_HEADDIM)
    k = proj[..., NA_WIDTH:2 * NA_WIDTH].reshape(Bsz, T, NA_HEADS, NA_HEADDIM)
    v = proj[..., 2 * NA_WIDTH:].reshape(Bsz, T, NA_HEADS, NA_HEADDIM)
    o = _neighbourhood_attn(q, k, v, rpb)
    return o.reshape(Bsz, T, NA_WIDTH) @ w_out

def _peer(h, w_q, sub_keys, u_tab, v_tab):
    Bsz, T, D = h.shape
    ht = h.reshape(-1, D)
    n_tok = ht.shape[0]
    q = (ht @ w_q).reshape(n_tok, PEER_HEADS, 2, PEER_HALF)
    s = jnp.einsum('thpd,hpkd->thpk', q, sub_keys).astype(jnp.float32)
    s_top, i_top = lax.top_k(s, PEER_TOPK)
    cand = (s_top[:, :, 0, :, None] + s_top[:, :, 1, None, :]).reshape(n_tok, PEER_HEADS, PEER_TOPK ** 2)
    cand_id = (i_top[:, :, 0, :, None] * PEER_NKEYS + i_top[:, :, 1, None, :]).reshape(n_tok, PEER_HEADS, PEER_TOPK ** 2)
    best, pos = lax.top_k(cand, PEER_TOPK)
    expert = jnp.take_along_axis(cand_id, pos, axis=-1)
    gate = jax.nn.softmax(best, axis=-1)
    nb = n_tok // PEER_BLOCK

    def block(args):
        xb, eb, gb = args
        act = jax.nn.gelu(jnp.einsum('thkd,td->thk', u_tab[eb], xb).astype(jnp.float32), approximate=False) * gb
        return jnp.einsum('thk,thkd->td', act.astype(v_tab.dtype), v_tab[eb])

    y = lax.map(block, (ht.reshape(nb, PEER_BLOCK, D),
                        expert.reshape(nb, PEER_BLOCK, PEER_HEADS, PEER_TOPK),
                        gate.reshape(nb, PEER_BLOCK, PEER_HEADS, PEER_TOPK)))
    return y.reshape(Bsz, T, D).astype(h.dtype)

def setup_inputs(seed: int = 0) -> dict:
    key = jax.random.key(seed)
    keys = iter(jax.random.split(key, 40))
    D = D_MODEL

    def normal(shape, scale):
        return scale * jax.random.normal(next(keys), shape, jnp.float32)

    def gain(shape):
        return 1.0 + normal(shape, 0.02)

    def a_log(shape):
        return jnp.log(jax.random.uniform(next(keys), shape, jnp.float32, 1.0, 16.0))

    def dt_bias(shape):
        dt = jnp.exp(jax.random.uniform(next(keys), shape, jnp.float32, math.log(1e-3), math.log(1e-1)))
        return dt + jnp.log(-jnp.expm1(-dt))

    nA, nB, nC, nD = [len(range(m, DEPTH, N_MIXERS)) for m in range(N_MIXERS)]
    return {
        'x': normal((BATCH, SEQ, D), 1.0),
        'norm_mix': gain((DEPTH, D)),
        'norm_ffn': gain((DEPTH, D)),
        'norm_final': gain((D,)),
        'gdn_w_in': normal((nA, D, GDN_IN), D ** -0.5),
        'gdn_conv': normal((nA, CONV_K, GDN_CONV_CH), CONV_K ** -0.5),
        'gdn_a_log': a_log((nA, 2, GDN_HEADS)),
        'gdn_dt_bias': dt_bias((nA, 2, GDN_HEADS)),
        'gdn_norm': gain((nA, GDN_DV)),
        'gdn_w_out': normal((nA, GDN_V, D), GDN_V ** -0.5),
        'ssd_w_in': normal((nB, D, SSD_IN), D ** -0.5),
        'ssd_conv': normal((nB, CONV_K, SSD_CONV_CH), CONV_K ** -0.5),
        'ssd_conv_b': normal((nB, SSD_CONV_CH), 0.02),
        'ssd_a_log': a_log((nB, 2, SSD_HEADS)),
        'ssd_dt_bias': dt_bias((nB, 2, SSD_HEADS)),
        'ssd_d': 1.0 + normal((nB, SSD_HEADS), 0.1),
        'ssd_norm': gain((nB, SSD_INNER)),
        'ssd_w_out': normal((nB, SSD_INNER, D), SSD_INNER ** -0.5),
        'swa_w_in': normal((nC, D, SWA_IN), D ** -0.5),
        'swa_sink': normal((nC, SWA_HEADS), 1.0),
        'swa_w_out': normal((nC, SWA_OUT, D), SWA_OUT ** -0.5),
        'na_w_in': normal((nD, D, NA_IN), D ** -0.5),
        'na_rpb': normal((nD, NA_HEADS, 2 * NA_ROWS - 1, 2 * NA_COLS - 1), 0.1),
        'na_w_out': normal((nD, NA_WIDTH, D), NA_WIDTH ** -0.5),
        'peer_w_q': normal((DEPTH, D, PEER_HEADS * PEER_QDIM), D ** -0.5),
        'peer_keys': normal((DEPTH, PEER_HEADS, 2, PEER_NKEYS, PEER_HALF), PEER_HALF ** -0.5),
        'peer_u': normal((DEPTH, PEER_EXPERTS, D), D ** -0.5),
        'peer_v': normal((DEPTH, PEER_EXPERTS, D), PEER_TOPK ** -0.5),
    }

def reference(x, norm_mix, norm_ffn, norm_final,
              gdn_w_in, gdn_conv, gdn_a_log, gdn_dt_bias, gdn_norm, gdn_w_out,
              ssd_w_in, ssd_conv, ssd_conv_b, ssd_a_log, ssd_dt_bias, ssd_d, ssd_norm, ssd_w_out,
              swa_w_in, swa_sink, swa_w_out,
              na_w_in, na_rpb, na_w_out,
              peer_w_q, peer_keys, peer_u, peer_v):
    for i in range(DEPTH):
        mixer, j = i % N_MIXERS, i // N_MIXERS
        h = _rmsnorm(x, norm_mix[i])
        if mixer == 0:
            y = _mixer_gdn(h, gdn_w_in[j], gdn_conv[j], gdn_a_log[j], gdn_dt_bias[j], gdn_norm[j], gdn_w_out[j])
        elif mixer == 1:
            y = _mixer_ssd(h, ssd_w_in[j], ssd_conv[j], ssd_conv_b[j], ssd_a_log[j], ssd_dt_bias[j],
                           ssd_d[j], ssd_norm[j], ssd_w_out[j])
        elif mixer == 2:
            y = _mixer_swa(h, swa_w_in[j], swa_sink[j], swa_w_out[j])
        else:
            y = _mixer_na(h, na_w_in[j], na_rpb[j], na_w_out[j])
        x = x + y.astype(x.dtype)
        x = x + _peer(_rmsnorm(x, norm_ffn[i]), peer_w_q[i], peer_keys[i], peer_u[i], peer_v[i])
    return _rmsnorm(x, norm_final)


_drawn_inputs = setup_inputs


def setup_inputs(seed=0):
    import zlib

    import numpy as np

    out = dict(_drawn_inputs(seed))
    spreads = {}
    factors = {}
    for name, (base, spread) in spreads.items():
        noise = np.random.default_rng([zlib.crc32(name.encode()), seed]).standard_normal(out[name].shape)
        drawn = base * np.exp(spread * noise) if base else spread * noise
        out[name] = jnp.asarray(drawn.astype(out[name].dtype))
    for name, factor in factors.items():
        out[name] = (out[name] * factor).astype(out[name].dtype)
    return out
```

```python
from contextlib import ExitStack

import numpy as np

import concourse.bass as bass
from concourse import mybir

F32 = mybir.dt.float32
U32 = mybir.dt.uint32
ALU = mybir.AluOpType
ACT = mybir.ActivationFunctionType
AX = mybir.AxisListType

P = 128
D = 1024
KD = D // P
T = 256
NT = T // P
EPS = 1e-6
TAPS = 5

GH = 8
GC = 3 * GH
GSYS = 2 * GH * NT
GB = GSYS // 4
LEVELS = 7

SH = 32
SP_ = 64
SG = 4
SR = SH // SG
SI = SH * SP_
SX = SI // P
SC = SX + 2 * SG

PH = 8
HP = 2 * PH
TOPK = 16
NEG = -3.0e38

RING = 4


def host_constants():
    j, i = np.arange(P)[:, None], np.arange(P)[None, :]
    rows = [j == i, j <= i, j >= i, j < i, j > i, np.ones((P, P)), np.broadcast_to(i, (P, P))]
    levels = []
    for flip in (False, True):
        for level in range(LEVELS):
            b = 1 << level
            hi, lo = (j, i) if flip else (i, j)
            levels.append((hi // b % 2 == 1) & (lo // b == hi // b - 1))
    return [np.stack([np.asarray(r, np.float32) for r in m], axis=1) for m in (rows, levels)]


C_EYE, C_UPI, C_LOI, C_UPS, C_LOS, C_ONE, C_IOTA, C_ALL = range(8)


def weight_stream(a):
    order = []
    for hf in range(2):
        order += [(("gz", hf, k), a["gdn_z"][hf, k]) for k in range(KD // 2)]
    order += [(("gq", m), a["gdn_qkv"][m]) for m in range(GC)]
    order += [(("go", k), a["gdn_out"][k]) for k in range(GH)]
    tables = []

    def peer(lyr):
        run = [(("pq", lyr, m), a["peer_wq"][lyr, m]) for m in range(HP)]
        run += [(("pk", lyr, m), a["peer_kT"][lyr, m]) for m in range(2)]
        tables.append(len(order) + len(run))
        return run + [None] * (2 * P)

    order += peer(0)
    for nb in range(SI // 512):
        order += [(("sz", nb, k), a["ssd_z"][nb, k]) for k in range(KD // 2)]
    order += [(("sx", m), a["ssd_xbc"][m]) for m in range(SC)]
    order += [(("so", k), a["ssd_out"][k]) for k in range(SX)]
    order += peer(1)
    return order, {o[0]: n for n, o in enumerate(order) if o is not None}, tables


def hybrid_encoder(nc, a, out):
    order, at, tables = weight_stream(a)
    ctx = ExitStack()
    with ctx:
        def sb(name, shape, dt=F32):
            return ctx.enter_context(nc.sbuf_tensor(name, shape, dt))

        def sem(name):
            return ctx.enter_context(nc.semaphore(name))

        PS = [ctx.enter_context(nc.psum_tensor(f"bank{i}", [P, 512], F32)) for i in range(8)]

        def cutter(tensor, size):
            at_column = [0]

            def take(*shape, dt=None):
                n = int(np.prod(shape))
                v = tensor[:, at_column[0]:at_column[0] + n]
                at_column[0] += n
                assert at_column[0] <= size, at_column
                if dt is not None:
                    v = v.bitcast(dt)
                if len(shape) > 1:
                    names = "abcd"[:len(shape)]
                    v = v.rearrange(f"p ({' '.join(names)}) -> p {' '.join(names)}", **dict(zip(names, shape)))
                return v

            return take

        def system(direction, head, chunk):
            return (direction * GH + head) * NT + chunk

        def t_count(n):
            return 2 * (n + 1) if n < (LEVELS - 1) * GB else 2 * (LEVELS - 1) * GB + n - (LEVELS - 1) * GB + 1

        def flat(v, names):
            return v.rearrange(f"p {names} -> p ({names})")

        x_sb = sb("x_sb", [P, NT, D])
        hT = sb("hT", [P, KD, T])
        ring = sb("ring", [P, RING, D])
        const = sb("const", [P, C_ALL, P])
        levels = sb("levels", [P, 2 * LEVELS, P], mybir.dt.float16)
        arena = sb("arena", [P, P * T])
        side = sb("side", [P, 4096])
        small = sb("small", [P, 2048])
        h_tok = side[:, 0:NT * D].rearrange("p (t d) -> p t d", t=NT)
        h_junk = side[:, NT * D:NT * D + D]
        last_gain = ring[:, 0, :]

        ident = const[:, C_EYE, :]
        upper = const[:, C_UPI, :]
        lower = const[:, C_LOI, :]
        ones = const[:, C_ONE, :]
        iota = const[:, C_IOTA, :]

        tiny = cutter(small, 2048)
        norm_w = tiny(4, KD)
        n_ss, n_ms, n_root, n_inv, n_new, n_rstd = (tiny(NT) for _ in range(6))
        g_ss, g_ms, g_root, g_inv, g_new, g_rstd = (tiny(NT, 2 * GH) for _ in range(6))

        g_conv = tiny(GC, TAPS)
        g_bias, g_alog, g_nega = (tiny(2 * GH) for _ in range(3))
        g_z, g_mx, g_ab, g_g, g_beta, g_gc, g_gt, g_wx, g_eg, g_egq = (tiny(NT, 2 * GH) for _ in range(10))
        g_wg = sb("g_wg", [P, KD, 4 * GH])
        g_gain = sb("g_gain", [P, P])
        take = cutter(arena, P * T)
        g_feat = take(GC, T)
        g_tok = take(NT, GC, P)
        g_siluz = take(NT, D)
        g_AT = take(GSYS, P)
        g_T = take(GSYS, P)
        g_TT = take(GSYS, P)
        g_Y = take(GSYS, P)
        spare = take(2048)
        g_pad = flat(g_Y, "s d")[:, 0:4 * 260].rearrange("p (s w) -> p s w", s=4)
        g_acc = flat(g_Y, "s d")[:, 1040:1040 + 4 * T].rearrange("p (s w) -> p s w", s=4)
        g_E = g_feat[:, 2 * GH:3 * GH, :]
        g_tmp = g_Y[:, 0:16, :]
        g_KE = spare[:, 0:512].rearrange("p (s w) -> p s w", s=2)
        g_QE = spare[:, 512:1024].rearrange("p (s w) -> p s w", s=2)
        g_row = spare[0:GH, 1024:1536]
        g_mask = g_tok[:, 0, 0:GH, :]
        g_PT = side[:, :].rearrange("p (s d) -> p s d", s=GSYS)
        g_vn = g_T
        g_kS = g_Y[:, 0:16, :]
        g_S = g_Y[:, 16:32, :]
        g_vp = g_AT[:, 0:16, :]
        g_inter = g_AT[:, 16:32, :]
        g_o = g_TT[:, 0:16, :]
        g_sq = g_TT[:, 16:32, :]

        s_conv = tiny(SC, TAPS)
        s_cbias = tiny(SC)
        s_wg = sb("s_wg", [P, KD, 2 * SH])
        s_bias, s_alog, s_nega, s_D = tiny(2 * SH), tiny(2 * SH), tiny(2 * SH), tiny(SH)
        s_z, s_mx, s_ab, s_dt, s_da, s_ac, s_nac = (tiny(NT, 2 * SH) for _ in range(7))
        s_ss, s_ms, s_root, s_inv, s_new, s_rstd = (tiny(NT, SG) for _ in range(6))
        take = cutter(arena, P * T)
        s_feat = take(SC, T)
        s_tok = take(NT, SI)
        s_siluz = take(NT, SI)
        s_y = take(NT, SI)
        s_skip = take(NT, SI)
        s_CB = take(SG, NT, 3, P)
        s_pad = take(4, 260)
        s_acc = take(4, T)
        s_row = take(2 * T)[0:SH, :]
        s_E = take(2, NT, 3, P)
        s_M = take(2, NT, 3, P)
        s_yT = s_feat[:, 0:SX, :]
        s_gain = side[:, 0:SI]

        take = cutter(arena, P * T)
        p_qT = take(HP, T)
        p_s = take(NT, HP, P)
        p_s2 = take(NT, HP, P)
        p_cand = take(NT * PH, TOPK * TOPK)
        p_cand2 = take(NT * PH, TOPK * TOPK)
        p_hot = take(NT * PH, TOPK * TOPK)
        p_top = take(NT, HP, TOPK)
        p_idx = take(NT, HP, TOPK, dt=U32)
        p_idxf = take(NT, HP, TOPK)
        p_best = take(NT * PH, TOPK)
        p_pos = take(NT * PH, TOPK, dt=U32)
        p_ab = take(2, NT * PH, TOPK, dt=U32)
        p_abf = take(2, NT * PH, TOPK)
        p_key = take(2, NT * PH, TOPK)
        p_gate = take(NT * PH, TOPK)
        p_sum, p_rsum = take(NT * PH), take(NT * PH)
        p_map = arena[:, :].rearrange("p (i t) -> p i t", i=P)
        take = cutter(side, 4096)
        p_T = take(3, T)
        p_A = take(8, P)
        p_B = take(8, P)
        p_act = take(2, T)
        p_ag = take(2, T)

        x_loaded, small_loaded, gain_loaded = sem("x_loaded"), sem("small_loaded"), sem("gain_loaded")
        last_gain_loaded = sem("last_gain_loaded")
        landed = [sem(f"unit_landed{i}") for i in range(RING)]
        unit_used = sem("unit_used")
        dve_chain = sem("dve_chain")
        n_sq, n_mean, n_rooted, n_h, n_hTps, n_hT = (sem("n_" + s) for s in (
            "squares", "mean", "root", "h", "hT_psum", "hT"))
        x_added = sem("x_added")
        oT_psum, oT_ready, o_ready = sem("oT_psum"), sem("oT_ready"), sem("o_ready")
        SEM = {s: sem(s) for s in (
            "g_gate_ps g_zs g_pads g_padded g_conved g_silued g_gateb g_gact g_gexp g_gg g_betas g_cum g_cumsb g_exps g_rows "
            "g_tokps g_toksb g_sqsum g_junk g_mean g_root g_qk g_backps g_backsb g_bc g_dexp g_logE g_E g_kq g_KE g_A g_P g_mask g_Yps g_Y "
            "g_Zps g_T g_kS g_U0 g_vn0 g_S1ps g_S1 g_RQ g_v1 g_int g_U1 g_vn1 g_Ops g_O g_osum g_omean g_oroot g_gz "
            "s_gate_ps s_gateb s_gexp s_pads s_mv s_yg s_zs s_padded s_conved s_silued s_gact s_sp s_da s_cum s_nac s_rowsps s_rows s_tokps s_toksb s_skip "
            "s_cbps s_cb s_cbl s_bc s_d s_e s_m s_yps s_y s_ss s_mean s_root "
            "p_qps p_q p_sps p_s p_top p_ex p_exd p_key p_Tps p_T p_hot p_mapps p_map p_hps p_gelu p_ag p_yps "
            "finished stored").split()}
        N_SMALL = 14

        block = ctx.enter_context(nc.Block())

        @block.sync
        def _(sp):
            sp.dma_start(x_sb[:, :, :], a["x"]).then_inc(x_loaded, 16)

            def load_unit(n):
                if n >= RING:
                    sp.wait_ge(unit_used, n - RING + 1)
                sp.dma_start(ring[:, n % RING, :], order[n][1]).then_inc(landed[n % RING], 16)

            def load_tables(lyr):
                n0 = tables[lyr]
                U, V = a["peer_u"][lyr], a["peer_v"][lyr]

                def one(k, src, wait):
                    sp.wait_ge(unit_used, wait)
                    sp.dma_start(ring[:, (n0 + k) % RING, :], src).then_inc(landed[(n0 + k) % RING], 16)

                one(0, U[0], n0 - RING + 1)
                one(1, U[1], n0 - RING + 2)
                one(2, V[0], n0 - RING + 3)
                with sp.Fori(0, P // 2 - 1) as it:
                    for k, table, i in ((3, U, 2), (4, V, 1), (5, U, 3), (6, V, 2)):
                        one(k, table[bass.ds(it * 2 + i, 1)].rearrange("a p c -> p (a c)"),
                            it * 4 + (n0 + k - RING + 1))
                one(2 * P - 1, V[P - 1], n0 + 2 * P - RING)

            n = 0
            while n < len(order):
                if order[n] is None:
                    load_tables(0 if n == tables[0] else 1)
                    n += 2 * P
                else:
                    load_unit(n)
                    n += 1
            sp.wait_ge(unit_used, len(order))
            sp.dma_start(last_gain, a["norm_final"].partition_broadcast(P)).then_inc(last_gain_loaded, 16)
            sp.wait_ge(SEM["finished"], 1)
            sp.dma_start(out, x_sb[:, :, :]).then_inc(SEM["stored"], 16)
            sp.wait_ge(SEM["stored"], 16)

        @block.tensor
        def _(pe):
            def mm(o, w, r, first=True, last=True):
                return pe.matmul(o, w, r, start=first, stop=last)

            def unit(name):
                n = at[name]
                pe.wait_ge(landed[n % RING], 16 * (n // RING + 1))
                return ring[:, n % RING, :]

            def turn_h(i):
                pe.wait_ge(n_h, 2 * (i + 1))
                for b in range(4):
                    for kk in range(2):
                        for t in range(NT):
                            k = 2 * b + kk
                            last = pe.transpose(PS[b][:, (2 * kk + t) * P:(2 * kk + t + 1) * P],
                                                h_tok[:, t, k * P:(k + 1) * P], ident)
                    last.then_inc(n_hTps, 1)
                pe.wait_ge(n_hT, KD * (i + 1))

            def by_token(name, bank):
                for q in range(KD // 2):
                    w = unit((*name, q))
                    for kk in range(2):
                        k = 2 * q + kk
                        for t in range(NT):
                            last = mm(PS[bank + t][:, :], hT[:, k, t * P:(t + 1) * P], w[:, kk * 512:(kk + 1) * 512],
                                      k == 0, k == KD - 1)
                    last.then_inc(unit_used, 1)

            def by_channel(name, bank):
                w = unit(name)
                for k in range(KD):
                    last = mm(PS[bank][:, 0:T], w[:, k * P:(k + 1) * P], hT[:, k, :], k == 0, k == KD - 1)
                last.then_inc(unit_used, 1)

            def out_projection(name, tiles, src):
                for k in range(tiles):
                    w = unit((name, k))
                    for t in range(NT):
                        for hf in range(2):
                            last = mm(PS[4 + 2 * t + hf][:, :], src[:, k, t * P:(t + 1) * P],
                                      w[:, hf * 512:(hf + 1) * 512], k == 0, k == tiles - 1)
                    last.then_inc(unit_used, 1)

            def gdn():
                for hf in range(2):
                    by_token(("gz", hf), 4 + 2 * hf)
                for t in range(NT):
                    for k in range(KD):
                        last = mm(PS[2][:, t * 32:(t + 1) * 32], hT[:, k, t * P:(t + 1) * P], g_wg[:, k, :],
                                  k == 0, k == KD - 1)
                last.then_inc(SEM["g_gate_ps"], 1)

                def turn_tok(gi):
                    pe.wait_ge(SEM["g_silued"], 2 * gi + 2)
                    if gi == 0:
                        pe.wait_ge(SEM["g_zs"], 4)
                    if gi >= 4:
                        pe.wait_ge(SEM["g_toksb"], gi - 3)
                    for t in range(NT):
                        for e in range(2):
                            last = pe.transpose(PS[4 + gi % 4][:, (2 * t + e) * P:(2 * t + e + 1) * P],
                                                g_feat[:, 2 * gi + e, t * P:(t + 1) * P], ident)
                    last.then_inc(SEM["g_tokps"], 1)

                for m in range(GC):
                    if m >= 2:
                        pe.wait_ge(SEM["g_padded"], m - 1)
                    by_channel(("gq", m), m % 2)
                    if m >= 3 and m % 2:
                        turn_tok((m - 3) // 2)
                pe.wait_ge(SEM["g_gg"], 1)
                for c in range(NT):
                    mm(PS[3][:, c * 16:c * 16 + 8], upper, g_g[:, c, 0:8])
                    mm(PS[3][:, c * 16 + 8:c * 16 + 16], lower, g_g[:, c, 8:16])
                    mm(PS[3][:, 32 + c * 16:48 + c * 16], ones, g_g[:, c, :])
                    mm(PS[2][0:GH, c * P:(c + 1) * P], g_g[:, c, 0:8], upper)
                    last = mm(PS[2][0:GH, T + c * P:T + (c + 1) * P], g_g[:, c, 8:16], lower)
                last.then_inc(SEM["g_cum"], 1)
                turn_tok(11)
                pe.wait_ge(SEM["g_qk"], 2)
                for gi in range(GH):
                    if gi >= 4:
                        pe.wait_ge(SEM["g_backsb"], gi - 3)
                    for e in range(2):
                        for t in range(NT):
                            last = pe.transpose(PS[4 + gi % 4][:, (2 * e + t) * P:(2 * e + t + 1) * P],
                                                g_tok[:, t, 2 * gi + e, :], ident)
                    last.then_inc(SEM["g_backps"], 1)
                pe.wait_ge(SEM["g_rows"], 1)
                pe.wait_ge(SEM["g_padded"], GC)
                for h in range(GH):
                    if h >= 2:
                        pe.wait_ge(SEM["g_dexp"], h - 1)
                    pick = const[0:GH, C_EYE, h:h + 1].to_broadcast([GH, P])
                    mm(PS[h % 2][:, 0:T], pick, g_row[:, 0:T])
                    mm(PS[h % 2][:, T:2 * T], pick, g_row[:, T:2 * T]).then_inc(SEM["g_bc"], 1)
                    if h == 0:
                        pe.wait_ge(SEM["g_cumsb"], 1)
                        pe.wait_ge(SEM["g_backsb"], GH)
                    if h >= 2:
                        pe.wait_ge(SEM["g_KE"], h - 1)
                    for c in range(NT):
                        kT = g_feat[:, GH + h, c * P:(c + 1) * P]
                        mm(PS[2 + h % 2][:, c * P:(c + 1) * P], kT, kT)
                        last = mm(PS[2 + h % 2][:, T + c * P:T + (c + 1) * P], kT, g_feat[:, h, c * P:(c + 1) * P])
                    last.then_inc(SEM["g_kq"], 1)

                def y_step(n):
                    level, b = divmod(n, GB)
                    pe.wait_ge(SEM["g_mask"], n + 1)
                    if n >= 2:
                        if n - 2 < GB:
                            pe.wait_ge(SEM["g_T"], t_count(n - 2))
                        else:
                            pe.wait_ge(SEM["g_Y"], n - 2 - GB + 1)
                    if n == 0:
                        pe.wait_ge(SEM["g_dexp"], GH)
                    if level:
                        pe.wait_ge(SEM["g_T"], t_count(n - GB))
                    for e in range(4):
                        last = mm(PS[n % 2][:, e * P:(e + 1) * P], g_mask[:, 4 * (n % 2) + e, :],
                                  g_T[:, 4 * b + e, :] if level else ident)
                    last.then_inc(SEM["g_Yps"], 1)

                def z_step(n):
                    level, b = divmod(n, GB)
                    pe.wait_ge(SEM["g_Y"], n - GB + 1)
                    if n - 2 >= GB:
                        pe.wait_ge(SEM["g_T"], t_count(n - 2))
                    for e in range(4):
                        s = 4 * b + e
                        if level < LEVELS - 1:
                            mm(PS[4 + n % 2][:, e * P:(e + 1) * P], g_TT[:, s, :], g_Y[:, s, :])
                        last = mm(PS[6 + n % 2][:, e * P:(e + 1) * P], g_Y[:, s, :], g_TT[:, s, :])
                    last.then_inc(SEM["g_Zps"], 1)

                for n in range(LEVELS * GB):
                    y_step(n)
                    if n - 1 >= GB:
                        z_step(n - 1)
                z_step(LEVELS * GB - 1)

                pe.wait_ge(SEM["g_T"], t_count(LEVELS * GB - 1))
                for q4 in range(4):
                    d, h0 = q4 // 2, 4 * (q4 % 2)
                    for e in range(4):
                        last = mm(PS[q4][:, e * P:(e + 1) * P], g_TT[:, system(d, h0 + e, d), :],
                                  g_tok[:, d, 2 * GH + h0 + e, :])
                    last.then_inc(SEM["g_U0"], 1)
                for q4 in range(4):
                    d, h0 = q4 // 2, 4 * (q4 % 2)
                    pe.wait_ge(SEM["g_vn0"], q4 + 1)
                    pe.wait_ge(SEM["g_kS"], q4 + 1)
                    for e in range(4):
                        last = mm(PS[4 + q4][:, e * P:(e + 1) * P], g_kS[:, d * GH + h0 + e, :],
                                  g_vn[:, system(d, h0 + e, d), :])
                    last.then_inc(SEM["g_S1ps"], 1)
                for q4 in range(4):
                    d, h0 = q4 // 2, 4 * (q4 % 2)
                    pe.wait_ge(SEM["g_S1"], q4 + 1)
                    c = 1 - d
                    for e in range(4):
                        S = g_S[:, d * GH + h0 + e, :]
                        mm(PS[q4][:, e * P:(e + 1) * P], g_feat[:, GH + h0 + e, c * P:(c + 1) * P], S)
                        last = mm(PS[4 + q4][:, e * P:(e + 1) * P], g_feat[:, h0 + e, c * P:(c + 1) * P], S)
                    last.then_inc(SEM["g_RQ"], 1)
                for q4 in range(4):
                    d, h0 = q4 // 2, 4 * (q4 % 2)
                    pe.wait_ge(SEM["g_v1"], q4 + 1)
                    for e in range(4):
                        last = mm(PS[q4][:, e * P:(e + 1) * P], g_TT[:, system(d, h0 + e, 1 - d), :],
                                  g_vp[:, d * GH + h0 + e, :])
                    last.then_inc(SEM["g_U1"], 1)
                pe.wait_ge(SEM["g_int"], 4)
                pe.wait_ge(SEM["g_vn1"], 4)
                pe.wait_ge(SEM["g_P"], 2 * GH)
                for c in range(NT):
                    for hg in range(2):
                        for e in range(4):
                            o = PS[4 + 2 * c + hg][:, e * P:(e + 1) * P]
                            f, r = system(0, 4 * hg + e, c), system(1, 4 * hg + e, c)
                            mm(o, g_PT[:, f, :], g_vn[:, f, :], True, False)
                            last = mm(o, g_PT[:, r, :], g_vn[:, r, :], False, True)
                        last.then_inc(SEM["g_Ops"], 1)
                pe.wait_ge(o_ready, 2)
                for b in range(4):
                    for kk in range(2):
                        for t in range(NT):
                            last = pe.transpose(PS[b][:, (2 * kk + t) * P:(2 * kk + t + 1) * P],
                                                g_o[:, t * GH + 2 * b + kk, :], ident)
                    last.then_inc(oT_psum, 1)
                pe.wait_ge(oT_ready, 4)
                out_projection("go", GH, hT)

            def ssd():
                for nb in range(SI // 512):
                    if nb >= 2:
                        pe.wait_ge(SEM["s_zs"], 2 * (nb - 1))
                    by_token(("sz", nb), 4 + 2 * (nb % 2))
                for t in range(NT):
                    for k in range(KD):
                        last = mm(PS[2][:, t * 64:(t + 1) * 64], hT[:, k, t * P:(t + 1) * P], s_wg[:, k, :],
                                  k == 0, k == KD - 1)
                last.then_inc(SEM["s_gate_ps"], 1)

                def turn_tok(gi):
                    pe.wait_ge(SEM["s_silued"], 2 * gi + 2)
                    if gi == 0:
                        pe.wait_ge(SEM["s_zs"], 8)
                    if gi >= 4:
                        pe.wait_ge(SEM["s_toksb"], gi - 3)
                    for t in range(NT):
                        for e in range(2):
                            last = pe.transpose(PS[4 + gi % 4][:, (2 * t + e) * P:(2 * t + e + 1) * P],
                                                s_feat[:, 2 * gi + e, t * P:(t + 1) * P], ident)
                    last.then_inc(SEM["s_tokps"], 1)

                for m in range(SC):
                    if m >= 2:
                        pe.wait_ge(SEM["s_padded"], m - 1)
                    by_channel(("sx", m), m % 2)
                    if m >= 3 and m % 2 and (m - 3) // 2 < SX // 2:
                        turn_tok((m - 3) // 2)
                pe.wait_ge(SEM["s_da"], 1)
                f, r = slice(0, SH), slice(SH, 2 * SH)
                mm(PS[3][:, 0:32], upper, s_da[:, 0, f])
                mm(PS[3][:, 64:96], ones, s_da[:, 0, f], True, False)
                mm(PS[3][:, 64:96], upper, s_da[:, 1, f], False, True)
                mm(PS[3][:, 96:128], lower, s_da[:, 1, r])
                mm(PS[3][:, 32:64], ones, s_da[:, 1, r], True, False)
                mm(PS[3][:, 32:64], lower, s_da[:, 0, r], False, True)
                mm(PS[2][0:SH, 0:P], s_da[:, 0, f], upper)
                mm(PS[2][0:SH, P:2 * P], s_da[:, 0, f], ones, True, False)
                mm(PS[2][0:SH, P:2 * P], s_da[:, 1, f], upper, False, True)
                mm(PS[2][0:SH, 2 * P:3 * P], s_da[:, 1, r], ones, True, False)
                mm(PS[2][0:SH, 2 * P:3 * P], s_da[:, 0, r], lower, False, True)
                mm(PS[2][0:SH, 3 * P:4 * P], s_da[:, 1, r], lower).then_inc(SEM["s_cum"], 1)
                pe.wait_ge(SEM["s_silued"], SC)
                pe.wait_ge(SEM["s_toksb"], SX // 2)
                for g in range(SG):
                    if g >= 2:
                        pe.wait_ge(SEM["s_cb"], g - 1)
                    for st in range(NT):
                        last = mm(PS[6 + g % 2][:, st * T:(st + 1) * T], s_feat[:, SX + g, st * P:(st + 1) * P],
                                  s_feat[:, SX + SG + g, :])
                    last.then_inc(SEM["s_cbps"], 1)
                pe.wait_ge(SEM["s_rows"], 1)
                pe.wait_ge(SEM["s_nac"], 1)
                pe.wait_ge(SEM["s_padded"], SC)

                def spread(h):
                    if h >= 2:
                        pe.wait_ge(SEM["s_e"], h - 1)
                    pick = const[0:SH, C_EYE, h:h + 1].to_broadcast([SH, P])
                    mm(PS[h % 2][:, 0:T], pick, s_row[:, 0:T])
                    mm(PS[h % 2][:, T:2 * T], pick, s_row[:, T:2 * T]).then_inc(SEM["s_bc"], 1)

                def y_head(h):
                    g, b = h // SR, 2 + 2 * (h // SR % 2)
                    if h % SR == 0 and g >= 2:
                        pe.wait_ge(SEM["s_y"], 2 * (g - 1))
                    pe.wait_ge(SEM["s_m"], h + 1)
                    o = slice(h % SR * SP_, (h % SR + 1) * SP_)
                    x0, x1 = (s_tok[:, t, h * SP_:(h + 1) * SP_] for t in range(NT))
                    mm(PS[b][:, o], s_M[:, h % 2, 0, 0, :], x0, True, False)
                    mm(PS[b][:, o], s_M[:, h % 2, 1, 2, :], x1, False, True)
                    mm(PS[b + 1][:, o], s_M[:, h % 2, 0, 2, :], x0, True, False)
                    mm(PS[b + 1][:, o], s_M[:, h % 2, 1, 0, :], x1, False, True).then_inc(SEM["s_yps"], 1)

                for h in range(SH):
                    spread(h)
                    if h >= 2:
                        y_head(h - 2)
                y_head(SH - 2)
                y_head(SH - 1)
                for gi in range(SX // 2):
                    pe.wait_ge(o_ready, 2 + 8)
                    if gi >= 4:
                        pe.wait_ge(oT_ready, 4 + gi - 3)
                    for kk in range(2):
                        for t in range(NT):
                            k = 2 * gi + kk
                            last = pe.transpose(PS[gi % 4][:, (2 * kk + t) * P:(2 * kk + t + 1) * P],
                                                s_y[:, t, k * P:(k + 1) * P], ident)
                    last.then_inc(oT_psum, 1)
                pe.wait_ge(oT_ready, 4 + SX // 2)
                out_projection("so", SX, s_yT)

            def route(lyr):
                for m in range(HP):
                    if m >= 2:
                        pe.wait_ge(SEM["p_q"], HP * lyr + m - 1)
                    by_channel(("pq", lyr, m), m % 2)
                pe.wait_ge(SEM["p_q"], HP * (lyr + 1))
                for half in range(2):
                    w = unit(("pk", lyr, half))
                    for t in range(NT):
                        for hq in range(2):
                            g = 4 * half + 2 * t + hq
                            if g >= 4:
                                pe.wait_ge(SEM["p_s"], 8 * lyr + g - 3)
                            for e in range(4):
                                hp = 8 * half + 4 * hq + e
                                last = mm(PS[2 + g % 4][:, e * P:(e + 1) * P], p_qT[:, hp, t * P:(t + 1) * P],
                                          w[:, (hp % 8) * P:(hp % 8 + 1) * P])
                            last.then_inc(unit_used if g % 4 == 3 else SEM["p_sps"], 1)
                pe.wait_ge(SEM["p_key"], lyr + 1)
                for half in range(2):
                    for t in range(NT):
                        v = flat(p_key[:, half, t * PH:(t + 1) * PH, :], "h k")
                        pe.transpose(PS[6][:, half * T + t * P:half * T + (t + 1) * P], v, ident)
                for t in range(NT):
                    last = pe.transpose(PS[7][:, t * P:(t + 1) * P], flat(p_gate[:, t * PH:(t + 1) * PH, :], "h k"), ident)
                last.then_inc(SEM["p_Tps"], 1)

                def tokens8(it, first=False):
                    for half in range(2):
                        if not first:
                            pe.wait_ge(SEM["p_map"], it * 2 + (64 * lyr + half - 1))
                        for e in range(4):
                            u = 4 * half + e
                            pe.wait_ge(SEM["p_hot"], it * 8 + (T * lyr + u + 1))
                            last = mm(PS[half][:, e * P:(e + 1) * P], p_B[:, u, :], p_A[:, u, :])
                        last.then_inc(SEM["p_mapps"], 1)

                tokens8(0, True)
                with pe.Fori(1, T // 8) as it:
                    tokens8(it)

            def experts(lyr):
                n0 = tables[lyr]

                def table(k, it):
                    n = n0 + k
                    pe.wait_ge(landed[n % RING], it * 16 + 16 * (n // RING + 1))
                    return ring[:, n % RING, :]

                def hidden(i, k, it, wait=True):
                    if wait:
                        pe.wait_ge(SEM["p_gelu"], it * 2 + (P * lyr + i - 1))
                    w = table(k, it)
                    for c in range(KD):
                        last = mm(PS[i % 2][:, 0:T], w[:, c * P:(c + 1) * P], hT[:, c, :], c == 0, c == KD - 1)
                    last.then_inc(unit_used, 1)

                def values(i, k, it, first=False, last_one=False):
                    pe.wait_ge(SEM["p_ag"], it * 2 + (P * lyr + i + 1))
                    w = table(k, it)
                    for t in range(NT):
                        for hf in range(2):
                            last = mm(PS[4 + 2 * t + hf][:, :], p_ag[:, i % 2, t * P:(t + 1) * P],
                                      w[:, hf * 512:(hf + 1) * 512], first, last_one)
                    last.then_inc(unit_used, 1)

                pe.wait_ge(SEM["p_map"], 64 * (lyr + 1))
                hidden(0, 0, 0, False)
                hidden(1, 1, 0, False)
                values(0, 2, 0, first=True)
                with pe.Fori(0, P // 2 - 1) as it:
                    hidden(2, 3, it)
                    values(1, 4, it)
                    hidden(3, 5, it)
                    values(2, 6, it)
                values(P - 1, 2 * P - 1, 0, last_one=True)

            pe.wait_ge(small_loaded, 16 * N_SMALL)
            turn_h(0)
            gdn()
            turn_h(1)
            route(0)
            experts(0)
            turn_h(2)
            ssd()
            turn_h(3)
            route(1)
            experts(1)

        @block.vector
        def _(dve):
            chain = [0]

            def link(ins):
                chain[0] += 1
                ins.then_inc(dve_chain, 1)
                dve.wait_ge(dve_chain, chain[0])

            def wide(v, n):
                return v.rearrange("p (a o) -> p a o", o=1).to_broadcast([v.shape[0], v.shape[1], n])

            def rows(v, n):
                return v.rearrange("p (o c) -> p o c", o=1).to_broadcast([v.shape[0], n, v.shape[1]])

            def polish(ms, root, inv, new, rstd, signal=None):
                link(dve.reciprocal(inv, root))
                link(dve.tensor_tensor(new, inv, inv, ALU.mult))
                link(dve.tensor_tensor(new, new, ms, ALU.mult))
                link(dve.tensor_scalar(new, new, -0.5, 1.5, ALU.mult, ALU.add))
                link(dve.tensor_tensor(rstd, inv, new, ALU.mult))

            def norm_stats(i):
                dve.wait_ge(n_sq, 2 * (i + 1))
                dve.tensor_scalar(n_ms, n_ss, 1.0 / D, EPS, ALU.mult, ALU.add).then_inc(n_mean, 1)
                dve.wait_ge(n_rooted, i + 1)
                polish(n_ms, n_root, n_inv, n_new, n_rstd)

            def norm(i):
                norm_stats(i)
                for t in range(NT):
                    dve.tensor_scalar(h_tok[:, t, :], x_sb[:, t, :], n_rstd[:, t:t + 1], None, ALU.mult).then_inc(n_h, 1)

            def residual(last_unit):
                dve.wait_ge(unit_used, last_unit + 1)
                for t in range(NT):
                    for hf in range(2):
                        v = x_sb[:, t, hf * 512:(hf + 1) * 512]
                        dve.tensor_tensor(v, PS[4 + 2 * t + hf][:, :], v, ALU.add).then_inc(x_added, 1)

            def conv(m, pad, acc, taps, padded, conved, silued):
                dve.wait_ge(padded, m + 1)
                if m >= 4:
                    dve.wait_ge(silued, m - 3)
                o = acc[:, m % 4, :]
                link(dve.tensor_scalar(o, pad[:, m % 4, 0:T], taps[:, m, 0:1], None, ALU.mult))
                for j in range(1, TAPS):
                    ins = dve.scalar_tensor_tensor(o, pad[:, m % 4, j:j + T], taps[:, m, j:j + 1], o, ALU.mult, ALU.add)
                    if j < TAPS - 1:
                        link(ins)
                    else:
                        ins.then_inc(conved, 1)

            def gdn():
                link(dve.memset(flat(g_pad, "s w"), 0.0))
                dve.memset(g_E[:, 0, 0:1], 0.0).then_inc(SEM["g_pads"], 1)
                dve.wait_ge(SEM["g_gate_ps"], 1)
                dve.wait_ge(small_loaded, 16 * N_SMALL)
                logits = PS[2][:, 0:64].rearrange("p (t c) -> p t c", t=NT)
                link(dve.tensor_tensor(g_z, logits[:, :, 0:16], rows(g_bias, NT), ALU.add))
                link(dve.tensor_scalar(g_mx, g_z, 0.0, None, ALU.max))
                dve.scalar_tensor_tensor(g_ab, g_mx, -2.0, g_z, ALU.mult, ALU.add).then_inc(SEM["g_gateb"], 1)
                dve.wait_ge(SEM["g_gact"], 1)
                link(dve.tensor_tensor(g_z, g_mx, g_ab, ALU.add))
                dve.scalar_tensor_tensor(g_g, g_z, -1.0, rows(g_nega, NT), ALU.mult, ALU.mult).then_inc(SEM["g_gg"], 1)

                def tok_copy(gi):
                    dve.wait_ge(SEM["g_tokps"], gi + 1)
                    dve.tensor_copy(g_tok[:, :, 2 * gi:2 * gi + 2, :],
                                    PS[4 + gi % 4][:, :].rearrange("p (t e d) -> p t e d", t=NT, e=2)
                                    ).then_inc(SEM["g_toksb"], 1)

                for m in range(GC):
                    conv(m, g_pad, g_acc, g_conv, SEM["g_padded"], SEM["g_conved"], SEM["g_silued"])
                    if m >= 5 and m % 2:
                        tok_copy((m - 5) // 2)
                dve.wait_ge(SEM["g_cum"], 1)
                link(dve.tensor_copy(flat(g_gc, "t c"), PS[3][:, 0:32]))
                dve.tensor_tensor(flat(g_gt, "t c"), PS[3][:, 32:64], flat(g_gc, "t c"), ALU.subtract).then_inc(SEM["g_cumsb"], 1)
                tok_copy(10)
                tok_copy(11)
                dve.wait_ge(SEM["g_sqsum"], GH)
                dve.tensor_scalar(g_ms, g_ss, 1.0, EPS, ALU.mult, ALU.add).then_inc(SEM["g_mean"], 1)
                dve.wait_ge(SEM["g_root"], 1)
                polish(g_ms, g_root, g_inv, g_new, g_rstd)
                dve.wait_ge(SEM["g_toksb"], 12)
                for t in range(NT):
                    v = g_tok[:, t, 0:2 * GH, :]
                    dve.tensor_tensor(v, v, wide(g_rstd[:, t, :], P), ALU.mult).then_inc(SEM["g_qk"], 1)
                dve.wait_ge(SEM["g_exps"], 2)
                link(dve.tensor_scalar(g_egq, g_eg, P ** -0.5, None, ALU.mult))

                def decay(h):
                    dve.wait_ge(SEM["g_bc"], h + 1)
                    tmp = g_tmp[:, 2 * (h % 2):2 * (h % 2) + 2, :]
                    for c in range(NT):
                        lo = slice(c * P, (c + 1) * P)
                        dve.tensor_scalar(g_E[:, h, lo], PS[h % 2][:, lo], g_gc[:, c, h:h + 1], 0.0, ALU.subtract, ALU.min)
                        last = dve.tensor_scalar(tmp[:, c, :], PS[h % 2][:, T + c * P:T + (c + 1) * P],
                                                 g_gc[:, c, GH + h:GH + h + 1], 0.0, ALU.subtract, ALU.min)
                    last.then_inc(SEM["g_dexp"], 1)
                    dve.wait_ge(SEM["g_dexp"], h + 1)
                    dve.tensor_tensor(g_E[:, h, :], g_E[:, h, :], flat(tmp, "c d"), ALU.add).then_inc(SEM["g_logE"], 1)

                def system_rows(h):
                    dve.wait_ge(SEM["g_kq"], h + 1)
                    dve.wait_ge(SEM["g_E"], h + 1)
                    KE, QE, b = g_KE[:, h % 2, :], g_QE[:, h % 2, :], PS[2 + h % 2]
                    if h >= 2:
                        dve.wait_ge(SEM["g_P"], 2 * (h - 1))
                    dve.tensor_tensor(KE, b[:, 0:T], g_E[:, h, :], ALU.mult)
                    dve.scalar_tensor_tensor(QE, b[:, T:2 * T], P ** -0.5, g_E[:, h, :], ALU.mult, ALU.mult).then_inc(SEM["g_KE"], 1)
                    dve.wait_ge(SEM["g_KE"], h + 1)
                    for d in range(2):
                        for c in range(NT):
                            last = dve.scalar_tensor_tensor(
                                g_AT[:, system(d, h, c), :], KE[:, c * P:(c + 1) * P],
                                g_beta[:, c, d * GH + h:d * GH + h + 1],
                                const[:, C_LOS if d else C_UPS, :], ALU.mult, ALU.mult)
                    last.then_inc(SEM["g_A"], 1)

                dve.wait_ge(SEM["g_betas"], 1)
                for h in range(GH):
                    decay(h)
                    if h:
                        system_rows(h - 1)
                system_rows(GH - 1)

                for n in range(LEVELS * GB):
                    level, b = divmod(n, GB)
                    Tb, TTb = g_T[:, 4 * b:4 * b + 4, :], g_TT[:, 4 * b:4 * b + 4, :]

                    def bank(i):
                        return PS[i][:, :].rearrange("p (s d) -> p s d", s=4)

                    if level == 0:
                        dve.wait_ge(SEM["g_Yps"], n + 1)
                        dve.tensor_tensor(Tb, rows(ident, 4), bank(n % 2), ALU.subtract).then_inc(SEM["g_T"], 1)
                        dve.tensor_tensor(TTb, rows(ident, 4), g_mask[:, 4 * (n % 2):4 * (n % 2) + 4, :],
                                          ALU.subtract).then_inc(SEM["g_T"], 1)
                        continue
                    dve.wait_ge(SEM["g_Zps"], n - GB + 1)
                    if level < LEVELS - 1:
                        dve.tensor_tensor(Tb, Tb, bank(4 + n % 2), ALU.subtract).then_inc(SEM["g_T"], 1)
                    dve.tensor_tensor(TTb, TTb, bank(6 + n % 2), ALU.subtract).then_inc(SEM["g_T"], 1)

                def quad(v, q4, c):
                    d, h0 = q4 // 2, 4 * (q4 % 2)
                    return wide(v[:, c, d * GH + h0:d * GH + h0 + 4], P)

                def bank(i):
                    return PS[i][:, :].rearrange("p (s d) -> p s d", s=4)

                def vn(q4, c):
                    s = system(q4 // 2, 4 * (q4 % 2), c)
                    return g_vn[:, s:s + 7:2, :]

                for q4 in range(4):
                    dve.wait_ge(SEM["g_U0"], q4 + 1)
                    dve.tensor_tensor(vn(q4, q4 // 2), bank(q4), quad(g_beta, q4, q4 // 2), ALU.mult).then_inc(SEM["g_vn0"], 1)
                for q4 in range(4):
                    d, h0 = q4 // 2, 4 * (q4 % 2)
                    c = 1 - d
                    vp = g_vp[:, 4 * q4:4 * q4 + 4, :]
                    dve.wait_ge(SEM["g_RQ"], q4 + 1)
                    link(dve.tensor_tensor(vp, bank(q4), quad(g_eg, q4, c), ALU.mult))
                    dve.tensor_tensor(vp, g_tok[:, c, 2 * GH + h0:2 * GH + h0 + 4, :], vp, ALU.subtract).then_inc(SEM["g_v1"], 1)
                for q4 in range(4):
                    dve.tensor_tensor(g_inter[:, 4 * q4:4 * q4 + 4, :], bank(4 + q4), quad(g_egq, q4, 1 - q4 // 2),
                                      ALU.mult).then_inc(SEM["g_int"], 1)
                for q4 in range(4):
                    dve.wait_ge(SEM["g_U1"], q4 + 1)
                    dve.tensor_tensor(vn(q4, 1 - q4 // 2), bank(q4), quad(g_beta, q4, 1 - q4 // 2), ALU.mult).then_inc(SEM["g_vn1"], 1)
                dve.wait_ge(SEM["g_int"], 4)
                for c in range(NT):
                    for hg in range(2):
                        b = 2 * c + hg
                        dve.wait_ge(SEM["g_Ops"], b + 1)
                        q = (1 - c) * GH + 4 * hg
                        dve.tensor_tensor(g_o[:, 4 * b:4 * b + 4, :], bank(4 + b), g_inter[:, q:q + 4, :], ALU.add).then_inc(SEM["g_O"], 1)
                dve.wait_ge(SEM["g_O"], 4)
                link(dve.tensor_tensor(flat(g_sq, "s d"), flat(g_o, "s d"), flat(g_o, "s d"), ALU.mult))
                ss, ms, root, inv, new, rstd = (v[:, 0, :] for v in (g_ss, g_ms, g_root, g_inv, g_new, g_rstd))
                link(dve.tensor_reduce(ss, g_sq, AX.X, ALU.add))
                dve.tensor_scalar(ms, ss, 1.0 / P, EPS, ALU.mult, ALU.add).then_inc(SEM["g_omean"], 1)
                dve.wait_ge(SEM["g_oroot"], 1)
                polish(ms, root, inv, new, rstd)
                link(dve.tensor_tensor(g_o, g_o, wide(rstd, P), ALU.mult))
                dve.wait_ge(SEM["g_gz"], 2)
                for t in range(NT):
                    v = flat(g_o[:, t * GH:(t + 1) * GH, :], "s d")
                    dve.tensor_tensor(v, v, g_siluz[:, t, :], ALU.mult).then_inc(o_ready, 1)
                residual(at[("go", GH - 1)])

            def ssd():
                link(dve.memset(flat(s_pad, "s w"), 0.0))
                dve.memset(s_E[:, 0, 0, 0, 0:1], 0.0).then_inc(SEM["s_pads"], 1)
                dve.wait_ge(SEM["s_gate_ps"], 1)
                logits = PS[2][:, 0:128].rearrange("p (t c) -> p t c", t=NT)
                link(dve.tensor_tensor(s_z, logits, rows(s_bias, NT), ALU.add))
                link(dve.tensor_scalar(s_mx, s_z, 0.0, None, ALU.max))
                dve.scalar_tensor_tensor(s_ab, s_mx, -2.0, s_z, ALU.mult, ALU.add).then_inc(SEM["s_gateb"], 1)
                dve.wait_ge(SEM["s_gact"], 1)
                link(dve.tensor_tensor(s_dt, s_mx, s_ab, ALU.add))
                dve.scalar_tensor_tensor(s_da, s_dt, -1.0, rows(s_nega, NT), ALU.mult, ALU.mult).then_inc(SEM["s_da"], 1)

                def tok_copy(gi):
                    dve.wait_ge(SEM["s_tokps"], gi + 1)
                    dve.tensor_copy(s_tok[:, :, gi * T:(gi + 1) * T],
                                    PS[4 + gi % 4][:, :].rearrange("p (t w) -> p t w", t=NT)).then_inc(SEM["s_toksb"], 1)

                for m in range(SC):
                    conv(m, s_pad, s_acc, s_conv, SEM["s_padded"], SEM["s_conved"], SEM["s_silued"])
                    if m >= 5 and m % 2 and (m - 5) // 2 < SX // 2:
                        tok_copy((m - 5) // 2)
                dve.wait_ge(SEM["s_cum"], 1)
                link(dve.tensor_copy(flat(s_ac, "t c"), PS[3][:, 0:128]))
                dve.tensor_scalar(s_nac, s_ac, -1.0, None, ALU.mult).then_inc(SEM["s_nac"], 1)
                for g in range(SG):
                    dve.wait_ge(SEM["s_cbps"], g + 1)
                    for st in range(NT):
                        v = PS[6 + g % 2][:, st * T + st * P:st * T + (st + 1) * P]
                        w = PS[6 + g % 2][:, st * T + (1 - st) * P:st * T + (2 - st) * P]
                        dve.tensor_tensor(s_CB[:, g, st, 0, :], v, upper, ALU.mult)
                        dve.tensor_tensor(s_CB[:, g, st, 1, :], v, lower, ALU.mult)
                        last = dve.tensor_copy(s_CB[:, g, st, 2, :], w)
                    last.then_inc(SEM["s_cb"], 1)
                dve.wait_ge(SEM["s_cb"], SG)

                def decay(h):
                    dve.wait_ge(SEM["s_bc"], h + 1)
                    if h >= 2:
                        dve.wait_ge(SEM["s_mv"], h - 1)
                    for st in range(NT):
                        for d in range(2):
                            last = dve.tensor_scalar(s_E[:, h % 2, st, d, :], PS[h % 2][:, d * T + st * P:d * T + (st + 1) * P],
                                                     s_ac[:, st, d * SH + h:d * SH + h + 1], 0.0, ALU.subtract, ALU.min)
                    last.then_inc(SEM["s_d"], 1)

                def weigh(h):
                    g = h // SR
                    dve.wait_ge(SEM["s_e"], h + 1)
                    if h >= 2:
                        dve.wait_ge(SEM["s_yps"], h - 1)
                    for st in range(NT):
                        for part in (0, 1, 2):
                            d = part if part < 2 else st
                            last = dve.scalar_tensor_tensor(
                                s_M[:, h % 2, st, part, :], s_CB[:, g, st, part, :], s_dt[:, st, d * SH + h:d * SH + h + 1],
                                s_E[:, h % 2, st, part, :], ALU.mult, ALU.mult)
                    last.then_inc(SEM["s_mv"], 1)

                def group_out(g):
                    for lt in range(NT):
                        dve.wait_ge(SEM["s_yps"], SR * (g + 1))
                        v = slice(g * 512, (g + 1) * 512)
                        dve.tensor_tensor(s_y[:, lt, v], PS[2 + 2 * (g % 2) + lt][:, :], s_skip[:, lt, v], ALU.add).then_inc(SEM["s_y"], 1)

                dve.wait_ge(SEM["s_skip"], 2)
                for h in range(SH):
                    decay(h)
                    if h:
                        weigh(h - 1)
                    if h > SR and h % SR == 3:
                        group_out(h // SR - 1)
                weigh(SH - 1)
                group_out(SG - 1)
                dve.wait_ge(SEM["s_ss"], NT * SG)
                dve.tensor_scalar(s_ms, s_ss, 1.0 / 512, EPS, ALU.mult, ALU.add).then_inc(SEM["s_mean"], 1)
                dve.wait_ge(SEM["s_root"], 1)
                polish(s_ms, s_root, s_inv, s_new, s_rstd)
                dve.wait_ge(gain_loaded, 16)
                for g in range(SG):
                    for t in range(NT):
                        v = s_y[:, t, g * 512:(g + 1) * 512]
                        dve.scalar_tensor_tensor(v, v, s_rstd[:, t, g:g + 1], s_gain[:, g * 512:(g + 1) * 512],
                                                 ALU.mult, ALU.mult).then_inc(o_ready, 1)
                residual(at[("so", SX - 1)])

            def top16(values, rest, top, idx):
                link(dve.max(top[:, 0:8], values))
                dve.max_index(idx[:, 0:8], top[:, 0:8], values)
                link(dve.match_replace(rest, top[:, 0:8], values, NEG))
                link(dve.max(top[:, 8:16], rest))
                dve.max_index(idx[:, 8:16], top[:, 8:16], rest)

            def route(lyr):
                for half in range(2):
                    for t in range(NT):
                        for hq in range(2):
                            dve.wait_ge(SEM["p_s"], 8 * lyr + 4 * half + 2 * t + hq + 1)
                            for e in range(4):
                                hp = 8 * half + 4 * hq + e
                                top16(p_s[:, t, hp, :], p_s2[:, t, hp, :], p_top[:, t, hp, :], p_idx[:, t, hp, :])
                link(dve.memset(p_sum, 0.0))
                link(dve.tensor_copy(flat(p_idxf, "t h k"), flat(p_idx, "t h k")))
                halves = p_top.rearrange("p t (h e) k -> p (t h) e k", e=2)
                first = halves[:, :, 0, :].rearrange("p h (k o) -> p h k o", o=1)
                second = halves[:, :, 1, :].rearrange("p h (o k) -> p h o k", o=1)
                grid = [P, PH, TOPK, TOPK]
                for t in range(NT):
                    hs = slice(t * PH, (t + 1) * PH)
                    link(dve.tensor_tensor(p_cand[:, hs, :].rearrange("p h (a b) -> p h a b", a=TOPK),
                                           first[:, hs].to_broadcast(grid), second[:, hs].to_broadcast(grid), ALU.add))
                for r in range(NT * PH):
                    top16(p_cand[:, r, :], p_cand2[:, r, :], p_best[:, r, :], p_pos[:, r, :])
                link(dve.memset(p_rsum, 0.0))
                dve.tensor_tensor(p_gate, p_best, p_best[:, :, 0:1].to_broadcast([P, NT * PH, TOPK]),
                                  ALU.subtract).then_inc(SEM["p_ex"], 1)
                link(dve.tensor_scalar(p_ab[:, 0], p_pos, 4, None, ALU.logical_shift_right))
                link(dve.tensor_scalar(p_ab[:, 1], p_pos, 15, None, ALU.bitwise_and))
                link(dve.tensor_copy(flat(p_abf, "e h k"), flat(p_ab, "e h k")))
                hot = p_hot.rearrange("p h (k a) -> p h k a", a=TOPK)
                idx = p_idxf.rearrange("p t (h e) k -> p (t h) e k", e=2)
                full = [P, NT * PH, TOPK, TOPK]
                lane = const[:, C_IOTA, 0:TOPK].rearrange("p (o q k) -> p o q k", o=1, q=1)
                for e in range(2):
                    place = p_abf[:, e].rearrange("p h (k o) -> p h k o", o=1)
                    link(dve.tensor_tensor(hot, place.to_broadcast(full), lane.to_broadcast(full), ALU.is_equal))
                    names = idx[:, :, e, :].rearrange("p h (o k) -> p h o k", o=1)
                    link(dve.tensor_tensor(hot, hot, names.to_broadcast(full), ALU.mult))
                    link(dve.tensor_reduce(p_key[:, e], hot, AX.X, ALU.add))
                dve.wait_ge(SEM["p_exd"], lyr + 1)
                link(dve.tensor_reduce(p_sum, p_gate, AX.X, ALU.add))
                link(dve.reciprocal(p_rsum, p_sum))
                dve.tensor_tensor(p_gate, p_gate, wide(p_rsum, TOPK), ALU.mult).then_inc(SEM["p_key"], 1)
                dve.wait_ge(SEM["p_Tps"], lyr + 1)
                dve.tensor_copy(flat(p_T[:, 0:2], "e t"), PS[6][:, :])
                link(dve.tensor_copy(p_T[:, 2], PS[7][:, 0:T]))

                def tokens8(it, first=False):
                    for u in range(8):
                        if not first and u % 4 == 0:
                            dve.wait_ge(SEM["p_mapps"], it * 2 + (64 * lyr + u // 4 - 1))
                        tok = bass.ds(it * 8 + u, 1)
                        dve.tensor_scalar(p_A[:, u, :], iota, p_T[:, 0, tok], p_T[:, 2, tok], ALU.is_equal, ALU.mult)
                        dve.tensor_scalar(p_B[:, u, :], iota, p_T[:, 1, tok], None, ALU.is_equal).then_inc(SEM["p_hot"], 1)

                tokens8(0, True)
                with dve.Fori(1, T // 8) as it:
                    tokens8(it)

            def experts(lyr):
                n0 = tables[lyr]

                def gated(i, it=None):
                    if it is None:
                        dve.wait_ge(SEM["p_gelu"], P * lyr + i + 1)
                        row = p_map[:, i, :]
                    else:
                        dve.wait_ge(SEM["p_gelu"], it * 2 + (P * lyr + i + 1))
                        dve.wait_ge(unit_used, it * 4 + (n0 + 2 * i - 1))
                        row = flat(p_map[:, bass.ds(it * 2 + i, 1), :], "i t")
                    dve.tensor_tensor(p_ag[:, i % 2, :], p_act[:, i % 2, :], row, ALU.mult).then_inc(SEM["p_ag"], 1)

                dve.wait_ge(SEM["p_map"], 64 * (lyr + 1))
                gated(0)
                gated(1)
                with dve.Fori(0, P // 2 - 1) as it:
                    gated(2, it)
                    gated(3, it)
                residual(n0 + 2 * P - 1)

            dve.wait_ge(x_loaded, 16)
            norm(0)
            gdn()
            norm(1)
            route(0)
            experts(0)
            norm(2)
            ssd()
            norm(3)
            route(1)
            experts(1)
            norm_stats(4)
            dve.wait_ge(last_gain_loaded, 16)
            for t in range(NT):
                ins = dve.scalar_tensor_tensor(x_sb[:, t, :], x_sb[:, t, :], n_rstd[:, t:t + 1], last_gain, ALU.mult, ALU.mult)
            ins.then_inc(SEM["finished"], 1)

        @block.scalar
        def _(act):
            def copy(o, i, scale=1.0):
                return act.activation(o, i, ACT.Copy, scale=scale)

            def norm_squares(i):
                for t in range(NT):
                    act.activation(h_junk, x_sb[:, t, :], ACT.Square, accum_out=n_ss[:, t:t + 1]).then_inc(n_sq, 1)
                    act.wait_ge(n_sq, 2 * i + t + 1)
                act.wait_ge(n_mean, i + 1)
                act.activation(n_root, n_ms, ACT.Sqrt).then_inc(n_rooted, 1)

            def norm(i):
                if i:
                    act.wait_ge(x_added, 4 * i)
                else:
                    act.wait_ge(x_loaded, 16)
                    act.wait_ge(small_loaded, 16 * N_SMALL)
                norm_squares(i)
                for k in range(KD):
                    act.wait_ge(n_hTps, 4 * i + k // 2 + 1)
                    copy(hT[:, k, :], PS[k // 2][:, (k % 2) * T:(k % 2 + 1) * T], norm_w[:, i, k:k + 1]).then_inc(n_hT, 1)

            def softplus_tail(ab, exps, n):
                act.activation(ab, ab, ACT.Exp).then_inc(exps, 1)
                act.wait_ge(exps, n)
                return act.activation(ab, ab, ACT.Ln, bias=1.0)

            def gdn():
                for hf in range(2):
                    act.wait_ge(unit_used, at[("gz", hf, 3)] + 1)
                    for t in range(NT):
                        act.activation(g_siluz[:, t, hf * 512:(hf + 1) * 512], PS[4 + 2 * hf + t][:, :], ACT.Silu).then_inc(SEM["g_zs"], 1)
                act.wait_ge(SEM["g_gateb"], 1)
                act.activation(g_beta, PS[2][:, 0:64].rearrange("p (t c) -> p t c", t=NT)[:, :, 16:32], ACT.Sigmoid).then_inc(SEM["g_betas"], 1)
                act.activation(g_nega, g_alog, ACT.Exp)
                softplus_tail(g_ab, SEM["g_gexp"], 1).then_inc(SEM["g_gact"], 1)

                def silu(m):
                    act.wait_ge(SEM["g_conved"], m + 1)
                    act.activation(g_feat[:, m, :], g_acc[:, m % 4, :], ACT.Silu).then_inc(SEM["g_silued"], 1)

                act.wait_ge(SEM["g_pads"], 1)
                for m in range(GC):
                    act.wait_ge(unit_used, at[("gq", m)] + 1)
                    if m >= 4:
                        act.wait_ge(SEM["g_conved"], m - 3)
                    copy(g_pad[:, m % 4, 2:2 + T], PS[m % 2][:, 0:T]).then_inc(SEM["g_padded"], 1)
                    if m:
                        silu(m - 1)
                    if m >= 5 and m % 2 and (m - 5) // 2 < GH:
                        gi = (m - 5) // 2
                        act.wait_ge(SEM["g_toksb"], gi + 1)
                        for t in range(NT):
                            for e in range(2):
                                last = act.activation(h_junk[:, 0:P], g_tok[:, t, 2 * gi + e, :],
                                                      ACT.Square, accum_out=g_ss[:, t, 2 * gi + e:2 * gi + e + 1])
                                if 2 * t + e < 3:
                                    last.then_inc(SEM["g_junk"], 1)
                                    act.wait_ge(SEM["g_junk"], 3 * gi + 2 * t + e + 1)
                        last.then_inc(SEM["g_sqsum"], 1)
                        act.wait_ge(SEM["g_sqsum"], gi + 1)
                silu(GC - 1)
                act.wait_ge(SEM["g_cumsb"], 1)
                act.activation(g_eg, g_gc, ACT.Exp).then_inc(SEM["g_exps"], 1)
                act.activation(g_wx, g_gt, ACT.Exp).then_inc(SEM["g_exps"], 1)
                copy(g_row, PS[2][0:GH, :]).then_inc(SEM["g_rows"], 1)
                act.wait_ge(SEM["g_mean"], 1)
                act.activation(g_root, g_ms, ACT.Sqrt).then_inc(SEM["g_root"], 1)
                for gi in range(GH):
                    act.wait_ge(SEM["g_backps"], gi + 1)
                    copy(g_feat[:, 2 * gi:2 * gi + 2, :], PS[4 + gi % 4][:, :].rearrange("p (e t) -> p e t", e=2)).then_inc(SEM["g_backsb"], 1)
                for h in range(GH):
                    act.wait_ge(SEM["g_logE"], h + 1)
                    act.activation(g_E[:, h, :], g_E[:, h, :], ACT.Exp).then_inc(SEM["g_E"], 1)
                for n in range(GB, LEVELS * GB):
                    b = n % GB
                    act.wait_ge(SEM["g_Yps"], n + 1)
                    copy(g_Y[:, 4 * b:4 * b + 4, :], PS[n % 2][:, :].rearrange("p (s d) -> p s d", s=4)).then_inc(SEM["g_Y"], 1)
                for q4 in range(4):
                    act.wait_ge(SEM["g_S1ps"], q4 + 1)
                    copy(g_S[:, 4 * q4:4 * q4 + 4, :], PS[4 + q4][:, :].rearrange("p (s d) -> p s d", s=4)).then_inc(SEM["g_S1"], 1)
                act.wait_ge(SEM["g_omean"], 1)
                act.activation(g_root[:, 0, :], g_ms[:, 0, :], ACT.Sqrt).then_inc(SEM["g_oroot"], 1)
                for b in range(4):
                    act.wait_ge(oT_psum, b + 1)
                    copy(hT[:, 2 * b:2 * b + 2, :], PS[b][:, :].rearrange("p (e t) -> p e t", e=2)).then_inc(oT_ready, 1)

            def ssd():
                for nb in range(SI // 512):
                    act.wait_ge(unit_used, at[("sz", nb, 3)] + 1)
                    for t in range(NT):
                        act.activation(s_siluz[:, t, nb * 512:(nb + 1) * 512], PS[4 + 2 * (nb % 2) + t][:, :], ACT.Silu).then_inc(SEM["s_zs"], 1)
                act.activation(s_nega, s_alog, ACT.Exp)
                act.wait_ge(SEM["s_gateb"], 1)
                softplus_tail(s_ab, SEM["s_gexp"], 1).then_inc(SEM["s_gact"], 1)

                def silu(m):
                    act.wait_ge(SEM["s_conved"], m + 1)
                    act.activation(s_feat[:, m, :], s_acc[:, m % 4, :], ACT.Silu, bias=s_cbias[:, m:m + 1]).then_inc(SEM["s_silued"], 1)

                act.wait_ge(SEM["s_pads"], 1)
                for m in range(SC):
                    act.wait_ge(unit_used, at[("sx", m)] + 1)
                    if m >= 4:
                        act.wait_ge(SEM["s_conved"], m - 3)
                    copy(s_pad[:, m % 4, 2:2 + T], PS[m % 2][:, 0:T]).then_inc(SEM["s_padded"], 1)
                    if m:
                        silu(m - 1)
                silu(SC - 1)
                act.wait_ge(SEM["s_cum"], 1)
                copy(s_row, PS[2][0:SH, :]).then_inc(SEM["s_rows"], 1)
                act.wait_ge(SEM["s_nac"], 1)

                def group_squares(g):
                    for t in range(NT):
                        act.wait_ge(SEM["s_yg"], 2 * g + t + 1)
                        act.activation(h_junk[:, 0:512], s_y[:, t, g * 512:(g + 1) * 512], ACT.Square,
                                       accum_out=s_ss[:, t, g:g + 1]).then_inc(SEM["s_ss"], 1)
                        act.wait_ge(SEM["s_ss"], 2 * g + t + 1)

                for h in range(SH):
                    act.wait_ge(SEM["s_bc"], h + 1)
                    if h >= 2:
                        act.wait_ge(SEM["s_mv"], h - 1)
                    act.wait_ge(SEM["s_d"], h + 1)
                    act.activation(s_E[:, h % 2, 0, 2, :], PS[h % 2][:, P:2 * P], ACT.Exp, bias=s_nac[:, 0, h:h + 1])
                    act.activation(s_E[:, h % 2, 1, 2, :], PS[h % 2][:, T:T + P], ACT.Exp, bias=s_nac[:, 1, SH + h:SH + h + 1])
                    v = s_E[:, h % 2, :, 0:2, :].rearrange("p t e d -> p t (e d)")
                    act.activation(v, v, ACT.Exp).then_inc(SEM["s_e"], 1)
                    if h > SR and h % SR == 5:
                        group_squares(h // SR - 1)
                group_squares(SG - 1)
                act.wait_ge(SEM["s_mean"], 1)
                act.activation(s_root, s_ms, ACT.Sqrt).then_inc(SEM["s_root"], 1)
                for gi in range(SX // 2):
                    act.wait_ge(oT_psum, 4 + gi + 1)
                    copy(s_yT[:, 2 * gi:2 * gi + 2, :], PS[gi % 4][:, :].rearrange("p (e t) -> p e t", e=2)).then_inc(oT_ready, 1)

            def route(lyr):
                for m in range(HP):
                    act.wait_ge(unit_used, at[("pq", lyr, m)] + 1)
                    copy(p_qT[:, m, :], PS[m % 2][:, 0:T]).then_inc(SEM["p_q"], 1)
                for half in range(2):
                    for t in range(NT):
                        for hq in range(2):
                            g = 4 * half + 2 * t + hq
                            if g % 4 == 3:
                                act.wait_ge(unit_used, at[("pk", lyr, half)] + 1)
                            else:
                                act.wait_ge(SEM["p_sps"], 6 * lyr + 3 * half + g % 4 + 1)
                            hp = 8 * half + 4 * hq
                            copy(p_s[:, t, hp:hp + 4, :], PS[2 + g % 4][:, :].rearrange("p (e k) -> p e k", e=4)).then_inc(SEM["p_s"], 1)
                act.wait_ge(SEM["p_ex"], lyr + 1)
                act.activation(p_gate, p_gate, ACT.Exp).then_inc(SEM["p_exd"], 1)

                def tokens8(it):
                    for half in range(2):
                        act.wait_ge(SEM["p_mapps"], it * 2 + (64 * lyr + half + 1))
                        copy(p_map[:, :, bass.ds(it * 8 + 4 * half, 4)],
                             PS[half][:, :].rearrange("p (t i) -> p i t", t=4)).then_inc(SEM["p_map"], 1)

                with act.Fori(0, T // 8) as it:
                    tokens8(it)

            def experts(lyr):
                n0 = tables[lyr]

                def gelu(i, k, it=None):
                    if it is None:
                        act.wait_ge(unit_used, n0 + k + 1)
                    else:
                        act.wait_ge(unit_used, it * 4 + (n0 + k + 1))
                        act.wait_ge(SEM["p_ag"], it * 2 + (P * lyr + i - 1))
                    act.activation(p_act[:, i % 2, :], PS[i % 2][:, 0:T], ACT.Gelu).then_inc(SEM["p_gelu"], 1)

                gelu(0, 0)
                gelu(1, 1)
                with act.Fori(0, P // 2 - 1) as it:
                    gelu(2, 3, it)
                    gelu(3, 5, it)

            norm(0)
            gdn()
            norm(1)
            route(0)
            experts(0)
            norm(2)
            ssd()
            norm(3)
            route(1)
            experts(1)
            act.wait_ge(x_added, 16)
            norm_squares(4)

        @block.gpsimd
        def _(pool):
            def rows(v, n):
                return v.rearrange("p (o c) -> p o c", o=1).to_broadcast([v.shape[0], n, v.shape[1]])

            def wide(v, n):
                return v.rearrange("p (a o) -> p a o", o=1).to_broadcast([v.shape[0], v.shape[1], n])

            loads = [(const[:, :, :], a["const"]), (levels[:, :, :], a["levels"]), (norm_w, a["norms"]),
                     (g_conv, a["gdn_conv"]), (g_wg[:, :, :], a["gdn_gates"]),
                     (g_bias, a["gdn_dt_bias"].partition_broadcast(P)), (g_alog, a["gdn_a_log"].partition_broadcast(P)),
                     (g_gain[:, :], a["gdn_norm"].partition_broadcast(P)),
                     (s_conv, a["ssd_conv"]), (s_cbias, a["ssd_conv_b"]), (s_wg[:, :, :], a["ssd_gates"]),
                     (s_bias, a["ssd_dt_bias"].partition_broadcast(P)), (s_alog, a["ssd_a_log"].partition_broadcast(P)),
                     (s_D, a["ssd_d"].partition_broadcast(P))]
            assert len(loads) == N_SMALL
            for o, i in loads:
                pool.dma_start(o, i).then_inc(small_loaded, 16)
            pool.wait_ge(small_loaded, 16 * N_SMALL)
            pool.wait_ge(SEM["g_zs"], 4)
            for t in range(NT):
                v = g_siluz[:, t, :].rearrange("p (h d) -> p h d", h=GH)
                pool.tensor_tensor(v, v, rows(g_gain[:, :], GH), ALU.mult).then_inc(SEM["g_gz"], 1)
            for h in range(GH):
                pool.wait_ge(SEM["g_KE"], h + 1)
                for d in range(2):
                    v = g_QE[:, h % 2, :].rearrange("p (c i) -> p c i", c=NT)
                    s = system(d, h, 0)
                    pool.tensor_tensor(g_PT[:, s:s + 2, :], v, rows(lower if d else upper, NT), ALU.mult).then_inc(SEM["g_P"], 1)
            for n in range(LEVELS * GB):
                level, b = divmod(n, GB)
                if n < GB:
                    pool.wait_ge(SEM["g_A"], 2 * (b % 4) + 2)
                if n >= 2:
                    pool.wait_ge(SEM["g_Yps"], n - 1)
                    if n - 2 < GB:
                        pool.wait_ge(SEM["g_T"], t_count(n - 2))
                d = b // (GB // 2)
                pool.tensor_tensor(g_mask[:, 4 * (n % 2):4 * (n % 2) + 4, :], g_AT[:, 4 * b:4 * b + 4, :],
                                   rows(levels[:, d * LEVELS + level, :], 4), ALU.mult).then_inc(SEM["g_mask"], 1)
            pool.wait_ge(SEM["g_U0"], 1)
            for q4 in range(4):
                d, h0 = q4 // 2, 4 * (q4 % 2)
                pool.tensor_tensor(g_kS[:, 4 * q4:4 * q4 + 4, :], g_tok[:, d, GH + h0:GH + h0 + 4, :],
                                   wide(g_wx[:, d, d * GH + h0:d * GH + h0 + 4], P), ALU.mult).then_inc(SEM["g_kS"], 1)
            pool.wait_ge(n_hT, 3 * KD)
            pool.dma_start(s_gain, a["ssd_norm"].partition_broadcast(P)).then_inc(gain_loaded, 16)
            pool.wait_ge(SEM["s_toksb"], SX // 2)
            for t in range(NT):
                v = s_tok[:, t, :].rearrange("p (h d) -> p h d", h=SH)
                pool.tensor_tensor(s_skip[:, t, :].rearrange("p (h d) -> p h d", h=SH), v, wide(s_D, SP_),
                                   ALU.mult).then_inc(SEM["s_skip"], 1)
            pool.wait_ge(SEM["s_zs"], 8)
            for h in range(SH):
                pool.wait_ge(SEM["s_mv"], h + 1)
                m = s_M[:, h % 2]
                pool.tensor_tensor(m[:, :, 0, :], m[:, :, 0, :], m[:, :, 1, :], ALU.add).then_inc(SEM["s_m"], 1)
                if h > SR and h % SR == 4 or h == SH - 1:
                    g = h // SR - (h != SH - 1)
                    for t in range(NT):
                        pool.wait_ge(SEM["s_y"], 2 * g + t + 1)
                        v = s_y[:, t, g * 512:(g + 1) * 512]
                        pool.tensor_tensor(v, v, s_siluz[:, t, g * 512:(g + 1) * 512], ALU.mult).then_inc(SEM["s_yg"], 1)


def layout(i):
    c = np.ascontiguousarray

    def by_token(w):
        n = w.shape[1] // 512
        return c(w.reshape(KD // 2, 2, P, n, 512).transpose(3, 0, 2, 1, 4).reshape(n, KD // 2, P, D))

    def by_channel(w):
        n = w.shape[1] // P
        return c(w.reshape(KD, P, n, P).transpose(2, 1, 0, 3).reshape(n, P, D))

    def gates(w):
        return c(w.reshape(KD, P, -1).transpose(1, 0, 2))

    def taps(w):
        return c(w.reshape(TAPS, -1, P).transpose(2, 1, 0))

    masks, levels = host_constants()
    g, s = i["gdn_w_in"][0], i["ssd_w_in"][0]
    qkv, ch = GC * P, SC * P
    return {
        "x": c(i["x"][0].reshape(NT, P, D).transpose(1, 0, 2)),
        "const": masks, "levels": levels.astype(np.float16),
        "norms": c(np.stack([i["norm_mix"][0], i["norm_ffn"][0], i["norm_mix"][1], i["norm_ffn"][1]])
                   .reshape(4, KD, P).transpose(2, 0, 1)),
        "norm_final": i["norm_final"],
        "gdn_qkv": by_channel(g[:, :qkv]), "gdn_z": by_token(g[:, qkv:qkv + D]), "gdn_gates": gates(g[:, qkv + D:]),
        "gdn_conv": taps(i["gdn_conv"][0]), "gdn_a_log": c(i["gdn_a_log"][0].reshape(-1)),
        "gdn_dt_bias": c(i["gdn_dt_bias"][0].reshape(-1)), "gdn_norm": c(i["gdn_norm"][0]),
        "gdn_out": c(i["gdn_w_out"][0].reshape(GH, P, D)),
        "ssd_z": by_token(s[:, :SI]), "ssd_xbc": by_channel(s[:, SI:SI + ch]), "ssd_gates": gates(s[:, SI + ch:]),
        "ssd_conv": taps(i["ssd_conv"][0]), "ssd_conv_b": c(i["ssd_conv_b"][0].reshape(SC, P).T),
        "ssd_a_log": c(i["ssd_a_log"][0].reshape(-1)), "ssd_dt_bias": c(i["ssd_dt_bias"][0].reshape(-1)),
        "ssd_d": c(i["ssd_d"][0]), "ssd_norm": c(i["ssd_norm"][0]), "ssd_out": c(i["ssd_w_out"][0].reshape(SX, P, D)),
        "peer_wq": np.stack([by_channel(i["peer_w_q"][n]) for n in range(2)]),
        "peer_kT": c(i["peer_keys"].reshape(2, 2, HP // 2, P, P).transpose(0, 1, 4, 2, 3).reshape(2, 2, P, D)),
        "peer_u": c(i["peer_u"].reshape(2, P, P, KD, P).transpose(0, 1, 4, 3, 2).reshape(2, P, P, D)),
        "peer_v": c(i["peer_v"].reshape(2, P, P, D)),
    }


def kernel(**inputs):
    import concourse.bacc as _bacc
    from concourse.bass_utils import run_bass_kernel_spmd as _run

    arrays = layout({k: np.asarray(v) for k, v in inputs.items()})
    nc = _bacc.Bacc("TRN2", target_bir_lowering=False, num_devices=1)
    a = {k: nc.dram_tensor(f"in_{k}", v.shape, mybir.dt.from_np(v.dtype), kind="ExternalInput").ap()
         for k, v in arrays.items()}
    out = nc.dram_tensor("out", (P, NT, D), F32, kind="ExternalOutput").ap()
    hybrid_encoder(nc, a, out)
    r = _run(nc, [{f"in_{k}": v for k, v in arrays.items()}], core_ids=[0])
    got = r.results[0]["out"]
    return np.ascontiguousarray(got.transpose(1, 0, 2)).reshape(1, T, D)
```

```python
from contextlib import ExitStack

import numpy as np

import concourse.bass as bass
from concourse import mybir

F32 = mybir.dt.float32
F32R = mybir.dt.float32r
U32 = mybir.dt.uint32
ALU = mybir.AluOpType
ACT = mybir.ActivationFunctionType
AX = mybir.AxisListType

P = 128
D = 1024
KD = D // P
T = 256
NT = T // P
EPS = 1e-6
TAPS = 5

GH = 8
GC = 3 * GH
GSYS = 2 * GH * NT
GB = GSYS // 4
LEVELS = 7

SH = 32
SP_ = 64
SG = 4
SR = SH // SG
SI = SH * SP_
SX = SI // P
SC = SX + 2 * SG

PH = 8
HP = 2 * PH
TOPK = 16
NEG = -3.0e38

RING = 4
SPLIT = 4
EARLY = 48


def host_constants():
    j, i = np.arange(P)[:, None], np.arange(P)[None, :]
    rows = [j == i, j <= i, j >= i, j < i, j > i, np.ones((P, P)), np.broadcast_to(i, (P, P))]
    levels = []
    for flip in (False, True):
        for level in range(LEVELS):
            b = 1 << level
            hi, lo = (j, i) if flip else (i, j)
            levels.append((hi // b % 2 == 1) & (lo // b == hi // b - 1))
    return [np.stack([np.asarray(r, np.float32) for r in m], axis=1) for m in (rows, levels)]


C_EYE, C_UPI, C_LOI, C_UPS, C_LOS, C_ONE, C_IOTA, C_ALL = range(8)


def weight_stream(a):
    order = []
    for hf in range(2):
        order += [(("gz", hf, k), a["gdn_z"][hf, k]) for k in range(KD // 2)]
    order += [(("gq", m), a["gdn_qkv"][m]) for m in range(GC)]
    order += [(("go", k), a["gdn_out"][k]) for k in range(GH)]
    tables = []

    def peer(lyr):
        run = [(("pq", lyr, m), a["peer_wq"][lyr, m]) for m in range(HP)]
        tables.append(len(order) + len(run))
        return run + [None] * (2 * P)

    order += peer(0)
    for nb in range(SI // 512):
        order += [(("sz", nb, k), a["ssd_z"][nb, k]) for k in range(KD // 2)]
    order += [(("sx", m), a["ssd_xbc"][m]) for m in range(SC)]
    order += [(("so", k), a["ssd_out"][k]) for k in range(SX)]
    order += peer(1)
    return order, {o[0]: n for n, o in enumerate(order) if o is not None}, tables


def hybrid_encoder(nc, a, out):
    order, at, tables = weight_stream(a)
    ctx = ExitStack()
    with ctx:
        def sb(name, shape, dt=F32):
            return ctx.enter_context(nc.sbuf_tensor(name, shape, dt))

        def sem(name):
            return ctx.enter_context(nc.semaphore(name))

        PS = [ctx.enter_context(nc.psum_tensor(f"bank{i}", [P, 512], F32)) for i in range(8)]

        def cutter(tensor, size):
            at_column = [0]

            def take(*shape, dt=None):
                n = int(np.prod(shape))
                v = tensor[:, at_column[0]:at_column[0] + n]
                at_column[0] += n
                assert at_column[0] <= size, at_column
                if dt is not None:
                    v = v.bitcast(dt)
                if len(shape) > 1:
                    names = "abcd"[:len(shape)]
                    v = v.rearrange(f"p ({' '.join(names)}) -> p {' '.join(names)}", **dict(zip(names, shape)))
                return v

            return take

        def system(direction, head, chunk):
            return (direction * GH + head) * NT + chunk

        def t_count(n):
            return 2 * (n + 1) if n < (LEVELS - 1) * GB else 2 * (LEVELS - 1) * GB + n - (LEVELS - 1) * GB + 1

        def flat(v, names):
            return v.rearrange(f"p {names} -> p ({names})")

        x_sb = sb("x_sb", [P, NT, D])
        hT = [sb("hT_" + s, [P, KD, T], F32R) for s in ("hi", "lo")]
        ring = sb("ring", [P, RING, D])
        w_part = [sb("w_" + s, [P, SPLIT, D // 2], F32R) for s in ("hi", "lo")]
        p_ag = [sb("p_ag_" + s, [P, 2, T], F32R) for s in ("hi", "lo")]
        const = sb("const", [P, C_ALL, P])
        arena = sb("arena", [P, P * T])
        work = sb("work", [P, 1792])
        small = sb("small", [P, 2048])
        h_tok = arena[:, 14336:14336 + NT * D].rearrange("p (t d) -> p t d", t=NT)
        h_junk = arena[:, 18432:18432 + D]
        last_gain = ring[:, 0, :]

        ident = const[:, C_EYE, :]
        upper = const[:, C_UPI, :]
        lower = const[:, C_LOI, :]
        ones = const[:, C_ONE, :]
        iota = const[:, C_IOTA, :]

        tiny = cutter(small, 2048)
        norm_w = tiny(4, KD)
        n_ss, n_ms, n_root, n_inv, n_new, n_rstd = (tiny(NT) for _ in range(6))
        g_ss, g_ms, g_root, g_inv, g_new, g_rstd = (tiny(NT, 2 * GH) for _ in range(6))

        g_conv = tiny(GC, TAPS)
        g_bias, g_alog, g_nega = (tiny(2 * GH) for _ in range(3))
        g_z, g_mx, g_ab, g_g, g_beta, g_gc, g_gt, g_wx, g_eg, g_egq = (tiny(NT, 2 * GH) for _ in range(10))
        take = cutter(work, 1792)
        levels = take(LEVELS * P).bitcast(mybir.dt.float16).rearrange("p (l d) -> p l d", d=P)
        g_wg = take(KD, 4 * GH)
        g_gain = take(1, P)
        take = cutter(arena, P * T)
        g_feat = take(GC, T)
        g_tok = take(NT, GC, P)
        g_siluz = take(NT, D)
        g_AT = take(GSYS, P)
        g_T = take(GSYS, P)
        g_TT = take(GSYS, P)
        g_Y = take(GSYS, P)
        spare = take(2048)
        g_pad = flat(g_Y, "s d")[:, 0:4 * 260].rearrange("p (s w) -> p s w", s=4)
        g_acc = flat(g_Y, "s d")[:, 1040:1040 + 4 * T].rearrange("p (s w) -> p s w", s=4)
        g_E = g_feat[:, 2 * GH:3 * GH, :]
        g_tmp = g_Y[:, 0:16, :]
        g_KE = spare[:, 0:512].rearrange("p (s w) -> p s w", s=2)
        g_PTb = spare.rearrange("p (h c d) -> p h c d", h=GH, c=NT)
        g_row = spare[0:GH, 1024:1536]
        g_mask = g_tok[:, 0, 0:GH, :]
        g_vn = g_T
        g_kS = g_Y[:, 0:16, :]
        g_S = g_Y[:, 16:32, :]
        g_vp = g_AT[:, 0:16, :]
        g_inter = g_AT[:, 16:32, :]
        g_o = g_TT[:, 0:16, :]
        g_sq = g_TT[:, 16:32, :]

        s_conv = tiny(SC, TAPS)
        s_cbias = tiny(SC)
        s_wg = work[:, 0:KD * 2 * SH].rearrange("p (k c) -> p k c", k=KD)
        s_bias, s_alog, s_nega, s_D = tiny(2 * SH), tiny(2 * SH), tiny(2 * SH), tiny(SH)
        s_z, s_mx, s_ab, s_dt, s_da, s_ac, s_nac = (tiny(NT, 2 * SH) for _ in range(7))
        s_ss, s_ms, s_root, s_inv, s_new, s_rstd = (tiny(NT, SG) for _ in range(6))
        take = cutter(arena, P * T)
        s_feat = take(SC, T)
        s_tok = take(NT, SI)
        s_siluz = take(NT, SI)
        s_y = take(NT, SI)
        s_skip = take(NT, SI)
        s_CB = take(SG, NT, 3, P)
        s_pad = take(4, 260)
        s_acc = take(4, T)
        s_row = take(2 * T)[0:SH, :]
        s_E = take(2, NT, 3, P)
        s_M = take(2, NT, 3, P)
        s_junk = take(512)
        s_gain = arena[:, 25600:25600 + SI]

        take = cutter(arena, P * T)
        take(EARLY * T)
        p_qT = take(HP, T)
        p_s = take(NT, HP, P)
        p_cand = take(NT * PH, TOPK * TOPK)
        p_kT = flat(p_cand, "h k")[:, 0:HP * P].rearrange("p (h k) -> p h k", h=HP)
        p_hot = flat(p_qT, "h t").rearrange("p (h k) -> p h k", h=NT * PH)
        p_top = take(NT, HP, TOPK)
        p_idx = take(NT, HP, TOPK, dt=U32)
        p_idxf = take(NT, HP, TOPK)
        p_best = take(NT * PH, TOPK)
        p_pos = take(NT * PH, TOPK, dt=U32)
        p_ab = take(2, NT * PH, TOPK, dt=U32)
        p_abf = take(2, NT * PH, TOPK)
        p_key = take(2, NT * PH, TOPK)
        p_gate = take(NT * PH, TOPK)
        p_sum, p_rsum = take(NT * PH), take(NT * PH)
        p_map = arena[:, :].rearrange("p (i t) -> p i t", i=P)
        take = cutter(work, 1792)
        p_T = take(3, T)
        p_A = take(4, P)
        p_B = take(4, P)
        p_act = work[:, 0:2 * T].rearrange("p (s t) -> p s t", s=2)

        x_loaded, small_loaded, gain_loaded = sem("x_loaded"), sem("small_loaded"), sem("gain_loaded")
        last_gain_loaded = sem("last_gain_loaded")
        landed = [sem(f"unit_landed{i}") for i in range(RING)]
        hi_ready, lo_ready = sem("hi_ready"), sem("lo_ready")
        half_used = sem("half_used")
        dve_chain = sem("dve_chain")
        n_sq, n_mean, n_rooted, n_h, n_hTps, n_hT = (sem("n_" + s) for s in (
            "squares", "mean", "root", "h", "hT_psum", "hT"))
        n_hTlo, oT_lo, keys_loaded, s_wg_loaded = sem("n_hT_lo"), sem("oT_lo"), sem("keys_loaded"), sem("s_wg_loaded")
        x_added = sem("x_added")
        oT_psum, oT_ready, o_ready = sem("oT_psum"), sem("oT_ready"), sem("o_ready")
        SEM = {s: sem(s) for s in (
            "g_gate_ps g_zs g_pads g_padded g_conved g_silued g_gateb g_gact g_gexp g_gg g_betas g_cum g_cumsb g_exps g_rows "
            "g_tokps g_toksb g_sqsum g_junk g_mean g_root g_qk g_backps g_backsb g_bc g_dexp g_logE g_E g_kq g_KE g_A g_P g_mask g_Yps g_Y "
            "g_Zps g_T g_kS g_U0 g_vn0 g_S1ps g_S1 g_RQ g_v1 g_int g_U1 g_vn1 g_Ops g_O g_osum g_omean g_oroot g_gz "
            "s_gate_ps s_gateb s_gexp s_pads s_mv s_yg s_zs s_padded s_conved s_silued s_gact s_sp s_da s_cum s_nac s_rowsps s_rows s_tokps s_toksb s_skip "
            "s_cbps s_cb s_cbl s_bc s_d s_e s_m s_yps s_y s_ss s_mean s_root "
            "p_qps p_q p_sps p_s p_top p_ex p_exd p_key p_Tps p_T p_hot p_mapps p_map p_mul p_gelu p_gated p_ag_hi p_ag "
            "finished stored").split()}
        N_SMALL = 13

        block = ctx.enter_context(nc.Block())

        @block.sync
        def _(sp):
            sp.dma_start(x_sb[:, :, :], a["x"]).then_inc(x_loaded, 16)

            def load_unit(n):
                if n >= RING:
                    sp.wait_ge(lo_ready, 2 * (n - RING + 1))
                sp.dma_start(ring[:, n % RING, :], order[n][1]).then_inc(landed[n % RING], 16)

            def load_tables(lyr):
                n0 = tables[lyr]
                U, V = a["peer_u"][lyr], a["peer_v"][lyr]

                def one(k, table, i, it=0, tiles=0):
                    sp.wait_ge(lo_ready, it * 8 + 2 * (n0 + k - RING + 1))
                    src = table[bass.ds(it * tiles + i, 1)].rearrange("a p c -> p (a c)") if tiles else table[i]
                    sp.dma_start(ring[:, (n0 + k) % RING, :], src).then_inc(landed[(n0 + k) % RING], 16)

                for base, table in ((0, U), (EARLY, V)):
                    with sp.Fori(0, EARLY // 4) as it:
                        for q in range(4):
                            one(base + q, table, q, it, 4)
                base, i = 2 * EARLY, EARLY
                one(base, U, i)
                one(base + 1, U, i + 1)
                one(base + 2, V, i)
                with sp.Fori(0, (P - EARLY) // 2 - 1) as it:
                    one(base + 3, U, i + 2, it, 2)
                    one(base + 4, V, i + 1, it, 2)
                    one(base + 5, U, i + 3, it, 2)
                    one(base + 6, V, i + 2, it, 2)
                one(2 * P - 1, V, P - 1)

            n = 0
            while n < len(order):
                if order[n] is None:
                    load_tables(0 if n == tables[0] else 1)
                    n += 2 * P
                else:
                    load_unit(n)
                    n += 1
            sp.wait_ge(half_used, 2 * len(order))
            sp.dma_start(last_gain, a["norm_final"].partition_broadcast(P)).then_inc(last_gain_loaded, 16)
            sp.wait_ge(SEM["finished"], 1)
            sp.dma_start(out, x_sb[:, :, :]).then_inc(SEM["stored"], 16)
            sp.wait_ge(SEM["stored"], 16)

        @block.tensor
        def _(pe):
            def mm(o, w, r, first=True, last=True):
                return pe.matmul(o, w, r, start=first, stop=last)

            def part_mm(o, w, r, first, last):
                mm(o, w(0), r(0), first, False)
                mm(o, w(0), r(1), False, False)
                return mm(o, w(1), r(0), False, last)

            def half(n, hf, it=0, step=0):
                pe.wait_ge(lo_ready, it * step + (2 * n + hf + 1))
                return (2 * n + hf) % SPLIT

            def turn_h(i):
                pe.wait_ge(n_h, 2 * (i + 1))
                for b in range(4):
                    for kk in range(2):
                        for t in range(NT):
                            k = 2 * b + kk
                            last = pe.transpose(PS[b][:, (2 * kk + t) * P:(2 * kk + t + 1) * P],
                                                h_tok[:, t, k * P:(k + 1) * P], ident)
                    last.then_inc(n_hTps, 1)
                pe.wait_ge(n_hTlo, KD * (i + 1))

            def by_token(name, bank):
                for q in range(KD // 2):
                    for kk in range(2):
                        k = 2 * q + kk
                        s = half(at[(*name, q)], kk)
                        for t in range(NT):
                            last = part_mm(PS[bank + t][:, :], lambda p: hT[p][:, k, t * P:(t + 1) * P],
                                           lambda p: w_part[p][:, s, :], k == 0, k == KD - 1)
                        last.then_inc(half_used, 1)

            def columns(o, n, it=0, step=0):
                for hf in range(2):
                    s = half(n, hf, it, step)
                    for kk in range(KD // 2):
                        k = KD // 2 * hf + kk
                        last = part_mm(o, lambda p: w_part[p][:, s, kk * P:(kk + 1) * P],
                                       lambda p: hT[p][:, k, :], k == 0, k == KD - 1)
                    last.then_inc(half_used, 1)

            def rows_of(n, src, first, last_one, it=0, step=0):
                for hf in range(2):
                    s = half(n, hf, it, step)
                    for t in range(NT):
                        last = part_mm(PS[4 + 2 * t + hf][:, :], lambda p: src(p, t),
                                       lambda p: w_part[p][:, s, :], first, last_one)
                    last.then_inc(half_used, 1)

            def by_channel(name, bank):
                columns(PS[bank][:, 0:T], at[name])

            def out_row(name, k, tiles):
                rows_of(at[(name, k)], lambda p, t: hT[p][:, k % KD, t * P:(t + 1) * P], k == 0, k == tiles - 1)

            def gate_logits(o, wg, k, t):
                mm(o, hT[0][:, k, t * P:(t + 1) * P].bitcast(F32), wg[:, k, :], k == 0, False)
                return mm(o, hT[1][:, k, t * P:(t + 1) * P].bitcast(F32), wg[:, k, :], False, k == KD - 1)

            def gdn():
                for hf in range(2):
                    by_token(("gz", hf), 4 + 2 * hf)
                for t in range(NT):
                    for k in range(KD):
                        last = gate_logits(PS[2][:, t * 32:(t + 1) * 32], g_wg, k, t)
                last.then_inc(SEM["g_gate_ps"], 1)

                def turn_tok(gi):
                    pe.wait_ge(SEM["g_silued"], 2 * gi + 2)
                    if gi == 0:
                        pe.wait_ge(SEM["g_zs"], 4)
                    if gi >= 4:
                        pe.wait_ge(SEM["g_toksb"], gi - 3)
                    for t in range(NT):
                        for e in range(2):
                            last = pe.transpose(PS[4 + gi % 4][:, (2 * t + e) * P:(2 * t + e + 1) * P],
                                                g_feat[:, 2 * gi + e, t * P:(t + 1) * P], ident)
                    last.then_inc(SEM["g_tokps"], 1)

                for m in range(GC):
                    if m >= 2:
                        pe.wait_ge(SEM["g_padded"], m - 1)
                    by_channel(("gq", m), m % 2)
                    if m >= 3 and m % 2:
                        turn_tok((m - 3) // 2)
                pe.wait_ge(SEM["g_gg"], 1)
                for c in range(NT):
                    mm(PS[3][:, c * 16:c * 16 + 8], upper, g_g[:, c, 0:8])
                    mm(PS[3][:, c * 16 + 8:c * 16 + 16], lower, g_g[:, c, 8:16])
                    mm(PS[3][:, 32 + c * 16:48 + c * 16], ones, g_g[:, c, :])
                    mm(PS[2][0:GH, c * P:(c + 1) * P], g_g[:, c, 0:8], upper)
                    last = mm(PS[2][0:GH, T + c * P:T + (c + 1) * P], g_g[:, c, 8:16], lower)
                last.then_inc(SEM["g_cum"], 1)
                turn_tok(11)
                pe.wait_ge(SEM["g_qk"], 2)
                for gi in range(GH):
                    if gi >= 4:
                        pe.wait_ge(SEM["g_backsb"], gi - 3)
                    for e in range(2):
                        for t in range(NT):
                            last = pe.transpose(PS[4 + gi % 4][:, (2 * e + t) * P:(2 * e + t + 1) * P],
                                                g_tok[:, t, 2 * gi + e, :], ident)
                    last.then_inc(SEM["g_backps"], 1)
                pe.wait_ge(SEM["g_rows"], 1)
                pe.wait_ge(SEM["g_padded"], GC)
                for h in range(GH):
                    if h >= 2:
                        pe.wait_ge(SEM["g_dexp"], h - 1)
                    pick = const[0:GH, C_EYE, h:h + 1].to_broadcast([GH, P])
                    mm(PS[h % 2][:, 0:T], pick, g_row[:, 0:T])
                    mm(PS[h % 2][:, T:2 * T], pick, g_row[:, T:2 * T]).then_inc(SEM["g_bc"], 1)
                    if h == 0:
                        pe.wait_ge(SEM["g_cumsb"], 1)
                        pe.wait_ge(SEM["g_backsb"], GH)
                    if h >= 2:
                        pe.wait_ge(SEM["g_KE"], h - 1)
                    for c in range(NT):
                        kT = g_feat[:, GH + h, c * P:(c + 1) * P]
                        mm(PS[2 + h % 2][:, c * P:(c + 1) * P], kT, kT)
                        last = mm(PS[2 + h % 2][:, T + c * P:T + (c + 1) * P], kT, g_feat[:, h, c * P:(c + 1) * P])
                    last.then_inc(SEM["g_kq"], 1)

                def y_step(n):
                    level, b = divmod(n, GB)
                    pe.wait_ge(SEM["g_mask"], n + 1)
                    if n >= 2:
                        if n - 2 < GB:
                            pe.wait_ge(SEM["g_T"], t_count(n - 2))
                        else:
                            pe.wait_ge(SEM["g_Y"], n - 2 - GB + 1)
                    if n == 0:
                        pe.wait_ge(SEM["g_dexp"], GH)
                    if level:
                        pe.wait_ge(SEM["g_T"], t_count(n - GB))
                    for e in range(4):
                        last = mm(PS[n % 2][:, e * P:(e + 1) * P], g_mask[:, 4 * (n % 2) + e, :],
                                  g_T[:, 4 * b + e, :] if level else ident)
                    last.then_inc(SEM["g_Yps"], 1)

                def z_step(n):
                    level, b = divmod(n, GB)
                    pe.wait_ge(SEM["g_Y"], n - GB + 1)
                    if n - 2 >= GB:
                        pe.wait_ge(SEM["g_T"], t_count(n - 2))
                    for e in range(4):
                        s = 4 * b + e
                        if level < LEVELS - 1:
                            mm(PS[4 + n % 2][:, e * P:(e + 1) * P], g_TT[:, s, :], g_Y[:, s, :])
                        last = mm(PS[6 + n % 2][:, e * P:(e + 1) * P], g_Y[:, s, :], g_TT[:, s, :])
                    last.then_inc(SEM["g_Zps"], 1)

                for n in range(LEVELS * GB):
                    y_step(n)
                    if n - 1 >= GB:
                        z_step(n - 1)
                z_step(LEVELS * GB - 1)

                pe.wait_ge(SEM["g_T"], t_count(LEVELS * GB - 1))
                for q4 in range(4):
                    d, h0 = q4 // 2, 4 * (q4 % 2)
                    for e in range(4):
                        last = mm(PS[q4][:, e * P:(e + 1) * P], g_TT[:, system(d, h0 + e, d), :],
                                  g_tok[:, d, 2 * GH + h0 + e, :])
                    last.then_inc(SEM["g_U0"], 1)
                for q4 in range(4):
                    d, h0 = q4 // 2, 4 * (q4 % 2)
                    pe.wait_ge(SEM["g_vn0"], q4 + 1)
                    pe.wait_ge(SEM["g_kS"], q4 + 1)
                    for e in range(4):
                        last = mm(PS[4 + q4][:, e * P:(e + 1) * P], g_kS[:, d * GH + h0 + e, :],
                                  g_vn[:, system(d, h0 + e, d), :])
                    last.then_inc(SEM["g_S1ps"], 1)
                for q4 in range(4):
                    d, h0 = q4 // 2, 4 * (q4 % 2)
                    pe.wait_ge(SEM["g_S1"], q4 + 1)
                    c = 1 - d
                    for e in range(4):
                        S = g_S[:, d * GH + h0 + e, :]
                        mm(PS[q4][:, e * P:(e + 1) * P], g_feat[:, GH + h0 + e, c * P:(c + 1) * P], S)
                        last = mm(PS[4 + q4][:, e * P:(e + 1) * P], g_feat[:, h0 + e, c * P:(c + 1) * P], S)
                    last.then_inc(SEM["g_RQ"], 1)
                for q4 in range(4):
                    d, h0 = q4 // 2, 4 * (q4 % 2)
                    pe.wait_ge(SEM["g_v1"], q4 + 1)
                    for e in range(4):
                        last = mm(PS[q4][:, e * P:(e + 1) * P], g_TT[:, system(d, h0 + e, 1 - d), :],
                                  g_vp[:, d * GH + h0 + e, :])
                    last.then_inc(SEM["g_U1"], 1)
                pe.wait_ge(SEM["g_int"], 4)
                pe.wait_ge(SEM["g_vn1"], 4)
                pe.wait_ge(SEM["g_P"], 2 * NT)
                for c in range(NT):
                    for hg in range(2):
                        for e in range(4):
                            o = PS[4 + 2 * c + hg][:, e * P:(e + 1) * P]
                            f, r = system(0, 4 * hg + e, c), system(1, 4 * hg + e, c)
                            mm(o, g_tok[:, c, 4 * hg + e, :], g_vn[:, f, :], True, False)
                            last = mm(o, g_PTb[:, 4 * hg + e, c, :], g_vn[:, r, :], False, True)
                        last.then_inc(SEM["g_Ops"], 1)
                pe.wait_ge(o_ready, 2)
                for b in range(4):
                    for kk in range(2):
                        for t in range(NT):
                            last = pe.transpose(PS[b][:, (2 * kk + t) * P:(2 * kk + t + 1) * P],
                                                g_o[:, t * GH + 2 * b + kk, :], ident)
                    last.then_inc(oT_psum, 1)
                pe.wait_ge(oT_lo, 4)
                for k in range(GH):
                    out_row("go", k, GH)

            def ssd():
                for nb in range(SI // 512):
                    if nb >= 2:
                        pe.wait_ge(SEM["s_zs"], 2 * (nb - 1))
                    by_token(("sz", nb), 4 + 2 * (nb % 2))
                pe.wait_ge(s_wg_loaded, 16)
                for t in range(NT):
                    for k in range(KD):
                        last = gate_logits(PS[2][:, t * 64:(t + 1) * 64], s_wg, k, t)
                last.then_inc(SEM["s_gate_ps"], 1)

                def turn_tok(gi):
                    pe.wait_ge(SEM["s_silued"], 2 * gi + 2)
                    if gi == 0:
                        pe.wait_ge(SEM["s_zs"], 8)
                    if gi >= 4:
                        pe.wait_ge(SEM["s_toksb"], gi - 3)
                    for t in range(NT):
                        for e in range(2):
                            last = pe.transpose(PS[4 + gi % 4][:, (2 * t + e) * P:(2 * t + e + 1) * P],
                                                s_feat[:, 2 * gi + e, t * P:(t + 1) * P], ident)
                    last.then_inc(SEM["s_tokps"], 1)

                for m in range(SC):
                    if m >= 2:
                        pe.wait_ge(SEM["s_padded"], m - 1)
                    by_channel(("sx", m), m % 2)
                    if m >= 3 and m % 2 and (m - 3) // 2 < SX // 2:
                        turn_tok((m - 3) // 2)
                pe.wait_ge(SEM["s_da"], 1)
                f, r = slice(0, SH), slice(SH, 2 * SH)
                mm(PS[3][:, 0:32], upper, s_da[:, 0, f])
                mm(PS[3][:, 64:96], ones, s_da[:, 0, f], True, False)
                mm(PS[3][:, 64:96], upper, s_da[:, 1, f], False, True)
                mm(PS[3][:, 96:128], lower, s_da[:, 1, r])
                mm(PS[3][:, 32:64], ones, s_da[:, 1, r], True, False)
                mm(PS[3][:, 32:64], lower, s_da[:, 0, r], False, True)
                mm(PS[2][0:SH, 0:P], s_da[:, 0, f], upper)
                mm(PS[2][0:SH, P:2 * P], s_da[:, 0, f], ones, True, False)
                mm(PS[2][0:SH, P:2 * P], s_da[:, 1, f], upper, False, True)
                mm(PS[2][0:SH, 2 * P:3 * P], s_da[:, 1, r], ones, True, False)
                mm(PS[2][0:SH, 2 * P:3 * P], s_da[:, 0, r], lower, False, True)
                mm(PS[2][0:SH, 3 * P:4 * P], s_da[:, 1, r], lower).then_inc(SEM["s_cum"], 1)
                pe.wait_ge(SEM["s_silued"], SC)
                pe.wait_ge(SEM["s_toksb"], SX // 2)
                for g in range(SG):
                    if g >= 2:
                        pe.wait_ge(SEM["s_cb"], g - 1)
                    for st in range(NT):
                        last = mm(PS[6 + g % 2][:, st * T:(st + 1) * T], s_feat[:, SX + g, st * P:(st + 1) * P],
                                  s_feat[:, SX + SG + g, :])
                    last.then_inc(SEM["s_cbps"], 1)
                pe.wait_ge(SEM["s_rows"], 1)
                pe.wait_ge(SEM["s_nac"], 1)
                pe.wait_ge(SEM["s_padded"], SC)

                def spread(h):
                    if h >= 2:
                        pe.wait_ge(SEM["s_e"], h - 1)
                    pick = const[0:SH, C_EYE, h:h + 1].to_broadcast([SH, P])
                    mm(PS[h % 2][:, 0:T], pick, s_row[:, 0:T])
                    mm(PS[h % 2][:, T:2 * T], pick, s_row[:, T:2 * T]).then_inc(SEM["s_bc"], 1)

                def y_head(h):
                    g, b = h // SR, 2 + 2 * (h // SR % 2)
                    if h % SR == 0 and g >= 2:
                        pe.wait_ge(SEM["s_y"], 2 * (g - 1))
                    pe.wait_ge(SEM["s_m"], h + 1)
                    o = slice(h % SR * SP_, (h % SR + 1) * SP_)
                    x0, x1 = (s_tok[:, t, h * SP_:(h + 1) * SP_] for t in range(NT))
                    mm(PS[b][:, o], s_M[:, h % 2, 0, 0, :], x0, True, False)
                    mm(PS[b][:, o], s_M[:, h % 2, 1, 2, :], x1, False, True)
                    mm(PS[b + 1][:, o], s_M[:, h % 2, 0, 2, :], x0, True, False)
                    mm(PS[b + 1][:, o], s_M[:, h % 2, 1, 0, :], x1, False, True).then_inc(SEM["s_yps"], 1)

                for h in range(SH):
                    spread(h)
                    if h >= 2:
                        y_head(h - 2)
                y_head(SH - 2)
                y_head(SH - 1)
                pe.wait_ge(o_ready, 2 + 8)

                def turn_y(gi):
                    if gi >= 4:
                        pe.wait_ge(oT_lo, 4 + gi - 3)
                    for kk in range(2):
                        for t in range(NT):
                            k = 2 * gi + kk
                            last = pe.transpose(PS[gi % 4][:, (2 * kk + t) * P:(2 * kk + t + 1) * P],
                                                s_y[:, t, k * P:(k + 1) * P], ident)
                    last.then_inc(oT_psum, 1)

                for gi in range(4):
                    turn_y(gi)
                for k in range(SX):
                    if k % 2 == 0:
                        pe.wait_ge(oT_lo, 4 + k // 2 + 1)
                    out_row("so", k, SX)
                    if k % 2 and k // 2 + 4 < SX // 2:
                        turn_y(k // 2 + 4)

            def route(lyr):
                for m in range(HP):
                    if m >= 2:
                        pe.wait_ge(SEM["p_q"], HP * lyr + m - 1)
                    by_channel(("pq", lyr, m), m % 2)
                pe.wait_ge(SEM["p_q"], HP * (lyr + 1))
                pe.wait_ge(keys_loaded, 16 * (lyr + 1))
                for g in range(8):
                    t, first_head = g // 2 % 2, 8 * (g // 4) + 4 * (g % 2)
                    if g >= 4:
                        pe.wait_ge(SEM["p_s"], 8 * lyr + g - 3)
                    for e in range(4):
                        hp = first_head + e
                        last = mm(PS[2 + g % 4][:, e * P:(e + 1) * P], p_qT[:, hp, t * P:(t + 1) * P], p_kT[:, hp, :])
                    last.then_inc(SEM["p_sps"], 1)

            def hidden(lyr, i, n, it=0, tiles=0):
                if tiles or i >= 2:
                    pe.wait_ge(SEM["p_gelu"], it * tiles + (P * lyr + i - 1))
                columns(PS[i % 2][:, 0:T], n, it, 8)

            def values(lyr, i, n, it=0, tiles=0, first=False, last_one=False):
                pe.wait_ge(SEM["p_ag"], it * tiles + (P * lyr + i + 1))
                rows_of(n, lambda p, t: p_ag[p][:, i % 2, t * P:(t + 1) * P], first, last_one, it, 8)

            def experts(lyr):
                n0 = tables[lyr]
                for i in range(4):
                    hidden(lyr, i, n0 + i)
                with pe.Fori(0, EARLY // 4 - 1) as it:
                    for i in range(4, 8):
                        hidden(lyr, i, n0 + i, it, 4)
                pe.wait_ge(SEM["p_key"], lyr + 1)
                for e in range(2):
                    for t in range(NT):
                        v = flat(p_key[:, e, t * PH:(t + 1) * PH, :], "h k")
                        pe.transpose(PS[6][:, e * T + t * P:e * T + (t + 1) * P], v, ident)
                for t in range(NT):
                    last = pe.transpose(PS[7][:, t * P:(t + 1) * P], flat(p_gate[:, t * PH:(t + 1) * PH, :], "h k"), ident)
                last.then_inc(SEM["p_Tps"], 1)
                pe.wait_ge(SEM["p_gelu"], P * lyr + EARLY)

                def tokens16(it, first=False):
                    for u in range(16):
                        if not first and u % 4 == 0:
                            pe.wait_ge(SEM["p_mul"], it * 4 + (64 * lyr + u // 4 - 3))
                        pe.wait_ge(SEM["p_hot"], it * 16 + (T * lyr + u + 1))
                        mm(PS[u // 4][:, u % 4 * P:(u % 4 + 1) * P], p_B[:, u % 4, :], p_A[:, u % 4, :]
                           ).then_inc(SEM["p_mapps"], 1)

                tokens16(0, True)
                with pe.Fori(1, T // 16) as it:
                    tokens16(it)
                n1, n2 = n0 + EARLY, n0 + 2 * EARLY
                for i in range(4):
                    values(lyr, i, n1 + i, first=i == 0)
                with pe.Fori(0, EARLY // 4 - 1) as it:
                    for i in range(4, 8):
                        values(lyr, i, n1 + i, it, 4)
                i = EARLY
                pe.wait_ge(SEM["p_mul"], 64 * (lyr + 1))
                hidden(lyr, i, n2)
                hidden(lyr, i + 1, n2 + 1)
                values(lyr, i, n2 + 2)
                with pe.Fori(0, (P - EARLY) // 2 - 1) as it:
                    hidden(lyr, i + 2, n2 + 3, it, 2)
                    values(lyr, i + 1, n2 + 4, it, 2)
                    hidden(lyr, i + 3, n2 + 5, it, 2)
                    values(lyr, i + 2, n2 + 6, it, 2)
                values(lyr, P - 1, n0 + 2 * P - 1, last_one=True)

            pe.wait_ge(small_loaded, 16 * N_SMALL)
            turn_h(0)
            gdn()
            turn_h(1)
            route(0)
            experts(0)
            turn_h(2)
            ssd()
            turn_h(3)
            route(1)
            experts(1)

        @block.vector
        def _(dve):
            chain = [0]

            def link(ins):
                chain[0] += 1
                ins.then_inc(dve_chain, 1)
                dve.wait_ge(dve_chain, chain[0])

            def wide(v, n):
                return v.rearrange("p (a o) -> p a o", o=1).to_broadcast([v.shape[0], v.shape[1], n])

            def rows(v, n):
                return v.rearrange("p (o c) -> p o c", o=1).to_broadcast([v.shape[0], n, v.shape[1]])

            def polish(ms, root, inv, new, rstd, signal=None):
                link(dve.reciprocal(inv, root))
                link(dve.tensor_tensor(new, inv, inv, ALU.mult))
                link(dve.tensor_tensor(new, new, ms, ALU.mult))
                link(dve.tensor_scalar(new, new, -0.5, 1.5, ALU.mult, ALU.add))
                link(dve.tensor_tensor(rstd, inv, new, ALU.mult))

            def norm_stats(i):
                dve.wait_ge(n_sq, 2 * (i + 1))
                dve.tensor_scalar(n_ms, n_ss, 1.0 / D, EPS, ALU.mult, ALU.add).then_inc(n_mean, 1)
                dve.wait_ge(n_rooted, i + 1)
                polish(n_ms, n_root, n_inv, n_new, n_rstd)

            def norm(i):
                norm_stats(i)
                for t in range(NT):
                    dve.tensor_scalar(h_tok[:, t, :], x_sb[:, t, :], n_rstd[:, t:t + 1], None, ALU.mult).then_inc(n_h, 1)
                for k in range(KD):
                    if k % 2 == 0:
                        dve.wait_ge(n_hT, KD * i + k + 2)
                    dve.scalar_tensor_tensor(hT[1][:, k, :], PS[k // 2][:, (k % 2) * T:(k % 2 + 1) * T], norm_w[:, i, k:k + 1],
                                             hT[0][:, k, :].bitcast(F32), ALU.mult, ALU.subtract).then_inc(n_hTlo, 1)

            def rest_of_oT(base, gi):
                dve.wait_ge(oT_ready, base + gi + 1)
                b = gi % 4
                dve.tensor_tensor(hT[1][:, 2 * b:2 * b + 2, :], PS[b][:, :].rearrange("p (e t) -> p e t", e=2),
                                  hT[0][:, 2 * b:2 * b + 2, :].bitcast(F32), ALU.subtract).then_inc(oT_lo, 1)

            def rest_of_unit(n, it=0, step=0):
                for hf in range(2):
                    dve.wait_ge(hi_ready, it * step + (2 * n + hf + 1))
                    s = (2 * n + hf) % SPLIT
                    dve.tensor_tensor(w_part[1][:, s, :], ring[:, n % RING, hf * 512:(hf + 1) * 512],
                                      w_part[0][:, s, :].bitcast(F32), ALU.subtract).then_inc(lo_ready, 1)

            def residual(last_unit):
                dve.wait_ge(half_used, 2 * (last_unit + 1))
                for t in range(NT):
                    for hf in range(2):
                        v = x_sb[:, t, hf * 512:(hf + 1) * 512]
                        dve.tensor_tensor(v, PS[4 + 2 * t + hf][:, :], v, ALU.add).then_inc(x_added, 1)

            def conv(m, pad, acc, taps, padded, conved, silued):
                dve.wait_ge(padded, m + 1)
                if m >= 4:
                    dve.wait_ge(silued, m - 3)
                o = acc[:, m % 4, :]
                link(dve.tensor_scalar(o, pad[:, m % 4, 0:T], taps[:, m, 0:1], None, ALU.mult))
                for j in range(1, TAPS):
                    ins = dve.scalar_tensor_tensor(o, pad[:, m % 4, j:j + T], taps[:, m, j:j + 1], o, ALU.mult, ALU.add)
                    if j < TAPS - 1:
                        link(ins)
                    else:
                        ins.then_inc(conved, 1)

            def gdn():
                link(dve.memset(flat(g_pad, "s w"), 0.0))
                dve.memset(g_E[:, 0, 0:1], 0.0).then_inc(SEM["g_pads"], 1)
                dve.wait_ge(SEM["g_gate_ps"], 1)
                dve.wait_ge(small_loaded, 16 * N_SMALL)
                logits = PS[2][:, 0:64].rearrange("p (t c) -> p t c", t=NT)
                link(dve.tensor_tensor(g_z, logits[:, :, 0:16], rows(g_bias, NT), ALU.add))
                link(dve.tensor_scalar(g_mx, g_z, 0.0, None, ALU.max))
                dve.scalar_tensor_tensor(g_ab, g_mx, -2.0, g_z, ALU.mult, ALU.add).then_inc(SEM["g_gateb"], 1)
                dve.wait_ge(SEM["g_gact"], 1)
                link(dve.tensor_tensor(g_z, g_mx, g_ab, ALU.add))
                dve.scalar_tensor_tensor(g_g, g_z, -1.0, rows(g_nega, NT), ALU.mult, ALU.mult).then_inc(SEM["g_gg"], 1)

                def tok_copy(gi):
                    dve.wait_ge(SEM["g_tokps"], gi + 1)
                    dve.tensor_copy(g_tok[:, :, 2 * gi:2 * gi + 2, :],
                                    PS[4 + gi % 4][:, :].rearrange("p (t e d) -> p t e d", t=NT, e=2)
                                    ).then_inc(SEM["g_toksb"], 1)

                for m in range(GC):
                    conv(m, g_pad, g_acc, g_conv, SEM["g_padded"], SEM["g_conved"], SEM["g_silued"])
                    if m >= 5 and m % 2:
                        tok_copy((m - 5) // 2)
                dve.wait_ge(SEM["g_cum"], 1)
                link(dve.tensor_copy(flat(g_gc, "t c"), PS[3][:, 0:32]))
                dve.tensor_tensor(flat(g_gt, "t c"), PS[3][:, 32:64], flat(g_gc, "t c"), ALU.subtract).then_inc(SEM["g_cumsb"], 1)
                tok_copy(10)
                tok_copy(11)
                dve.wait_ge(SEM["g_sqsum"], GH)
                dve.tensor_scalar(g_ms, g_ss, 1.0, EPS, ALU.mult, ALU.add).then_inc(SEM["g_mean"], 1)
                dve.wait_ge(SEM["g_root"], 1)
                polish(g_ms, g_root, g_inv, g_new, g_rstd)
                dve.wait_ge(SEM["g_toksb"], 12)
                for t in range(NT):
                    v = g_tok[:, t, 0:2 * GH, :]
                    dve.tensor_tensor(v, v, wide(g_rstd[:, t, :], P), ALU.mult).then_inc(SEM["g_qk"], 1)
                dve.wait_ge(SEM["g_exps"], 2)
                link(dve.tensor_scalar(g_egq, g_eg, P ** -0.5, None, ALU.mult))

                def decay(h):
                    dve.wait_ge(SEM["g_bc"], h + 1)
                    tmp = g_tmp[:, 2 * (h % 2):2 * (h % 2) + 2, :]
                    for c in range(NT):
                        lo = slice(c * P, (c + 1) * P)
                        dve.tensor_scalar(g_E[:, h, lo], PS[h % 2][:, lo], g_gc[:, c, h:h + 1], 0.0, ALU.subtract, ALU.min)
                        last = dve.tensor_scalar(tmp[:, c, :], PS[h % 2][:, T + c * P:T + (c + 1) * P],
                                                 g_gc[:, c, GH + h:GH + h + 1], 0.0, ALU.subtract, ALU.min)
                    last.then_inc(SEM["g_dexp"], 1)
                    dve.wait_ge(SEM["g_dexp"], h + 1)
                    dve.tensor_tensor(g_E[:, h, :], g_E[:, h, :], flat(tmp, "c d"), ALU.add).then_inc(SEM["g_logE"], 1)

                def system_rows(h):
                    dve.wait_ge(SEM["g_kq"], h + 1)
                    dve.wait_ge(SEM["g_E"], h + 1)
                    KE, QE, b = g_KE[:, h % 2, :], g_E[:, h, :], PS[2 + h % 2]
                    dve.tensor_tensor(KE, b[:, 0:T], g_E[:, h, :], ALU.mult)
                    dve.scalar_tensor_tensor(QE, b[:, T:2 * T], P ** -0.5, g_E[:, h, :], ALU.mult, ALU.mult).then_inc(SEM["g_KE"], 1)
                    dve.wait_ge(SEM["g_KE"], h + 1)
                    for d in range(2):
                        for c in range(NT):
                            last = dve.scalar_tensor_tensor(
                                g_AT[:, system(d, h, c), :], KE[:, c * P:(c + 1) * P],
                                g_beta[:, c, d * GH + h:d * GH + h + 1],
                                const[:, C_LOS if d else C_UPS, :], ALU.mult, ALU.mult)
                    last.then_inc(SEM["g_A"], 1)

                dve.wait_ge(SEM["g_betas"], 1)
                for h in range(GH):
                    decay(h)
                    if h:
                        system_rows(h - 1)
                system_rows(GH - 1)

                for n in range(LEVELS * GB):
                    level, b = divmod(n, GB)
                    Tb, TTb = g_T[:, 4 * b:4 * b + 4, :], g_TT[:, 4 * b:4 * b + 4, :]

                    def bank(i):
                        return PS[i][:, :].rearrange("p (s d) -> p s d", s=4)

                    if level == 0:
                        dve.wait_ge(SEM["g_Yps"], n + 1)
                        dve.tensor_tensor(Tb, rows(ident, 4), bank(n % 2), ALU.subtract).then_inc(SEM["g_T"], 1)
                        dve.tensor_tensor(TTb, rows(ident, 4), g_mask[:, 4 * (n % 2):4 * (n % 2) + 4, :],
                                          ALU.subtract).then_inc(SEM["g_T"], 1)
                        continue
                    dve.wait_ge(SEM["g_Zps"], n - GB + 1)
                    if level < LEVELS - 1:
                        dve.tensor_tensor(Tb, Tb, bank(4 + n % 2), ALU.subtract).then_inc(SEM["g_T"], 1)
                    dve.tensor_tensor(TTb, TTb, bank(6 + n % 2), ALU.subtract).then_inc(SEM["g_T"], 1)

                def quad(v, q4, c):
                    d, h0 = q4 // 2, 4 * (q4 % 2)
                    return wide(v[:, c, d * GH + h0:d * GH + h0 + 4], P)

                def bank(i):
                    return PS[i][:, :].rearrange("p (s d) -> p s d", s=4)

                def vn(q4, c):
                    s = system(q4 // 2, 4 * (q4 % 2), c)
                    return g_vn[:, s:s + 7:2, :]

                for q4 in range(4):
                    dve.wait_ge(SEM["g_U0"], q4 + 1)
                    dve.tensor_tensor(vn(q4, q4 // 2), bank(q4), quad(g_beta, q4, q4 // 2), ALU.mult).then_inc(SEM["g_vn0"], 1)
                for q4 in range(4):
                    d, h0 = q4 // 2, 4 * (q4 % 2)
                    c = 1 - d
                    vp = g_vp[:, 4 * q4:4 * q4 + 4, :]
                    dve.wait_ge(SEM["g_RQ"], q4 + 1)
                    link(dve.tensor_tensor(vp, bank(q4), quad(g_eg, q4, c), ALU.mult))
                    dve.tensor_tensor(vp, g_tok[:, c, 2 * GH + h0:2 * GH + h0 + 4, :], vp, ALU.subtract).then_inc(SEM["g_v1"], 1)
                for q4 in range(4):
                    dve.tensor_tensor(g_inter[:, 4 * q4:4 * q4 + 4, :], bank(4 + q4), quad(g_egq, q4, 1 - q4 // 2),
                                      ALU.mult).then_inc(SEM["g_int"], 1)
                for q4 in range(4):
                    dve.wait_ge(SEM["g_U1"], q4 + 1)
                    dve.tensor_tensor(vn(q4, 1 - q4 // 2), bank(q4), quad(g_beta, q4, 1 - q4 // 2), ALU.mult).then_inc(SEM["g_vn1"], 1)
                dve.wait_ge(SEM["g_int"], 4)
                for c in range(NT):
                    for hg in range(2):
                        b = 2 * c + hg
                        dve.wait_ge(SEM["g_Ops"], b + 1)
                        q = (1 - c) * GH + 4 * hg
                        dve.tensor_tensor(g_o[:, 4 * b:4 * b + 4, :], bank(4 + b), g_inter[:, q:q + 4, :], ALU.add).then_inc(SEM["g_O"], 1)
                dve.wait_ge(SEM["g_O"], 4)
                link(dve.tensor_tensor(flat(g_sq, "s d"), flat(g_o, "s d"), flat(g_o, "s d"), ALU.mult))
                ss, ms, root, inv, new, rstd = (v[:, 0, :] for v in (g_ss, g_ms, g_root, g_inv, g_new, g_rstd))
                link(dve.tensor_reduce(ss, g_sq, AX.X, ALU.add))
                dve.tensor_scalar(ms, ss, 1.0 / P, EPS, ALU.mult, ALU.add).then_inc(SEM["g_omean"], 1)
                dve.wait_ge(SEM["g_oroot"], 1)
                polish(ms, root, inv, new, rstd)
                link(dve.tensor_tensor(g_o, g_o, wide(rstd, P), ALU.mult))
                dve.wait_ge(SEM["g_gz"], 2)
                for t in range(NT):
                    v = flat(g_o[:, t * GH:(t + 1) * GH, :], "s d")
                    dve.tensor_tensor(v, v, g_siluz[:, t, :], ALU.mult).then_inc(o_ready, 1)
                for gi in range(4):
                    rest_of_oT(0, gi)
                residual(at[("go", GH - 1)])

            def ssd():
                link(dve.memset(flat(s_pad, "s w"), 0.0))
                dve.memset(s_E[:, 0, 0, 0, 0:1], 0.0).then_inc(SEM["s_pads"], 1)
                dve.wait_ge(SEM["s_gate_ps"], 1)
                logits = PS[2][:, 0:128].rearrange("p (t c) -> p t c", t=NT)
                link(dve.tensor_tensor(s_z, logits, rows(s_bias, NT), ALU.add))
                link(dve.tensor_scalar(s_mx, s_z, 0.0, None, ALU.max))
                dve.scalar_tensor_tensor(s_ab, s_mx, -2.0, s_z, ALU.mult, ALU.add).then_inc(SEM["s_gateb"], 1)
                dve.wait_ge(SEM["s_gact"], 1)
                link(dve.tensor_tensor(s_dt, s_mx, s_ab, ALU.add))
                dve.scalar_tensor_tensor(s_da, s_dt, -1.0, rows(s_nega, NT), ALU.mult, ALU.mult).then_inc(SEM["s_da"], 1)

                def tok_copy(gi):
                    dve.wait_ge(SEM["s_tokps"], gi + 1)
                    dve.tensor_copy(s_tok[:, :, gi * T:(gi + 1) * T],
                                    PS[4 + gi % 4][:, :].rearrange("p (t w) -> p t w", t=NT)).then_inc(SEM["s_toksb"], 1)

                for m in range(SC):
                    conv(m, s_pad, s_acc, s_conv, SEM["s_padded"], SEM["s_conved"], SEM["s_silued"])
                    if m >= 5 and m % 2 and (m - 5) // 2 < SX // 2:
                        tok_copy((m - 5) // 2)
                dve.wait_ge(SEM["s_cum"], 1)
                link(dve.tensor_copy(flat(s_ac, "t c"), PS[3][:, 0:128]))
                dve.tensor_scalar(s_nac, s_ac, -1.0, None, ALU.mult).then_inc(SEM["s_nac"], 1)
                for g in range(SG):
                    dve.wait_ge(SEM["s_cbps"], g + 1)
                    for st in range(NT):
                        v = PS[6 + g % 2][:, st * T + st * P:st * T + (st + 1) * P]
                        w = PS[6 + g % 2][:, st * T + (1 - st) * P:st * T + (2 - st) * P]
                        dve.tensor_tensor(s_CB[:, g, st, 0, :], v, upper, ALU.mult)
                        dve.tensor_tensor(s_CB[:, g, st, 1, :], v, lower, ALU.mult)
                        last = dve.tensor_copy(s_CB[:, g, st, 2, :], w)
                    last.then_inc(SEM["s_cb"], 1)
                dve.wait_ge(SEM["s_cb"], SG)

                def decay(h):
                    dve.wait_ge(SEM["s_bc"], h + 1)
                    if h >= 2:
                        dve.wait_ge(SEM["s_mv"], h - 1)
                    for st in range(NT):
                        for d in range(2):
                            last = dve.tensor_scalar(s_E[:, h % 2, st, d, :], PS[h % 2][:, d * T + st * P:d * T + (st + 1) * P],
                                                     s_ac[:, st, d * SH + h:d * SH + h + 1], 0.0, ALU.subtract, ALU.min)
                    last.then_inc(SEM["s_d"], 1)

                def weigh(h):
                    g = h // SR
                    dve.wait_ge(SEM["s_e"], h + 1)
                    if h >= 2:
                        dve.wait_ge(SEM["s_yps"], h - 1)
                    for st in range(NT):
                        for part in (0, 1, 2):
                            d = part if part < 2 else st
                            last = dve.scalar_tensor_tensor(
                                s_M[:, h % 2, st, part, :], s_CB[:, g, st, part, :], s_dt[:, st, d * SH + h:d * SH + h + 1],
                                s_E[:, h % 2, st, part, :], ALU.mult, ALU.mult)
                    last.then_inc(SEM["s_mv"], 1)

                def group_out(g):
                    for lt in range(NT):
                        dve.wait_ge(SEM["s_yps"], SR * (g + 1))
                        v = slice(g * 512, (g + 1) * 512)
                        dve.tensor_tensor(s_y[:, lt, v], PS[2 + 2 * (g % 2) + lt][:, :], s_skip[:, lt, v], ALU.add).then_inc(SEM["s_y"], 1)

                dve.wait_ge(SEM["s_skip"], 2)
                for h in range(SH):
                    decay(h)
                    if h:
                        weigh(h - 1)
                    if h > SR and h % SR == 3:
                        group_out(h // SR - 1)
                weigh(SH - 1)
                group_out(SG - 1)
                dve.wait_ge(SEM["s_ss"], NT * SG)
                dve.tensor_scalar(s_ms, s_ss, 1.0 / 512, EPS, ALU.mult, ALU.add).then_inc(SEM["s_mean"], 1)
                dve.wait_ge(SEM["s_root"], 1)
                polish(s_ms, s_root, s_inv, s_new, s_rstd)
                dve.wait_ge(gain_loaded, 16)
                for g in range(SG):
                    for t in range(NT):
                        v = s_y[:, t, g * 512:(g + 1) * 512]
                        dve.scalar_tensor_tensor(v, v, s_rstd[:, t, g:g + 1], s_gain[:, g * 512:(g + 1) * 512],
                                                 ALU.mult, ALU.mult).then_inc(o_ready, 1)
                for gi in range(SX // 2):
                    rest_of_oT(4, gi)
                residual(at[("so", SX - 1)])

            def top16(rows4):
                def all_four(op):
                    for values, top, idx in rows4:
                        last = op(values, top, idx)
                    return last

                link(all_four(lambda v, top, idx: dve.max(top[:, 0:8], v)))
                all_four(lambda v, top, idx: dve.max_index(idx[:, 0:8], top[:, 0:8], v))
                link(all_four(lambda v, top, idx: dve.match_replace(v, top[:, 0:8], v, NEG)))
                link(all_four(lambda v, top, idx: dve.max(top[:, 8:16], v)))
                all_four(lambda v, top, idx: dve.max_index(idx[:, 8:16], top[:, 8:16], v))

            def route(lyr):
                for g in range(8):
                    t, first_head = g // 2 % 2, 8 * (g // 4) + 4 * (g % 2)
                    dve.wait_ge(SEM["p_s"], 8 * lyr + g + 1)
                    top16([(p_s[:, t, hp, :], p_top[:, t, hp, :], p_idx[:, t, hp, :])
                           for hp in range(first_head, first_head + 4)])
                link(dve.memset(p_sum, 0.0))
                link(dve.tensor_copy(flat(p_idxf, "t h k"), flat(p_idx, "t h k")))
                halves = p_top.rearrange("p t (h e) k -> p (t h) e k", e=2)
                first = halves[:, :, 0, :].rearrange("p h (k o) -> p h k o", o=1)
                second = halves[:, :, 1, :].rearrange("p h (o k) -> p h o k", o=1)
                grid = [P, PH, TOPK, TOPK]
                for t in range(NT):
                    hs = slice(t * PH, (t + 1) * PH)
                    link(dve.tensor_tensor(p_cand[:, hs, :].rearrange("p h (a b) -> p h a b", a=TOPK),
                                           first[:, hs].to_broadcast(grid), second[:, hs].to_broadcast(grid), ALU.add))
                for r0 in range(0, NT * PH, 4):
                    top16([(p_cand[:, r, :], p_best[:, r, :], p_pos[:, r, :]) for r in range(r0, r0 + 4)])
                link(dve.memset(p_rsum, 0.0))
                dve.tensor_tensor(p_gate, p_best, p_best[:, :, 0:1].to_broadcast([P, NT * PH, TOPK]),
                                  ALU.subtract).then_inc(SEM["p_ex"], 1)
                link(dve.tensor_scalar(p_ab[:, 0], p_pos, 4, None, ALU.logical_shift_right))
                link(dve.tensor_scalar(p_ab[:, 1], p_pos, 15, None, ALU.bitwise_and))
                link(dve.tensor_copy(flat(p_abf, "e h k"), flat(p_ab, "e h k")))
                hot = p_hot.rearrange("p h (k a) -> p h k a", a=TOPK)
                idx = p_idxf.rearrange("p t (h e) k -> p (t h) e k", e=2)
                full = [P, NT * PH, TOPK, TOPK]
                lane = const[:, C_IOTA, 0:TOPK].rearrange("p (o q k) -> p o q k", o=1, q=1)
                for e in range(2):
                    place = p_abf[:, e].rearrange("p h (k o) -> p h k o", o=1)
                    link(dve.tensor_tensor(hot, place.to_broadcast(full), lane.to_broadcast(full), ALU.is_equal))
                    names = idx[:, :, e, :].rearrange("p h (o k) -> p h o k", o=1)
                    link(dve.tensor_tensor(hot, hot, names.to_broadcast(full), ALU.mult))
                    link(dve.tensor_reduce(p_key[:, e], hot, AX.X, ALU.add))
                dve.wait_ge(SEM["p_exd"], lyr + 1)
                link(dve.tensor_reduce(p_sum, p_gate, AX.X, ALU.add))
                link(dve.reciprocal(p_rsum, p_sum))
                dve.tensor_tensor(p_gate, p_gate, wide(p_rsum, TOPK), ALU.mult).then_inc(SEM["p_key"], 1)
                dve.wait_ge(SEM["p_Tps"], lyr + 1)
                dve.tensor_copy(flat(p_T[:, 0:2], "e t"), PS[6][:, :])
                link(dve.tensor_copy(p_T[:, 2], PS[7][:, 0:T]))

                def one_hot(it, u, first):
                    if not first or u >= 4:
                        dve.wait_ge(SEM["p_mapps"], it * 16 + (T * lyr + u - 3))
                    tok = bass.ds(it * 16 + u, 1)
                    dve.tensor_scalar(p_A[:, u % 4, :], iota, p_T[:, 0, tok], p_T[:, 2, tok], ALU.is_equal, ALU.mult)
                    dve.tensor_scalar(p_B[:, u % 4, :], iota, p_T[:, 1, tok], None, ALU.is_equal).then_inc(SEM["p_hot"], 1)

                def gate_early(it, q):
                    dve.wait_ge(SEM["p_map"], it * 4 + (64 * lyr + q + 1))
                    v = p_map[:, 0:EARLY, bass.ds(it * 16 + 4 * q, 4)]
                    dve.tensor_tensor(v, PS[q % 4][:, :].rearrange("p (t i) -> p i t", t=4)[:, 0:EARLY, :], v,
                                      ALU.mult).then_inc(SEM["p_mul"], 1)

                def tokens16(it, first=False):
                    for q in range(4):
                        for e in range(4):
                            one_hot(it, 4 * q + e, first)
                        if not first or q >= 2:
                            gate_early(it, q - 2)

                dve.wait_ge(SEM["p_gelu"], P * lyr + EARLY)
                tokens16(0, True)
                with dve.Fori(1, T // 16) as it:
                    tokens16(it)
                gate_early(T // 16, -2)
                gate_early(T // 16, -1)

            def experts(lyr):
                n0 = tables[lyr]
                n1, n2, n3 = n0 + EARLY, n0 + 2 * EARLY, n0 + 2 * P
                i0 = EARLY

                def parts(i, v, it=0, tiles=0):
                    link_in_loop(dve.tensor_copy(p_ag[0][:, i % 2, :], v), it, tiles, P * lyr + i)
                    dve.tensor_tensor(p_ag[1][:, i % 2, :], v, p_ag[0][:, i % 2, :].bitcast(F32),
                                      ALU.subtract).then_inc(SEM["p_ag"], 1)

                def link_in_loop(ins, it, tiles, count):
                    ins.then_inc(SEM["p_ag_hi"], 1)
                    dve.wait_ge(SEM["p_ag_hi"], it * tiles + (count + 1))

                def early(i, it=0, tiles=0):
                    if tiles or i >= 2:
                        dve.wait_ge(half_used, it * 8 + 2 * (n1 + i - 1))
                    row = flat(p_map[:, bass.ds(it * tiles + i, 1), :], "i t") if tiles else p_map[:, i, :]
                    parts(i, row, it, tiles)

                def late(i, it=0, tiles=0):
                    dve.wait_ge(SEM["p_gelu"], it * tiles + (P * lyr + i + 1))
                    row = flat(p_map[:, bass.ds(it * tiles + i, 1), :], "i t") if tiles else p_map[:, i, :]
                    v = p_act[:, i % 2, :]
                    dve.tensor_tensor(v, v, row, ALU.mult).then_inc(SEM["p_gated"], 1)
                    dve.wait_ge(SEM["p_gated"], it * tiles + ((P - EARLY) * lyr + i - EARLY + 1))
                    parts(i, v, it, tiles)

                dve.wait_ge(SEM["p_mul"], 64 * (lyr + 1))
                early(0)
                early(1)
                dve.wait_ge(lo_ready, 2 * (n1 + 2))
                with dve.Fori(0, EARLY // 4 - 1) as it:
                    for i in range(4):
                        rest_of_unit(n1 + i + 2, it, 8)
                        early(i + 2, it, 4)
                for i in range(EARLY - 4, EARLY):
                    rest_of_unit(n1 + i + 2)
                    if i + 2 < EARLY:
                        early(i + 2)
                rest_of_unit(n2 + 2)
                late(i0)
                rest_of_unit(n2 + 3)
                late(i0 + 1)
                rest_of_unit(n2 + 4)
                with dve.Fori(0, (P - EARLY) // 2 - 2) as it:
                    for e in range(2):
                        rest_of_unit(n2 + 5 + 2 * e, it, 8)
                        late(i0 + 2 + e, it, 2)
                        rest_of_unit(n2 + 6 + 2 * e, it, 8)
                rest_of_unit(n3 - 3)
                late(P - 2)
                rest_of_unit(n3 - 2)
                rest_of_unit(n3 - 1)
                late(P - 1)
                residual(n3 - 1)

            dve.wait_ge(x_loaded, 16)
            norm(0)
            gdn()
            norm(1)
            route(0)
            experts(0)
            norm(2)
            ssd()
            norm(3)
            route(1)
            experts(1)
            norm_stats(4)
            dve.wait_ge(last_gain_loaded, 16)
            for t in range(NT):
                ins = dve.scalar_tensor_tensor(x_sb[:, t, :], x_sb[:, t, :], n_rstd[:, t:t + 1], last_gain, ALU.mult, ALU.mult)
            ins.then_inc(SEM["finished"], 1)

        @block.scalar
        def _(act):
            def copy(o, i, scale=1.0):
                return act.activation(o, i, ACT.Copy, scale=scale)

            def split_half(n, hf, it=0, step=0):
                if n >= len(order):
                    return
                if hf == 0:
                    act.wait_ge(landed[n % RING], it * (step * 16 // (2 * RING)) + 16 * (n // RING + 1))
                if 2 * n + hf >= SPLIT:
                    act.wait_ge(half_used, it * step + (2 * n + hf + 1 - SPLIT))
                copy(w_part[0][:, (2 * n + hf) % SPLIT, :], ring[:, n % RING, hf * 512:(hf + 1) * 512]).then_inc(hi_ready, 1)

            def split(n, it=0, step=0):
                for hf in range(2):
                    split_half(n, hf, it, step)

            def norm_squares(i):
                for t in range(NT):
                    act.activation(h_junk, x_sb[:, t, :], ACT.Square, accum_out=n_ss[:, t:t + 1]).then_inc(n_sq, 1)
                    act.wait_ge(n_sq, 2 * i + t + 1)
                act.wait_ge(n_mean, i + 1)
                act.activation(n_root, n_ms, ACT.Sqrt).then_inc(n_rooted, 1)

            def norm(i):
                if i:
                    act.wait_ge(x_added, 4 * i)
                else:
                    act.wait_ge(x_loaded, 16)
                    act.wait_ge(small_loaded, 16 * N_SMALL)
                norm_squares(i)
                for k in range(KD):
                    act.wait_ge(n_hTps, 4 * i + k // 2 + 1)
                    copy(hT[0][:, k, :], PS[k // 2][:, (k % 2) * T:(k % 2 + 1) * T], norm_w[:, i, k:k + 1]).then_inc(n_hT, 1)

            def softplus_tail(ab, exps, n):
                act.activation(ab, ab, ACT.Exp).then_inc(exps, 1)
                act.wait_ge(exps, n)
                return act.activation(ab, ab, ACT.Ln, bias=1.0)

            def gdn():
                for hf in range(2):
                    for q in range(KD // 2):
                        split(at[("gz", hf, q)] + 2)
                    act.wait_ge(half_used, 2 * (at[("gz", hf, 3)] + 1))
                    for t in range(NT):
                        act.activation(g_siluz[:, t, hf * 512:(hf + 1) * 512], PS[4 + 2 * hf + t][:, :], ACT.Silu).then_inc(SEM["g_zs"], 1)
                act.wait_ge(SEM["g_gateb"], 1)
                act.activation(g_beta, PS[2][:, 0:64].rearrange("p (t c) -> p t c", t=NT)[:, :, 16:32], ACT.Sigmoid).then_inc(SEM["g_betas"], 1)
                act.activation(g_nega, g_alog, ACT.Exp)
                softplus_tail(g_ab, SEM["g_gexp"], 1).then_inc(SEM["g_gact"], 1)

                def silu(m):
                    act.wait_ge(SEM["g_conved"], m + 1)
                    act.activation(g_feat[:, m, :], g_acc[:, m % 4, :], ACT.Silu).then_inc(SEM["g_silued"], 1)

                act.wait_ge(SEM["g_pads"], 1)
                for m in range(GC):
                    split_half(at[("gq", m)] + 2, 0)
                    act.wait_ge(half_used, 2 * (at[("gq", m)] + 1))
                    if m >= 4:
                        act.wait_ge(SEM["g_conved"], m - 3)
                    copy(g_pad[:, m % 4, 2:2 + T], PS[m % 2][:, 0:T]).then_inc(SEM["g_padded"], 1)
                    split_half(at[("gq", m)] + 2, 1)
                    if m:
                        silu(m - 1)
                    if m >= 5 and m % 2 and (m - 5) // 2 < GH:
                        gi = (m - 5) // 2
                        act.wait_ge(SEM["g_toksb"], gi + 1)
                        for t in range(NT):
                            for e in range(2):
                                last = act.activation(h_junk[:, 0:P], g_tok[:, t, 2 * gi + e, :],
                                                      ACT.Square, accum_out=g_ss[:, t, 2 * gi + e:2 * gi + e + 1])
                                if 2 * t + e < 3:
                                    last.then_inc(SEM["g_junk"], 1)
                                    act.wait_ge(SEM["g_junk"], 3 * gi + 2 * t + e + 1)
                        last.then_inc(SEM["g_sqsum"], 1)
                        act.wait_ge(SEM["g_sqsum"], gi + 1)
                silu(GC - 1)
                act.wait_ge(SEM["g_cumsb"], 1)
                act.activation(g_eg, g_gc, ACT.Exp).then_inc(SEM["g_exps"], 1)
                act.activation(g_wx, g_gt, ACT.Exp).then_inc(SEM["g_exps"], 1)
                copy(g_row, PS[2][0:GH, :]).then_inc(SEM["g_rows"], 1)
                act.wait_ge(SEM["g_mean"], 1)
                act.activation(g_root, g_ms, ACT.Sqrt).then_inc(SEM["g_root"], 1)
                for gi in range(GH):
                    act.wait_ge(SEM["g_backps"], gi + 1)
                    copy(g_feat[:, 2 * gi:2 * gi + 2, :], PS[4 + gi % 4][:, :].rearrange("p (e t) -> p e t", e=2)).then_inc(SEM["g_backsb"], 1)
                for h in range(GH):
                    act.wait_ge(SEM["g_logE"], h + 1)
                    act.activation(g_E[:, h, :], g_E[:, h, :], ACT.Exp).then_inc(SEM["g_E"], 1)
                for n in range(GB, LEVELS * GB):
                    b = n % GB
                    act.wait_ge(SEM["g_Yps"], n + 1)
                    copy(g_Y[:, 4 * b:4 * b + 4, :], PS[n % 2][:, :].rearrange("p (s d) -> p s d", s=4)).then_inc(SEM["g_Y"], 1)
                for q4 in range(4):
                    act.wait_ge(SEM["g_S1ps"], q4 + 1)
                    copy(g_S[:, 4 * q4:4 * q4 + 4, :], PS[4 + q4][:, :].rearrange("p (s d) -> p s d", s=4)).then_inc(SEM["g_S1"], 1)
                act.wait_ge(SEM["g_omean"], 1)
                act.activation(g_root[:, 0, :], g_ms[:, 0, :], ACT.Sqrt).then_inc(SEM["g_oroot"], 1)
                for b in range(4):
                    act.wait_ge(oT_psum, b + 1)
                    copy(hT[0][:, 2 * b:2 * b + 2, :], PS[b][:, :].rearrange("p (e t) -> p e t", e=2)).then_inc(oT_ready, 1)
                for k in range(GH):
                    split(at[("go", k)] + 2)

            def ssd():
                for nb in range(SI // 512):
                    for q in range(KD // 2):
                        split(at[("sz", nb, q)] + 2)
                    act.wait_ge(half_used, 2 * (at[("sz", nb, 3)] + 1))
                    for t in range(NT):
                        act.activation(s_siluz[:, t, nb * 512:(nb + 1) * 512], PS[4 + 2 * (nb % 2) + t][:, :], ACT.Silu).then_inc(SEM["s_zs"], 1)
                act.activation(s_nega, s_alog, ACT.Exp)
                act.wait_ge(SEM["s_gateb"], 1)
                softplus_tail(s_ab, SEM["s_gexp"], 1).then_inc(SEM["s_gact"], 1)

                def silu(m):
                    act.wait_ge(SEM["s_conved"], m + 1)
                    act.activation(s_feat[:, m, :], s_acc[:, m % 4, :], ACT.Silu, bias=s_cbias[:, m:m + 1]).then_inc(SEM["s_silued"], 1)

                act.wait_ge(SEM["s_pads"], 1)
                for m in range(SC):
                    split_half(at[("sx", m)] + 2, 0)
                    act.wait_ge(half_used, 2 * (at[("sx", m)] + 1))
                    if m >= 4:
                        act.wait_ge(SEM["s_conved"], m - 3)
                    copy(s_pad[:, m % 4, 2:2 + T], PS[m % 2][:, 0:T]).then_inc(SEM["s_padded"], 1)
                    split_half(at[("sx", m)] + 2, 1)
                    if m:
                        silu(m - 1)
                silu(SC - 1)
                act.wait_ge(SEM["s_cum"], 1)
                copy(s_row, PS[2][0:SH, :]).then_inc(SEM["s_rows"], 1)
                act.wait_ge(SEM["s_nac"], 1)

                def group_squares(g):
                    for t in range(NT):
                        act.wait_ge(SEM["s_yg"], 2 * g + t + 1)
                        act.activation(s_junk, s_y[:, t, g * 512:(g + 1) * 512], ACT.Square,
                                       accum_out=s_ss[:, t, g:g + 1]).then_inc(SEM["s_ss"], 1)
                        act.wait_ge(SEM["s_ss"], 2 * g + t + 1)

                for h in range(SH):
                    act.wait_ge(SEM["s_bc"], h + 1)
                    if h >= 2:
                        act.wait_ge(SEM["s_mv"], h - 1)
                    act.wait_ge(SEM["s_d"], h + 1)
                    act.activation(s_E[:, h % 2, 0, 2, :], PS[h % 2][:, P:2 * P], ACT.Exp, bias=s_nac[:, 0, h:h + 1])
                    act.activation(s_E[:, h % 2, 1, 2, :], PS[h % 2][:, T:T + P], ACT.Exp, bias=s_nac[:, 1, SH + h:SH + h + 1])
                    v = s_E[:, h % 2, :, 0:2, :].rearrange("p t e d -> p t (e d)")
                    act.activation(v, v, ACT.Exp).then_inc(SEM["s_e"], 1)
                    if h > SR and h % SR == 5:
                        group_squares(h // SR - 1)
                group_squares(SG - 1)
                act.wait_ge(SEM["s_mean"], 1)
                act.activation(s_root, s_ms, ACT.Sqrt).then_inc(SEM["s_root"], 1)
                def y_out(gi):
                    act.wait_ge(oT_psum, 4 + gi + 1)
                    b = gi % 4
                    copy(hT[0][:, 2 * b:2 * b + 2, :], PS[b][:, :].rearrange("p (e t) -> p e t", e=2)).then_inc(oT_ready, 1)

                for gi in range(4):
                    y_out(gi)
                for k in range(SX):
                    split(at[("so", k)] + 2)
                    if k % 2 and k // 2 + 4 < SX // 2:
                        y_out(k // 2 + 4)

            def route(lyr):
                for m in range(HP):
                    split_half(at[("pq", lyr, m)] + 2, 0)
                    act.wait_ge(half_used, 2 * (at[("pq", lyr, m)] + 1))
                    copy(p_qT[:, m, :], PS[m % 2][:, 0:T]).then_inc(SEM["p_q"], 1)
                    split_half(at[("pq", lyr, m)] + 2, 1)
                for g in range(8):
                    t, first_head = g // 2 % 2, 8 * (g // 4) + 4 * (g % 2)
                    act.wait_ge(SEM["p_sps"], 8 * lyr + g + 1)
                    copy(p_s[:, t, first_head:first_head + 4, :], PS[2 + g % 4][:, :].rearrange("p (e k) -> p e k", e=4)).then_inc(SEM["p_s"], 1)

            def experts(lyr):
                n0 = tables[lyr]
                n1, n2, n3 = n0 + EARLY, n0 + 2 * EARLY, n0 + 2 * P
                i0 = EARLY

                def early(i, it=0, tiles=0):
                    split_half(n0 + i + 2, 0, it, 8)
                    act.wait_ge(half_used, it * 8 + 2 * (n0 + i + 1))
                    o = flat(p_map[:, bass.ds(it * tiles + i, 1), :], "i t") if tiles else p_map[:, i, :]
                    act.activation(o, PS[i % 2][:, 0:T], ACT.Gelu).then_inc(SEM["p_gelu"], 1)
                    split_half(n0 + i + 2, 1, it, 8)

                def late(i, n, it=0, tiles=0):
                    split_half(n + 2, 0, it, 8)
                    act.wait_ge(half_used, it * 8 + 2 * (n + 1))
                    if tiles or i >= i0 + 2:
                        act.wait_ge(SEM["p_ag"], it * tiles + (P * lyr + i - 1))
                    act.activation(p_act[:, i % 2, :], PS[i % 2][:, 0:T], ACT.Gelu).then_inc(SEM["p_gelu"], 1)
                    split_half(n + 2, 1, it, 8)

                for i in range(4):
                    early(i)
                with act.Fori(0, EARLY // 4 - 2) as it:
                    for i in range(4, 8):
                        early(i, it, 4)
                act.wait_ge(SEM["p_ex"], lyr + 1)
                act.activation(p_gate, p_gate, ACT.Exp).then_inc(SEM["p_exd"], 1)
                for i in range(EARLY - 4, EARLY):
                    early(i)

                def maps16(it):
                    for q in range(4):
                        act.wait_ge(SEM["p_mapps"], it * 16 + (T * lyr + 4 * q + 4))
                        copy(p_map[:, EARLY:P, bass.ds(it * 16 + 4 * q, 4)],
                             PS[q][:, :].rearrange("p (t i) -> p i t", t=4)[:, EARLY:P, :]).then_inc(SEM["p_map"], 1)

                with act.Fori(0, T // 16) as it:
                    maps16(it)
                with act.Fori(0, EARLY // 4) as it:
                    for i in range(4):
                        split(n1 + i + 2, it, 8)
                late(i0, n2)
                late(i0 + 1, n2 + 1)
                split(n2 + 4)
                with act.Fori(0, (P - EARLY) // 2 - 2) as it:
                    for e in range(2):
                        late(i0 + 2 + e, n2 + 3 + 2 * e, it, 2)
                        split(n2 + 6 + 2 * e, it, 8)
                late(P - 2, n3 - 5)
                split(n3 - 2)
                late(P - 1, n3 - 3)
                split(n3)
                split(n3 + 1)

            split(0)
            split(1)
            norm(0)
            gdn()
            norm(1)
            route(0)
            experts(0)
            norm(2)
            ssd()
            norm(3)
            route(1)
            experts(1)
            act.wait_ge(x_added, 16)
            norm_squares(4)

        @block.gpsimd
        def _(pool):
            def rows(v, n):
                return v.rearrange("p (o c) -> p o c", o=1).to_broadcast([v.shape[0], n, v.shape[1]])

            def wide(v, n):
                return v.rearrange("p (a o) -> p a o", o=1).to_broadcast([v.shape[0], v.shape[1], n])

            loads = [(const[:, :, :], a["const"]), (levels, a["levels"]), (norm_w, a["norms"]),
                     (g_conv, a["gdn_conv"]), (g_wg, a["gdn_gates"]),
                     (g_bias, a["gdn_dt_bias"].partition_broadcast(P)), (g_alog, a["gdn_a_log"].partition_broadcast(P)),
                     (g_gain[:, 0, :], a["gdn_norm"].partition_broadcast(P)),
                     (s_conv, a["ssd_conv"]), (s_cbias, a["ssd_conv_b"]),
                     (s_bias, a["ssd_dt_bias"].partition_broadcast(P)), (s_alog, a["ssd_a_log"].partition_broadcast(P)),
                     (s_D, a["ssd_d"].partition_broadcast(P))]
            assert len(loads) == N_SMALL
            for o, i in loads:
                pool.dma_start(o, i).then_inc(small_loaded, 16)

            def rest_of_unit(n, it=0, step=0):
                for hf in range(2):
                    pool.wait_ge(hi_ready, it * step + (2 * n + hf + 1))
                    s = (2 * n + hf) % SPLIT
                    pool.tensor_tensor(w_part[1][:, s, :], ring[:, n % RING, hf * 512:(hf + 1) * 512],
                                       w_part[0][:, s, :].bitcast(F32), ALU.subtract).then_inc(lo_ready, 1)

            def rest_of_units(first, end):
                for n in range(first, end):
                    rest_of_unit(n)

            def early_experts(lyr, start):
                rest_of_units(start, tables[lyr] + 2)
                with pool.Fori(0, EARLY // 4) as it:
                    for q in range(4):
                        rest_of_unit(tables[lyr] + 2 + q, it, 8)

            def load_keys(lyr):
                pool.wait_ge(x_added, 8 * lyr + 4)
                pool.dma_start(p_kT, a["peer_kT"][lyr]).then_inc(keys_loaded, 16)

            rest_of_units(0, at[("go", 2)])
            pool.wait_ge(small_loaded, 16 * N_SMALL)
            pool.wait_ge(SEM["g_zs"], 4)
            for t in range(NT):
                v = g_siluz[:, t, :].rearrange("p (h d) -> p h d", h=GH)
                pool.tensor_tensor(v, v, rows(g_gain[:, 0, :], GH), ALU.mult).then_inc(SEM["g_gz"], 1)
            for n in range(LEVELS * GB):
                level, b = divmod(n, GB)
                if n < GB:
                    pool.wait_ge(SEM["g_A"], 2 * (b % 4) + 2)
                if n >= 2:
                    pool.wait_ge(SEM["g_Yps"], n - 1)
                    if n - 2 < GB:
                        pool.wait_ge(SEM["g_T"], t_count(n - 2))
                d = b // (GB // 2)
                pool.tensor_tensor(g_mask[:, 4 * (n % 2):4 * (n % 2) + 4, :], g_AT[:, 4 * b:4 * b + 4, :],
                                   rows(levels[:, d * LEVELS + level, :], 4), ALU.mult).then_inc(SEM["g_mask"], 1)
            pool.wait_ge(SEM["g_U0"], 1)
            for q4 in range(4):
                d, h0 = q4 // 2, 4 * (q4 % 2)
                pool.tensor_tensor(g_kS[:, 4 * q4:4 * q4 + 4, :], g_tok[:, d, GH + h0:GH + h0 + 4, :],
                                   wide(g_wx[:, d, d * GH + h0:d * GH + h0 + 4], P), ALU.mult).then_inc(SEM["g_kS"], 1)
            QE = g_E.rearrange("p h (c i) -> p h c i", c=NT)
            for c in range(NT):
                pool.tensor_tensor(g_tok[:, c, 0:GH, :], QE[:, :, c, :], rows(upper, GH), ALU.mult).then_inc(SEM["g_P"], 1)
                pool.tensor_tensor(g_PTb[:, :, c, :], QE[:, :, c, :], rows(lower, GH), ALU.mult).then_inc(SEM["g_P"], 1)
            rest_of_units(at[("go", 2)], at[("pq", 0, 0)])
            load_keys(0)
            early_experts(0, at[("pq", 0, 0)])
            pool.wait_ge(x_added, 8)
            pool.dma_start(s_wg, a["ssd_gates"]).then_inc(s_wg_loaded, 16)
            pool.wait_ge(lo_ready, 2 * at[("sz", 0, 0)])
            rest_of_units(at[("sz", 0, 0)], at[("so", 2)])
            pool.wait_ge(SEM["s_silued"], SC)
            pool.dma_start(s_gain, a["ssd_norm"].partition_broadcast(P)).then_inc(gain_loaded, 16)
            pool.wait_ge(SEM["s_toksb"], SX // 2)
            for t in range(NT):
                v = s_tok[:, t, :].rearrange("p (h d) -> p h d", h=SH)
                pool.tensor_tensor(s_skip[:, t, :].rearrange("p (h d) -> p h d", h=SH), v, wide(s_D, SP_),
                                   ALU.mult).then_inc(SEM["s_skip"], 1)
            pool.wait_ge(SEM["s_zs"], 8)
            for h in range(SH):
                pool.wait_ge(SEM["s_mv"], h + 1)
                m = s_M[:, h % 2]
                pool.tensor_tensor(m[:, :, 0, :], m[:, :, 0, :], m[:, :, 1, :], ALU.add).then_inc(SEM["s_m"], 1)
                if h > SR and h % SR == 4 or h == SH - 1:
                    g = h // SR - (h != SH - 1)
                    for t in range(NT):
                        pool.wait_ge(SEM["s_y"], 2 * g + t + 1)
                        v = s_y[:, t, g * 512:(g + 1) * 512]
                        pool.tensor_tensor(v, v, s_siluz[:, t, g * 512:(g + 1) * 512], ALU.mult).then_inc(SEM["s_yg"], 1)
            rest_of_units(at[("so", 2)], at[("pq", 1, 0)])
            load_keys(1)
            early_experts(1, at[("pq", 1, 0)])


def layout(i):
    c = np.ascontiguousarray

    def by_token(w):
        n = w.shape[1] // 512
        return c(w.reshape(KD // 2, 2, P, n, 512).transpose(3, 0, 2, 1, 4).reshape(n, KD // 2, P, D))

    def by_channel(w):
        n = w.shape[1] // P
        return c(w.reshape(KD, P, n, P).transpose(2, 1, 0, 3).reshape(n, P, D))

    def gates(w):
        return c(w.reshape(KD, P, -1).transpose(1, 0, 2))

    def taps(w):
        return c(w.reshape(TAPS, -1, P).transpose(2, 1, 0))

    masks, levels = host_constants()
    g, s = i["gdn_w_in"][0], i["ssd_w_in"][0]
    qkv, ch = GC * P, SC * P
    return {
        "x": c(i["x"][0].reshape(NT, P, D).transpose(1, 0, 2)),
        "const": masks, "levels": levels.astype(np.float16),
        "norms": c(np.stack([i["norm_mix"][0], i["norm_ffn"][0], i["norm_mix"][1], i["norm_ffn"][1]])
                   .reshape(4, KD, P).transpose(2, 0, 1)),
        "norm_final": i["norm_final"],
        "gdn_qkv": by_channel(g[:, :qkv]), "gdn_z": by_token(g[:, qkv:qkv + D]), "gdn_gates": gates(g[:, qkv + D:]),
        "gdn_conv": taps(i["gdn_conv"][0]), "gdn_a_log": c(i["gdn_a_log"][0].reshape(-1)),
        "gdn_dt_bias": c(i["gdn_dt_bias"][0].reshape(-1)), "gdn_norm": c(i["gdn_norm"][0]),
        "gdn_out": c(i["gdn_w_out"][0].reshape(GH, P, D)),
        "ssd_z": by_token(s[:, :SI]), "ssd_xbc": by_channel(s[:, SI:SI + ch]), "ssd_gates": gates(s[:, SI + ch:]),
        "ssd_conv": taps(i["ssd_conv"][0]), "ssd_conv_b": c(i["ssd_conv_b"][0].reshape(SC, P).T),
        "ssd_a_log": c(i["ssd_a_log"][0].reshape(-1)), "ssd_dt_bias": c(i["ssd_dt_bias"][0].reshape(-1)),
        "ssd_d": c(i["ssd_d"][0]), "ssd_norm": c(i["ssd_norm"][0]), "ssd_out": c(i["ssd_w_out"][0].reshape(SX, P, D)),
        "peer_wq": np.stack([by_channel(i["peer_w_q"][n]) for n in range(2)]),
        "peer_kT": c(i["peer_keys"].reshape(2, HP, P, P).transpose(0, 3, 1, 2)),
        "peer_u": c(i["peer_u"].reshape(2, P, P, KD, P).transpose(0, 1, 4, 3, 2).reshape(2, P, P, D)),
        "peer_v": c(i["peer_v"].reshape(2, P, P, D)),
    }


def kernel(**inputs):
    import concourse.bacc as _bacc
    from concourse.bass_utils import run_bass_kernel_spmd as _run

    arrays = layout({k: np.asarray(v) for k, v in inputs.items()})
    nc = _bacc.Bacc("TRN2", target_bir_lowering=False, num_devices=1)
    a = {k: nc.dram_tensor(f"in_{k}", v.shape, mybir.dt.from_np(v.dtype), kind="ExternalInput").ap()
         for k, v in arrays.items()}
    out = nc.dram_tensor("out", (P, NT, D), F32, kind="ExternalOutput").ap()
    hybrid_encoder(nc, a, out)
    r = _run(nc, [{f"in_{k}": v for k, v in arrays.items()}], core_ids=[0])
    got = r.results[0]["out"]
    return np.ascontiguousarray(got.transpose(1, 0, 2)).reshape(1, T, D)
```

```python
from contextlib import ExitStack

import numpy as np

import concourse.bass as bass
from concourse import mybir

F32 = mybir.dt.float32
F32R = mybir.dt.float32r
U32 = mybir.dt.uint32
ALU = mybir.AluOpType
ACT = mybir.ActivationFunctionType
AX = mybir.AxisListType

P = 128
D = 1024
KD = D // P
T = 256
NT = T // P
EPS = 1e-6
TAPS = 5

GH = 8
GC = 3 * GH
GSYS = 2 * GH * NT
GB = GSYS // 4
LEVELS = 7

SH = 32
SP_ = 64
SG = 4
SR = SH // SG
SI = SH * SP_
SX = SI // P
SC = SX + 2 * SG

PH = 8
HP = 2 * PH
TOPK = 16
NEG = -3.0e38

RING = 4
SPLIT = 4
EARLY = 56


def host_constants():
    j, i = np.arange(P)[:, None], np.arange(P)[None, :]
    rows = [j == i, j <= i, j >= i, np.ones((P, P)), np.broadcast_to(i, (P, P))]
    levels = []
    for flip in (False, True):
        for level in range(LEVELS):
            b = 1 << level
            hi, lo = (j, i) if flip else (i, j)
            levels.append((hi // b % 2 == 1) & (lo // b == hi // b - 1))
    return [np.stack([np.asarray(r, np.float32) for r in m], axis=1) for m in (rows, levels)]


C_EYE, C_UPI, C_LOI, C_ONE, C_IOTA, C_ALL = range(6)


def weight_stream(a):
    order = []
    for hf in range(2):
        order += [(("gz", hf, k), a["gdn_z"][hf, k]) for k in range(KD // 2)]
    order += [(("gq", m), a["gdn_qkv"][m]) for m in range(GC)]
    order += [(("go", k), a["gdn_out"][k]) for k in range(GH)]
    tables = []

    def peer(lyr):
        run = [(("pq", lyr, m), a["peer_wq"][lyr, m]) for m in range(HP)]
        tables.append(len(order) + len(run))
        return run + [None] * (2 * P)

    order += peer(0)
    order += [(("sx", m), a["ssd_xbc"][m]) for m in range(SC)]
    for nb in range(SG):
        order += [(("sz", nb, k), a["ssd_z"][nb, k]) for k in range(KD // 2)]
    order += [(("so", k), a["ssd_out"][k]) for k in range(SX)]
    order += peer(1)
    return order, {o[0]: n for n, o in enumerate(order) if o is not None}, tables


def hybrid_encoder(nc, a, out):
    order, at, tables = weight_stream(a)
    ctx = ExitStack()
    with ctx:
        def sb(name, shape, dt=F32):
            return ctx.enter_context(nc.sbuf_tensor(name, shape, dt))

        def sem(name):
            return ctx.enter_context(nc.semaphore(name))

        PS = [ctx.enter_context(nc.psum_tensor(f"bank{i}", [P, 512], F32)) for i in range(8)]

        def cutter(tensor, size):
            at_column = [0]

            def take(*shape, dt=None):
                n = int(np.prod(shape))
                v = tensor[:, at_column[0]:at_column[0] + n]
                at_column[0] += n
                assert at_column[0] <= size, at_column
                if dt is not None:
                    v = v.bitcast(dt)
                if len(shape) > 1:
                    names = "abcd"[:len(shape)]
                    v = v.rearrange(f"p ({' '.join(names)}) -> p {' '.join(names)}", **dict(zip(names, shape)))
                return v

            return take

        def system(direction, head, chunk):
            return (direction * GH + head) * NT + chunk

        def flat(v, names):
            return v.rearrange(f"p {names} -> p ({names})")

        x_sb = sb("x_sb", [P, NT, D])
        hT = [sb("hT_" + s, [P, KD, T], F32R) for s in ("hi", "lo")]
        ring = sb("ring", [P, RING, D])
        w_part = [sb("w_" + s, [P, SPLIT, D // 2], F32R) for s in ("hi", "lo")]
        p_ag = [sb("p_ag_" + s, [P, 2, T], F32R) for s in ("hi", "lo")]
        const = sb("const", [P, C_ALL, P])
        arena = sb("arena", [P, P * T])
        work = sb("work", [P, 2304])
        small = sb("small", [P, 1660])
        h_tok = arena[:, 14336:14336 + NT * D].rearrange("p (t d) -> p t d", t=NT)
        h_junk = arena[:, 18432:18432 + D]
        last_gain = ring[:, 0, :]

        ident = const[:, C_EYE, :]
        upper = const[:, C_UPI, :]
        lower = const[:, C_LOI, :]
        ones = const[:, C_ONE, :]
        iota = const[:, C_IOTA, :]

        tiny = cutter(small, 1660)
        norm_w = tiny(4, KD)
        n_ss, n_ms, n_root, n_inv, n_new, n_rstd, n_idle = (tiny(NT) for _ in range(7))
        g_scratch = tiny(512)
        g_tiny = cutter(g_scratch, 512)
        g_ss, g_ms, g_root, g_inv, g_new, g_rstd = (g_tiny(NT, 2 * GH) for _ in range(6))

        g_conv = tiny(GC, TAPS)
        g_bias, g_alog, g_nega = (tiny(2 * GH) for _ in range(3))
        g_z, g_mx, g_ab, g_g, g_beta, g_gc, g_gt, g_wx, g_eg, g_egq = (g_tiny(NT, 2 * GH) for _ in range(10))
        take = cutter(work, 2304)
        levels = take(LEVELS * P).bitcast(mybir.dt.float16).rearrange("p (l d) -> p l d", d=P)
        g_wg = take(KD, 4 * GH)
        g_gain = take(1, P)
        take = cutter(arena, P * T)
        g_feat = take(GC, T)
        g_tok = take(NT, GC, P)
        g_siluz = take(NT, D)
        g_AT = take(GSYS, P)
        g_T = take(GSYS, P)
        g_TT = take(GSYS, P)
        g_Y = take(GSYS, P)
        spare = take(2048)
        g_pad = flat(g_Y, "s d")[:, 0:4 * 260].rearrange("p (s w) -> p s w", s=4)
        g_acc = flat(g_Y, "s d")[:, 1040:1040 + 4 * T].rearrange("p (s w) -> p s w", s=4)
        g_E = g_feat[:, 2 * GH:3 * GH, :]
        g_tmp = g_Y[:, 0:16, :]
        g_PTb = spare.rearrange("p (h c d) -> p h c d", h=GH, c=NT)
        g_mask = g_tok[:, 0, 0:GH, :]
        g_vn = g_T
        g_kS = g_Y[:, 0:16, :]
        g_S = g_Y[:, 16:32, :]
        g_vp = g_AT[:, 0:16, :]
        g_inter = g_AT[:, 16:32, :]
        g_o = g_TT[:, 0:16, :]
        g_sq = g_TT[:, 16:32, :]

        s_conv = tiny(SC, TAPS)
        s_cbias = tiny(SC)
        s_wg = work[:, 0:KD * 2 * SH].rearrange("p (k c) -> p k c", k=KD)
        s_bias, s_alog, s_nega, s_D = tiny(2 * SH), tiny(2 * SH), tiny(2 * SH), tiny(SH)
        s_dt, s_da, s_ac, s_nac = (tiny(NT, 2 * SH) for _ in range(4))
        over_g = cutter(g_scratch, 512)
        s_z, s_mx, s_ab = (over_g(NT, 2 * SH) for _ in range(3))
        s_ss, s_ms, s_root, s_inv, s_new, s_rstd = (tiny(NT, SG) for _ in range(6))
        take = cutter(arena, P * T)
        s_feat = take(SC, T)
        s_tok = take(NT, SI)
        s_siluz = take(NT, SI)
        s_y = take(NT, SI)
        s_skip = take(NT, SI)
        s_CB = take(SG, NT, 3, P)
        s_pad = take(4, 260)
        s_acc = take(4, T)
        s_E = take(2, NT, 3, P)
        s_M = take(2, NT, 3, P)
        s_junk = take(512)
        s_gain = arena[:, 25600:25600 + SI]

        take = cutter(arena, P * T)
        take(EARLY * T)
        p_qT = take(HP, T)
        p_s = take(NT, HP, P)
        p_cand = take(NT * PH, TOPK * TOPK)
        p_kT = flat(p_cand, "h k")[:, 0:HP * P].rearrange("p (h k) -> p h k", h=HP)
        p_hot = flat(p_qT, "h t").rearrange("p (h k) -> p h k", h=NT * PH)
        p_top = take(NT, HP, TOPK)
        p_idx = take(NT, HP, TOPK, dt=U32)
        p_idxf = take(NT, HP, TOPK)
        p_best = take(NT * PH, TOPK)
        p_pos = take(NT * PH, TOPK, dt=U32)
        p_ab = take(2, NT * PH, TOPK, dt=U32)
        p_abf = take(2, NT * PH, TOPK)
        p_key = take(2, NT * PH, TOPK)
        p_gate = take(NT * PH, TOPK)
        p_sum, p_rsum = take(NT * PH), take(NT * PH)
        p_map = arena[:, :].rearrange("p (i t) -> p i t", i=P)
        take = cutter(work, 2304)
        p_T = take(3, T)
        p_A = take(8, P)
        p_B = [flat(v[:, :, :], "s t").rearrange("p (s d) -> p s d", s=4) for v in p_ag]
        p_minus = g_scratch[:, 0:T]
        p_sq = take(4, P)
        p_act = work[:, 0:2 * T].rearrange("p (s t) -> p s t", s=2)

        row = [flat(p[0:SH, :, :], "s t") for p in p_ag]
        pick = sb("pick", [SH, SH], F32R)[:, :]

        x_loaded, small_loaded, gain_loaded = sem("x_loaded"), sem("small_loaded"), sem("gain_loaded")
        const_loaded = sem("const_loaded")
        last_gain_loaded = sem("last_gain_loaded")
        landed = [sem(f"unit_landed{i}") for i in range(RING)]
        hi_ready, lo_ready = sem("hi_ready"), sem("lo_ready")
        half_used = sem("half_used")
        dve_chain = sem("dve_chain")
        n_sq, n_mean, n_rooted, n_h, n_hTps, n_hT = (sem("n_" + s) for s in (
            "squares", "mean", "root", "h", "hT_psum", "hT"))
        row_hi, row_lo, picks, n_hTlo, oT_lo, keys_loaded, s_wg_loaded = sem("row_hi"), sem("row_lo"), sem("picks"), sem("n_hT_lo"), sem("oT_lo"), sem("keys_loaded"), sem("s_wg_loaded")
        x_added = sem("x_added")
        oT_psum, oT_ready, o_ready = sem("oT_psum"), sem("oT_ready"), sem("o_ready")
        SEM = {s: sem(s) for s in (
            "g_gate_ps g_zs g_pads g_padded g_conved g_silued g_gateb g_gact g_gexp g_gg g_betas g_cum g_cumsb g_exps "
            "g_tokps g_toksb g_sqsum g_mean g_root g_qk g_backps g_backsb g_bc g_dexp g_logE g_E g_kq g_QE g_A g_P g_mask g_Yps g_Y "
            "g_Zps g_TT g_Tps g_T g_kS g_U0 g_vn0 g_S1ps g_S1 g_RQ g_v1 g_int g_U1 g_vn1 g_Ops g_O g_osum g_omean g_oroot g_gz "
            "s_gate_ps s_gateb s_gexp s_pads s_mv s_yg s_zs s_padded s_conved s_silued s_gact s_da s_cum s_nac s_tokps s_toksb s_skip "
            "s_cbps s_cb s_bc s_d s_e s_off s_m s_yps s_y s_ss s_mean s_root "
            "p_q p_sps p_s p_ex p_exd p_key p_Tps p_Tsb p_hot p_hotS p_hotB p_dist p_sq p_mapps p_map p_mul p_gelu p_gated p_ag_hi p_ag "
            "finished stored").split()}
        N_SMALL = 11

        block = ctx.enter_context(nc.Block())

        @block.sync
        def _(sp):
            sp.dma_start(x_sb[:, :, :], a["x"]).then_inc(x_loaded, 16)

            def load_unit(n):
                if n >= RING:
                    sp.wait_ge(lo_ready, 2 * (n - RING + 1))
                sp.dma_start(ring[:, n % RING, :], order[n][1]).then_inc(landed[n % RING], 16)

            def load_tables(lyr):
                n0 = tables[lyr]
                U, V = a["peer_u"][lyr], a["peer_v"][lyr]

                def one(k, table, i, it=0, tiles=0):
                    sp.wait_ge(lo_ready, it * 8 + 2 * (n0 + k - RING + 1))
                    src = table[bass.ds(it * tiles + i, 1)].rearrange("a p c -> p (a c)") if tiles else table[i]
                    sp.dma_start(ring[:, (n0 + k) % RING, :], src).then_inc(landed[(n0 + k) % RING], 16)

                for base, table in ((0, U), (EARLY, V)):
                    with sp.Fori(0, EARLY // 4) as it:
                        for q in range(4):
                            one(base + q, table, q, it, 4)
                base, i = 2 * EARLY, EARLY
                one(base, U, i)
                one(base + 1, U, i + 1)
                one(base + 2, V, i)
                with sp.Fori(0, (P - EARLY) // 2 - 1) as it:
                    one(base + 3, U, i + 2, it, 2)
                    one(base + 4, V, i + 1, it, 2)
                    one(base + 5, U, i + 3, it, 2)
                    one(base + 6, V, i + 2, it, 2)
                one(2 * P - 1, V, P - 1)

            n = 0
            while n < len(order):
                if order[n] is None:
                    load_tables(0 if n == tables[0] else 1)
                    n += 2 * P
                else:
                    load_unit(n)
                    n += 1
            sp.wait_ge(half_used, 2 * len(order))
            sp.dma_start(last_gain, a["norm_final"].partition_broadcast(P)).then_inc(last_gain_loaded, 16)
            sp.wait_ge(SEM["finished"], 1)
            sp.dma_start(out, x_sb[:, :, :]).then_inc(SEM["stored"], 16)
            sp.wait_ge(SEM["stored"], 16)

        @block.tensor
        def _(pe):
            def mm(o, w, r, first=True, last=True):
                return pe.matmul(o, w, r, start=first, stop=last)

            def part_mm(o, w, r, first, last):
                mm(o, w(0), r(0), first, False)
                mm(o, w(0), r(1), False, False)
                return mm(o, w(1), r(0), False, last)

            def half(n, hf, it=0, step=0):
                pe.wait_ge(lo_ready, it * step + (2 * n + hf + 1))
                return (2 * n + hf) % SPLIT

            def turn_h(i):
                pe.wait_ge(n_h, 2 * (i + 1))
                for b in range(4):
                    for kk in range(2):
                        for t in range(NT):
                            k = 2 * b + kk
                            last = pe.transpose(PS[b][:, (2 * kk + t) * P:(2 * kk + t + 1) * P],
                                                h_tok[:, t, k * P:(k + 1) * P], ident)
                    last.then_inc(n_hTps, 1)

            def await_h(fresh, k):
                if fresh is not None:
                    pe.wait_ge(n_hTlo, KD * fresh + k + 1)

            def by_token(name, bank, fresh=None):
                for q in range(KD // 2):
                    for kk in range(2):
                        k = 2 * q + kk
                        s = half(at[(*name, q)], kk)
                        await_h(fresh, k)
                        for t in range(NT):
                            last = part_mm(PS[bank + t][:, :], lambda p: hT[p][:, k, t * P:(t + 1) * P],
                                           lambda p: w_part[p][:, s, :], k == 0, k == KD - 1)
                        last.then_inc(half_used, 1)

            def columns(o, n, it=0, step=0, fresh=None):
                for hf in range(2):
                    s = half(n, hf, it, step)
                    for kk in range(KD // 2):
                        k = KD // 2 * hf + kk
                        await_h(fresh, k)
                        last = part_mm(o, lambda p: w_part[p][:, s, kk * P:(kk + 1) * P],
                                       lambda p: hT[p][:, k, :], k == 0, k == KD - 1)
                    last.then_inc(half_used, 1)

            def rows_of(n, src, first, last_one, it=0, step=0):
                for hf in range(2):
                    s = half(n, hf, it, step)
                    for t in range(NT):
                        last = part_mm(PS[4 + 2 * t + hf][:, :], lambda p: src(p, t),
                                       lambda p: w_part[p][:, s, :], first, last_one)
                    last.then_inc(half_used, 1)

            def by_channel(name, bank, fresh=None):
                columns(PS[bank][:, 0:T], at[name], fresh=fresh)

            def out_row(name, k, tiles):
                rows_of(at[(name, k)], lambda p, t: hT[p][:, k % KD, t * P:(t + 1) * P], k == 0, k == tiles - 1)

            def spread_row(bank, h, heads):
                w = pick[0:heads, h:h + 1].to_broadcast([heads, P])
                mm(bank[:, :], w, row[0][0:heads, :], True, False)
                return mm(bank[:, :], w, row[1][0:heads, :], False, True)

            def gate_logits(o, wg, k, t):
                mm(o, hT[0][:, k, t * P:(t + 1) * P].bitcast(F32), wg[:, k, :], k == 0, False)
                return mm(o, hT[1][:, k, t * P:(t + 1) * P].bitcast(F32), wg[:, k, :], False, k == KD - 1)

            def gdn():
                for hf in range(2):
                    by_token(("gz", hf), 4 + 2 * hf, None if hf else 0)
                pe.wait_ge(small_loaded, 16 * N_SMALL)
                for t in range(NT):
                    for k in range(KD):
                        last = gate_logits(PS[2][:, t * 32:(t + 1) * 32], g_wg, k, t)
                last.then_inc(SEM["g_gate_ps"], 1)

                def turn_tok(gi):
                    pe.wait_ge(SEM["g_silued"], 2 * gi + 2)
                    if gi == 0:
                        pe.wait_ge(SEM["g_zs"], 4)
                    if gi >= 4:
                        pe.wait_ge(SEM["g_toksb"], gi - 3)
                    for t in range(NT):
                        for e in range(2):
                            last = pe.transpose(PS[4 + gi % 4][:, (2 * t + e) * P:(2 * t + e + 1) * P],
                                                g_feat[:, 2 * gi + e, t * P:(t + 1) * P], ident)
                    last.then_inc(SEM["g_tokps"], 1)

                for m in range(GC):
                    if m >= 2:
                        pe.wait_ge(SEM["g_padded"], m - 1)
                    by_channel(("gq", m), m % 2)
                    if m >= 3 and m % 2:
                        turn_tok((m - 3) // 2)
                pe.wait_ge(SEM["g_gg"], 1)
                for c in range(NT):
                    mm(PS[3][:, c * 16:c * 16 + 8], upper, g_g[:, c, 0:8])
                    mm(PS[3][:, c * 16 + 8:c * 16 + 16], lower, g_g[:, c, 8:16])
                    mm(PS[3][:, 32 + c * 16:48 + c * 16], ones, g_g[:, c, :])
                    mm(PS[2][0:GH, c * P:(c + 1) * P], g_g[:, c, 0:8], upper)
                    last = mm(PS[2][0:GH, T + c * P:T + (c + 1) * P], g_g[:, c, 8:16], lower)
                last.then_inc(SEM["g_cum"], 1)
                turn_tok(11)
                for gi in range(GH):
                    pe.wait_ge(SEM["g_qk"], gi // 2 + 1)
                    if gi >= 4:
                        pe.wait_ge(SEM["g_backsb"], gi - 3)
                    for e in range(2):
                        for t in range(NT):
                            last = pe.transpose(PS[4 + gi % 4][:, (2 * e + t) * P:(2 * e + t + 1) * P],
                                                g_tok[:, t, 2 * gi + e, :], ident)
                    last.then_inc(SEM["g_backps"], 1)
                pe.wait_ge(picks, 1)
                pe.wait_ge(row_lo, 1)
                pe.wait_ge(SEM["g_padded"], GC)
                for h in range(GH):
                    if h >= 2:
                        pe.wait_ge(SEM["g_dexp"], h - 1)
                    spread_row(PS[h % 2], h, GH).then_inc(SEM["g_bc"], 1)
                    if h == 0:
                        pe.wait_ge(SEM["g_cumsb"], 1)
                        pe.wait_ge(SEM["g_backsb"], GH)
                    if h >= 2:
                        pe.wait_ge(SEM["g_QE"], h - 1)
                    for c in range(NT):
                        kT = g_feat[:, GH + h, c * P:(c + 1) * P]
                        mm(PS[2 + h % 2][:, c * P:(c + 1) * P], kT, kT)
                        last = mm(PS[2 + h % 2][:, T + c * P:T + (c + 1) * P], kT, g_feat[:, h, c * P:(c + 1) * P])
                    last.then_inc(SEM["g_kq"], 1)

                def y_step(n):
                    b = n % GB
                    pe.wait_ge(SEM["g_mask"], n + 1)
                    if n == GB:
                        pe.wait_ge(SEM["g_dexp"], GH)
                    if n - 2 >= GB:
                        pe.wait_ge(SEM["g_Y"], n - 2 - GB + 1)
                    pe.wait_ge(SEM["g_T"], n - GB + 1)
                    for e in range(4):
                        last = mm(PS[n % 2][:, e * P:(e + 1) * P], g_mask[:, 4 * (n % 2) + e, :], g_T[:, 4 * b + e, :])
                    last.then_inc(SEM["g_Yps"], 1)

                def z_step(n):
                    level, b = divmod(n, GB)
                    pe.wait_ge(SEM["g_Y"], n - GB + 1)
                    if n - 2 >= GB:
                        pe.wait_ge(SEM["g_TT"], n - 2 + 1)
                    for e in range(4):
                        s = 4 * b + e
                        last = mm(PS[6 + n % 2][:, e * P:(e + 1) * P], g_Y[:, s, :], g_TT[:, s, :])
                    last.then_inc(SEM["g_Zps"], 1)

                def turn_T(n):
                    b = n % GB
                    pe.wait_ge(SEM["g_TT"], n + 1)
                    if n >= 2:
                        pe.wait_ge(SEM["g_T"], n - 2 + 1)
                    for e in range(4):
                        last = pe.transpose(PS[4 + n % 2][:, e * P:(e + 1) * P], g_TT[:, 4 * b + e, :], ident)
                    last.then_inc(SEM["g_Tps"], 1)

                for n in range(LEVELS * GB + 3):
                    if GB <= n < LEVELS * GB:
                        y_step(n)
                    if GB <= n - 1 < LEVELS * GB:
                        z_step(n - 1)
                    if 0 <= n - 3 < (LEVELS - 1) * GB:
                        turn_T(n - 3)

                pe.wait_ge(SEM["g_TT"], LEVELS * GB)
                for q4 in range(4):
                    d, h0 = q4 // 2, 4 * (q4 % 2)
                    for e in range(4):
                        last = mm(PS[q4][:, e * P:(e + 1) * P], g_TT[:, system(d, h0 + e, d), :],
                                  g_tok[:, d, 2 * GH + h0 + e, :])
                    last.then_inc(SEM["g_U0"], 1)
                for q4 in range(4):
                    d, h0 = q4 // 2, 4 * (q4 % 2)
                    pe.wait_ge(SEM["g_vn0"], q4 + 1)
                    pe.wait_ge(SEM["g_kS"], q4 + 1)
                    for e in range(4):
                        last = mm(PS[4 + q4][:, e * P:(e + 1) * P], g_kS[:, d * GH + h0 + e, :],
                                  g_vn[:, system(d, h0 + e, d), :])
                    last.then_inc(SEM["g_S1ps"], 1)
                for q4 in range(4):
                    d, h0 = q4 // 2, 4 * (q4 % 2)
                    pe.wait_ge(SEM["g_S1"], q4 + 1)
                    c = 1 - d
                    for e in range(4):
                        S = g_S[:, d * GH + h0 + e, :]
                        mm(PS[q4][:, e * P:(e + 1) * P], g_feat[:, GH + h0 + e, c * P:(c + 1) * P], S)
                        last = mm(PS[4 + q4][:, e * P:(e + 1) * P], g_feat[:, h0 + e, c * P:(c + 1) * P], S)
                    last.then_inc(SEM["g_RQ"], 1)
                for q4 in range(4):
                    d, h0 = q4 // 2, 4 * (q4 % 2)
                    pe.wait_ge(SEM["g_v1"], q4 + 1)
                    for e in range(4):
                        last = mm(PS[q4][:, e * P:(e + 1) * P], g_TT[:, system(d, h0 + e, 1 - d), :],
                                  g_vp[:, d * GH + h0 + e, :])
                    last.then_inc(SEM["g_U1"], 1)
                pe.wait_ge(SEM["g_int"], 4)
                pe.wait_ge(SEM["g_vn1"], 4)
                pe.wait_ge(SEM["g_P"], 2 * NT)
                for c in range(NT):
                    for hg in range(2):
                        for e in range(4):
                            o = PS[4 + 2 * c + hg][:, e * P:(e + 1) * P]
                            f, r = system(0, 4 * hg + e, c), system(1, 4 * hg + e, c)
                            mm(o, g_tok[:, c, 4 * hg + e, :], g_vn[:, f, :], True, False)
                            last = mm(o, g_PTb[:, 4 * hg + e, c, :], g_vn[:, r, :], False, True)
                        last.then_inc(SEM["g_Ops"], 1)
                for t in range(NT):
                    pe.wait_ge(o_ready, t + 1)
                    for b in range(4):
                        for kk in range(2):
                            last = pe.transpose(PS[b][:, (2 * kk + t) * P:(2 * kk + t + 1) * P],
                                                g_o[:, t * GH + 2 * b + kk, :], ident)
                        if t == NT - 1:
                            last.then_inc(oT_psum, 1)
                pe.wait_ge(oT_lo, 4)
                for k in range(GH):
                    out_row("go", k, GH)

            def ssd():
                await_h(2, KD - 1)
                pe.wait_ge(s_wg_loaded, 16)
                for t in range(NT):
                    for k in range(KD):
                        last = gate_logits(PS[2][:, t * 64:(t + 1) * 64], s_wg, k, t)
                last.then_inc(SEM["s_gate_ps"], 1)

                def turn_tok(gi):
                    pe.wait_ge(SEM["s_silued"], 2 * gi + 2)
                    if gi >= 4:
                        pe.wait_ge(SEM["s_toksb"], gi - 3)
                    for t in range(NT):
                        for e in range(2):
                            last = pe.transpose(PS[4 + gi % 4][:, (2 * t + e) * P:(2 * t + e + 1) * P],
                                                s_feat[:, 2 * gi + e, t * P:(t + 1) * P], ident)
                    last.then_inc(SEM["s_tokps"], 1)

                for m in range(SC):
                    if m >= 2:
                        pe.wait_ge(SEM["s_padded"], m - 1)
                    by_channel(("sx", m), m % 2)
                    if m >= 3 and m % 2 and (m - 3) // 2 < SX // 2:
                        turn_tok((m - 3) // 2)
                pe.wait_ge(SEM["s_da"], 1)
                f, r = slice(0, SH), slice(SH, 2 * SH)
                mm(PS[3][:, 0:32], upper, s_da[:, 0, f])
                mm(PS[3][:, 64:96], ones, s_da[:, 0, f], True, False)
                mm(PS[3][:, 64:96], upper, s_da[:, 1, f], False, True)
                mm(PS[3][:, 96:128], lower, s_da[:, 1, r])
                mm(PS[3][:, 32:64], ones, s_da[:, 1, r], True, False)
                mm(PS[3][:, 32:64], lower, s_da[:, 0, r], False, True)
                mm(PS[2][0:SH, 0:P], s_da[:, 0, f], upper)
                mm(PS[2][0:SH, P:2 * P], s_da[:, 0, f], ones, True, False)
                mm(PS[2][0:SH, P:2 * P], s_da[:, 1, f], upper, False, True)
                mm(PS[2][0:SH, 2 * P:3 * P], s_da[:, 1, r], ones, True, False)
                mm(PS[2][0:SH, 2 * P:3 * P], s_da[:, 0, r], lower, False, True)
                mm(PS[2][0:SH, 3 * P:4 * P], s_da[:, 1, r], lower).then_inc(SEM["s_cum"], 1)
                pe.wait_ge(SEM["s_silued"], SC)
                pe.wait_ge(SEM["s_toksb"], SX // 2)
                for g in range(SG):
                    if g >= 2:
                        pe.wait_ge(SEM["s_cb"], g - 1)
                    for st in range(NT):
                        last = mm(PS[6 + g % 2][:, st * T:(st + 1) * T], s_feat[:, SX + g, st * P:(st + 1) * P],
                                  s_feat[:, SX + SG + g, :])
                    last.then_inc(SEM["s_cbps"], 1)
                pe.wait_ge(picks, 2)
                pe.wait_ge(row_lo, 2)
                pe.wait_ge(SEM["s_nac"], 1)
                pe.wait_ge(SEM["s_padded"], SC)

                def spread(h):
                    if h >= 2:
                        pe.wait_ge(SEM["s_e"], h - 1)
                    spread_row(PS[h % 2], h, SH).then_inc(SEM["s_bc"], 1)

                def y_head(h):
                    g, b = h // SR, 2 + 2 * (h // SR % 2)
                    if h % SR == 0 and g >= 2:
                        pe.wait_ge(SEM["s_y"], 2 * (g - 1))
                    pe.wait_ge(SEM["s_m"], h + 1)
                    o = slice(h % SR * SP_, (h % SR + 1) * SP_)
                    x0, x1 = (s_tok[:, t, h * SP_:(h + 1) * SP_] for t in range(NT))
                    mm(PS[b][:, o], s_M[:, h % 2, 0, 0, :], x0, True, False)
                    mm(PS[b][:, o], s_M[:, h % 2, 1, 2, :], x1, False, True)
                    mm(PS[b + 1][:, o], s_M[:, h % 2, 0, 2, :], x0, True, False)
                    mm(PS[b + 1][:, o], s_M[:, h % 2, 1, 0, :], x1, False, True).then_inc(SEM["s_yps"], 1)

                def gate_half(h):
                    nb, q, kk = h // SR, h // 2 % (KD // 2), h % 2
                    k = 2 * q + kk
                    if k == 0:
                        pe.wait_ge(SEM["s_zs" if nb else "s_cb"], 2 * nb if nb else SG)
                    s = half(at[("sz", nb, q)], kk)
                    for t in range(NT):
                        last = part_mm(PS[6 + t][:, :], lambda p: hT[p][:, k, t * P:(t + 1) * P],
                                       lambda p: w_part[p][:, s, :], k == 0, k == KD - 1)
                    last.then_inc(half_used, 1)

                spread(0)
                for h in range(SH):
                    gate_half(h)
                    if h + 1 < SH:
                        spread(h + 1)
                    if h >= 2:
                        y_head(h - 2)
                y_head(SH - 2)
                y_head(SH - 1)
                def turn_y(gi):
                    pe.wait_ge(o_ready, 2 + NT * (gi // 2 + 1))
                    if gi >= 4:
                        pe.wait_ge(oT_lo, 4 + gi - 3)
                    for kk in range(2):
                        for t in range(NT):
                            k = 2 * gi + kk
                            last = pe.transpose(PS[gi % 4][:, (2 * kk + t) * P:(2 * kk + t + 1) * P],
                                                s_y[:, t, k * P:(k + 1) * P], ident)
                    last.then_inc(oT_psum, 1)

                for gi in range(4):
                    turn_y(gi)
                for k in range(SX):
                    if k % 2 == 0:
                        pe.wait_ge(oT_lo, 4 + k // 2 + 1)
                    out_row("so", k, SX)
                    if k % 2 and k // 2 + 4 < SX // 2:
                        turn_y(k // 2 + 4)

            def route(lyr):
                for m in range(HP):
                    if m >= 2:
                        pe.wait_ge(SEM["p_q"], HP * lyr + m - 1)
                    by_channel(("pq", lyr, m), 4 + m % 2, None if m else 2 * lyr + 1)
                pe.wait_ge(SEM["p_q"], HP * (lyr + 1))
                pe.wait_ge(keys_loaded, 16 * (lyr + 1))
                for g in range(8):
                    t, first_head = g // 2 % 2, 8 * (g // 4) + 4 * (g % 2)
                    if g >= 4:
                        pe.wait_ge(SEM["p_s"], 8 * lyr + g - 3)
                    for e in range(4):
                        hp = first_head + e
                        last = mm(PS[2 + g % 4][:, e * P:(e + 1) * P], p_qT[:, hp, t * P:(t + 1) * P], p_kT[:, hp, :])
                    last.then_inc(SEM["p_sps"], 1)

            def hidden(lyr, i, n, it=0, tiles=0):
                if tiles or i >= 2:
                    pe.wait_ge(SEM["p_gelu"], it * tiles + (P * lyr + i - 1))
                columns(PS[i % 2][:, 0:T], n, it, 8)

            def values(lyr, i, n, it=0, tiles=0, first=False, last_one=False):
                pe.wait_ge(SEM["p_ag"], it * tiles + (P * lyr + i + 1))
                rows_of(n, lambda p, t: p_ag[p][:, i % 2, t * P:(t + 1) * P], first, last_one, it, 8)

            def experts(lyr):
                n0 = tables[lyr]
                for i in range(4):
                    hidden(lyr, i, n0 + i)
                with pe.Fori(0, EARLY // 4 - 1) as it:
                    for i in range(4, 8):
                        hidden(lyr, i, n0 + i, it, 4)
                pe.wait_ge(SEM["p_key"], lyr + 1)
                for e in range(2):
                    for t in range(NT):
                        v = flat(p_key[:, e, t * PH:(t + 1) * PH, :], "h k")
                        pe.transpose(PS[6][:, e * T + t * P:e * T + (t + 1) * P], v, ident)
                for t in range(NT):
                    last = pe.transpose(PS[7][:, t * P:(t + 1) * P], flat(p_gate[:, t * PH:(t + 1) * PH, :], "h k"), ident)
                last.then_inc(SEM["p_Tps"], 1)
                pe.wait_ge(SEM["p_gelu"], P * lyr + EARLY)

                def tokens16(it, first=False):
                    for u in range(16):
                        if not first and u % 4 == 0:
                            pe.wait_ge(SEM["p_mul"], it * 4 + (64 * lyr + u // 4 - 3))
                        if u % 4 == 0:
                            pe.wait_ge(SEM["p_hotB"], it * 4 + (64 * lyr + u // 4 + 1))
                        made = 2 * (u // 4) + u % 2 + 1
                        pe.wait_ge(SEM["p_hot" if u % 4 < 2 else "p_hotS"], it * 8 + (T // 2 * lyr + made))
                        mm(PS[u // 4][:, u % 4 * P:(u % 4 + 1) * P], p_B[u // 4 % 2][:, u % 4, :].bitcast(F32), p_A[:, u % 8, :]
                           ).then_inc(SEM["p_mapps"], 1)

                tokens16(0, True)
                with pe.Fori(1, T // 16) as it:
                    tokens16(it)
                n1, n2 = n0 + EARLY, n0 + 2 * EARLY
                for i in range(4):
                    values(lyr, i, n1 + i, first=i == 0)
                with pe.Fori(0, EARLY // 4 - 1) as it:
                    for i in range(4, 8):
                        values(lyr, i, n1 + i, it, 4)
                i = EARLY
                pe.wait_ge(SEM["p_mul"], 64 * (lyr + 1))
                hidden(lyr, i, n2)
                hidden(lyr, i + 1, n2 + 1)
                values(lyr, i, n2 + 2)
                with pe.Fori(0, (P - EARLY) // 2 - 1) as it:
                    hidden(lyr, i + 2, n2 + 3, it, 2)
                    values(lyr, i + 1, n2 + 4, it, 2)
                    hidden(lyr, i + 3, n2 + 5, it, 2)
                    values(lyr, i + 2, n2 + 6, it, 2)
                values(lyr, P - 1, n0 + 2 * P - 1, last_one=True)

            pe.wait_ge(const_loaded, 32)
            turn_h(0)
            gdn()
            turn_h(1)
            route(0)
            experts(0)
            turn_h(2)
            ssd()
            turn_h(3)
            route(1)
            experts(1)

        @block.vector
        def _(dve):
            chain = [0]

            def link(ins):
                chain[0] += 1
                ins.then_inc(dve_chain, 1)
                dve.wait_ge(dve_chain, chain[0])

            def wide(v, n):
                return v.rearrange("p (a o) -> p a o", o=1).to_broadcast([v.shape[0], v.shape[1], n])

            def rows(v, n):
                return v.rearrange("p (o c) -> p o c", o=1).to_broadcast([v.shape[0], n, v.shape[1]])

            def polish(ms, root, inv, new, rstd, signal=None):
                link(dve.reciprocal(inv, root))
                link(dve.tensor_tensor(new, inv, inv, ALU.mult))
                link(dve.tensor_tensor(new, new, ms, ALU.mult))
                link(dve.tensor_scalar(new, new, -0.5, 1.5, ALU.mult, ALU.add))
                link(dve.tensor_tensor(rstd, inv, new, ALU.mult))

            def norm_stats(i):
                dve.wait_ge(n_sq, 2 * (i + 1))
                dve.tensor_scalar(n_ms, n_ss, 1.0 / D, EPS, ALU.mult, ALU.add).then_inc(n_mean, 1)
                dve.wait_ge(n_rooted, i + 1)
                polish(n_ms, n_root, n_inv, n_new, n_rstd)

            def norm(i):
                norm_stats(i)
                for t in range(NT):
                    dve.tensor_scalar(h_tok[:, t, :], x_sb[:, t, :], n_rstd[:, t:t + 1], None, ALU.mult).then_inc(n_h, 1)
                for k in range(KD):
                    if k % 2 == 0:
                        dve.wait_ge(n_hT, KD * i + k + 2)
                    dve.scalar_tensor_tensor(hT[1][:, k, :], PS[k // 2][:, (k % 2) * T:(k % 2 + 1) * T], norm_w[:, i, k:k + 1],
                                             hT[0][:, k, :].bitcast(F32), ALU.mult, ALU.subtract).then_inc(n_hTlo, 1)

            def rest_of_rows(i, heads):
                dve.wait_ge(row_hi, i + 1)
                dve.tensor_tensor(row[1][0:heads, :], PS[2][0:heads, :], row[0][0:heads, :].bitcast(F32),
                                  ALU.subtract).then_inc(row_lo, 1)

            def rest_of_oT(base, gi):
                dve.wait_ge(oT_ready, base + gi + 1)
                b = gi % 4
                dve.tensor_tensor(hT[1][:, 2 * b:2 * b + 2, :], PS[b][:, :].rearrange("p (e t) -> p e t", e=2),
                                  hT[0][:, 2 * b:2 * b + 2, :].bitcast(F32), ALU.subtract).then_inc(oT_lo, 1)

            def rest_of_unit(n, it=0, step=0):
                for hf in range(2):
                    rest_of_half(n, hf, it, step)

            def rest_of_half(n, hf, it=0, step=0):
                dve.wait_ge(hi_ready, it * step + (2 * n + hf + 1))
                s = (2 * n + hf) % SPLIT
                dve.tensor_tensor(w_part[1][:, s, :], ring[:, n % RING, hf * 512:(hf + 1) * 512],
                                  w_part[0][:, s, :].bitcast(F32), ALU.subtract).then_inc(lo_ready, 1)

            def residual(last_unit):
                dve.wait_ge(half_used, 2 * (last_unit + 1))
                for t in range(NT):
                    for hf in range(2):
                        v = x_sb[:, t, hf * 512:(hf + 1) * 512]
                        dve.tensor_tensor(v, PS[4 + 2 * t + hf][:, :], v, ALU.add).then_inc(x_added, 1)

            def conv(m, pad, acc, taps, padded, conved, silued):
                dve.wait_ge(padded, m + 1)
                if m >= 4:
                    dve.wait_ge(silued, m - 3)
                o = acc[:, m % 4, :]
                link(dve.tensor_scalar(o, pad[:, m % 4, 0:T], taps[:, m, 0:1], None, ALU.mult))
                for j in range(1, TAPS):
                    ins = dve.scalar_tensor_tensor(o, pad[:, m % 4, j:j + T], taps[:, m, j:j + 1], o, ALU.mult, ALU.add)
                    if j < TAPS - 1:
                        link(ins)
                    else:
                        ins.then_inc(conved, 1)

            def gdn():
                dve.memset(flat(g_pad, "s w"), 0.0).then_inc(SEM["g_pads"], 1)
                dve.wait_ge(SEM["g_gate_ps"], 1)
                dve.wait_ge(small_loaded, 16 * N_SMALL)
                logits = PS[2][:, 0:64].rearrange("p (t c) -> p t c", t=NT)
                link(dve.tensor_tensor(g_z, logits[:, :, 0:16], rows(g_bias, NT), ALU.add))
                link(dve.tensor_scalar(g_mx, g_z, 0.0, None, ALU.max))
                dve.scalar_tensor_tensor(g_ab, g_mx, -2.0, g_z, ALU.mult, ALU.add).then_inc(SEM["g_gateb"], 1)
                dve.wait_ge(SEM["g_gact"], 1)
                link(dve.tensor_tensor(g_z, g_mx, g_ab, ALU.add))
                dve.scalar_tensor_tensor(g_g, g_z, -1.0, rows(g_nega, NT), ALU.mult, ALU.mult).then_inc(SEM["g_gg"], 1)

                def tok_copy(gi):
                    dve.wait_ge(SEM["g_tokps"], gi + 1)
                    dve.tensor_copy(g_tok[:, :, 2 * gi:2 * gi + 2, :],
                                    PS[4 + gi % 4][:, :].rearrange("p (t e d) -> p t e d", t=NT, e=2)
                                    ).then_inc(SEM["g_toksb"], 1)

                for m in range(GC):
                    conv(m, g_pad, g_acc, g_conv, SEM["g_padded"], SEM["g_conved"], SEM["g_silued"])
                    if m >= 5 and m % 2:
                        tok_copy((m - 5) // 2)
                dve.wait_ge(SEM["g_cum"], 1)
                link(dve.tensor_copy(flat(g_gc, "t c"), PS[3][:, 0:32]))
                dve.tensor_tensor(flat(g_gt, "t c"), PS[3][:, 32:64], flat(g_gc, "t c"), ALU.subtract).then_inc(SEM["g_cumsb"], 1)
                rest_of_rows(0, GH)
                tok_copy(10)
                tok_copy(11)
                dve.wait_ge(SEM["g_sqsum"], GH)
                dve.tensor_scalar(g_ms, g_ss, 1.0, EPS, ALU.mult, ALU.add).then_inc(SEM["g_mean"], 1)
                dve.wait_ge(SEM["g_root"], 1)
                polish(g_ms, g_root, g_inv, g_new, g_rstd)
                dve.wait_ge(SEM["g_toksb"], 12)
                for j in range(4):
                    v = g_tok[:, :, 4 * j:4 * j + 4, :]
                    r = g_rstd[:, :, 4 * j:4 * j + 4].rearrange("p t (c o) -> p t c o", o=1).to_broadcast([P, NT, 4, P])
                    dve.tensor_tensor(v, v, r, ALU.mult).then_inc(SEM["g_qk"], 1)
                dve.wait_ge(SEM["g_exps"], 2)
                link(dve.tensor_scalar(g_egq, g_eg, P ** -0.5, None, ALU.mult))

                def decay(h):
                    dve.wait_ge(SEM["g_bc"], h + 1)
                    tmp = g_tmp[:, 2 * (h % 2):2 * (h % 2) + 2, :]
                    for c in range(NT):
                        lo = slice(c * P, (c + 1) * P)
                        dve.tensor_scalar(g_E[:, h, lo], PS[h % 2][:, lo], g_gc[:, c, h:h + 1], 0.0, ALU.subtract, ALU.min)
                        last = dve.tensor_scalar(tmp[:, c, :], PS[h % 2][:, T + c * P:T + (c + 1) * P],
                                                 g_gc[:, c, GH + h:GH + h + 1], 0.0, ALU.subtract, ALU.min)
                    last.then_inc(SEM["g_dexp"], 1)
                    dve.wait_ge(SEM["g_dexp"], h + 1)
                    dve.tensor_tensor(g_E[:, h, :], g_E[:, h, :], flat(tmp, "c d"), ALU.add).then_inc(SEM["g_logE"], 1)

                def system_rows(h):
                    dve.wait_ge(SEM["g_kq"], h + 1)
                    dve.wait_ge(SEM["g_E"], h + 1)
                    bank = PS[2 + h % 2]
                    for d in range(2):
                        for c in range(NT):
                            last = dve.scalar_tensor_tensor(
                                g_AT[:, system(d, h, c), :], bank[:, c * P:(c + 1) * P],
                                g_beta[:, c, d * GH + h:d * GH + h + 1], g_E[:, h, c * P:(c + 1) * P], ALU.mult, ALU.mult)
                    last.then_inc(SEM["g_A"], 1)
                    dve.wait_ge(SEM["g_A"], h + 1)
                    dve.scalar_tensor_tensor(g_E[:, h, :], bank[:, T:2 * T], P ** -0.5, g_E[:, h, :], ALU.mult,
                                             ALU.mult).then_inc(SEM["g_QE"], 1)

                dve.wait_ge(SEM["g_betas"], 1)
                for h in range(GH):
                    decay(h)
                    if h:
                        system_rows(h - 1)
                system_rows(GH - 1)

                for n in range(LEVELS * GB):
                    level, b = divmod(n, GB)
                    TTb = g_TT[:, 4 * b:4 * b + 4, :]

                    def bank(i):
                        return PS[i][:, :].rearrange("p (s d) -> p s d", s=4)

                    if level == 0:
                        dve.wait_ge(SEM["g_mask"], n + 1)
                        dve.tensor_tensor(TTb, rows(ident, 4), g_mask[:, 4 * (n % 2):4 * (n % 2) + 4, :],
                                          ALU.subtract).then_inc(SEM["g_TT"], 1)
                        continue
                    dve.wait_ge(SEM["g_Zps"], n - GB + 1)
                    dve.tensor_tensor(TTb, TTb, bank(6 + n % 2), ALU.subtract).then_inc(SEM["g_TT"], 1)

                def quad(v, q4, c):
                    d, h0 = q4 // 2, 4 * (q4 % 2)
                    return wide(v[:, c, d * GH + h0:d * GH + h0 + 4], P)

                def bank(i):
                    return PS[i][:, :].rearrange("p (s d) -> p s d", s=4)

                def vn(q4, c):
                    s = system(q4 // 2, 4 * (q4 % 2), c)
                    return g_vn[:, s:s + 7:2, :]

                for q4 in range(4):
                    dve.wait_ge(SEM["g_U0"], q4 + 1)
                    dve.tensor_tensor(vn(q4, q4 // 2), bank(q4), quad(g_beta, q4, q4 // 2), ALU.mult).then_inc(SEM["g_vn0"], 1)
                for q4 in range(4):
                    d, h0 = q4 // 2, 4 * (q4 % 2)
                    c = 1 - d
                    vp = g_vp[:, 4 * q4:4 * q4 + 4, :]
                    dve.wait_ge(SEM["g_RQ"], q4 + 1)
                    link(dve.tensor_tensor(vp, bank(q4), quad(g_eg, q4, c), ALU.mult))
                    dve.tensor_tensor(vp, g_tok[:, c, 2 * GH + h0:2 * GH + h0 + 4, :], vp, ALU.subtract).then_inc(SEM["g_v1"], 1)
                for q4 in range(4):
                    dve.tensor_tensor(g_inter[:, 4 * q4:4 * q4 + 4, :], bank(4 + q4), quad(g_egq, q4, 1 - q4 // 2),
                                      ALU.mult).then_inc(SEM["g_int"], 1)
                for q4 in range(4):
                    dve.wait_ge(SEM["g_U1"], q4 + 1)
                    dve.tensor_tensor(vn(q4, 1 - q4 // 2), bank(q4), quad(g_beta, q4, 1 - q4 // 2), ALU.mult).then_inc(SEM["g_vn1"], 1)
                dve.wait_ge(SEM["g_int"], 4)
                ss, ms, root, inv, new, rstd = (v[:, 0, :] for v in (g_ss, g_ms, g_root, g_inv, g_new, g_rstd))
                for t in range(NT):
                    for b in (2 * t, 2 * t + 1):
                        dve.wait_ge(SEM["g_Ops"], b + 1)
                        q = (1 - t) * GH + 4 * (b % 2)
                        dve.tensor_tensor(g_o[:, 4 * b:4 * b + 4, :], bank(4 + b), g_inter[:, q:q + 4, :], ALU.add).then_inc(SEM["g_O"], 1)
                    s = slice(t * GH, (t + 1) * GH)
                    dve.wait_ge(SEM["g_osum"], t + 1)
                    dve.tensor_scalar(ms[:, s], ss[:, s], 1.0 / P, EPS, ALU.mult, ALU.add).then_inc(SEM["g_omean"], 1)
                    dve.wait_ge(SEM["g_oroot"], t + 1)
                    polish(ms[:, s], root[:, s], inv[:, s], new[:, s], rstd[:, s])
                    link(dve.tensor_tensor(g_o[:, s, :], g_o[:, s, :], wide(rstd[:, s], P), ALU.mult))
                    if t == 0:
                        dve.wait_ge(SEM["g_gz"], 2)
                    v = flat(g_o[:, s, :], "s d")
                    dve.tensor_tensor(v, v, g_siluz[:, t, :], ALU.mult).then_inc(o_ready, 1)
                for gi in range(4):
                    rest_of_oT(0, gi)
                residual(at[("go", GH - 1)])

            def ssd():
                dve.memset(flat(s_pad, "s w"), 0.0).then_inc(SEM["s_pads"], 1)
                dve.wait_ge(SEM["s_gate_ps"], 1)
                logits = PS[2][:, 0:128].rearrange("p (t c) -> p t c", t=NT)
                link(dve.tensor_tensor(s_z, logits, rows(s_bias, NT), ALU.add))
                link(dve.tensor_scalar(s_mx, s_z, 0.0, None, ALU.max))
                dve.scalar_tensor_tensor(s_ab, s_mx, -2.0, s_z, ALU.mult, ALU.add).then_inc(SEM["s_gateb"], 1)
                dve.wait_ge(SEM["s_gact"], 1)
                link(dve.tensor_tensor(s_dt, s_mx, s_ab, ALU.add))
                dve.scalar_tensor_tensor(s_da, s_dt, -1.0, rows(s_nega, NT), ALU.mult, ALU.mult).then_inc(SEM["s_da"], 1)

                def tok_copy(gi):
                    dve.wait_ge(SEM["s_tokps"], gi + 1)
                    dve.tensor_copy(s_tok[:, :, gi * T:(gi + 1) * T],
                                    PS[4 + gi % 4][:, :].rearrange("p (t w) -> p t w", t=NT)).then_inc(SEM["s_toksb"], 1)

                for m in range(SC):
                    conv(m, s_pad, s_acc, s_conv, SEM["s_padded"], SEM["s_conved"], SEM["s_silued"])
                    if m >= 5 and m % 2 and (m - 5) // 2 < SX // 2:
                        tok_copy((m - 5) // 2)
                dve.wait_ge(SEM["s_cum"], 1)
                link(dve.tensor_copy(flat(s_ac, "t c"), PS[3][:, 0:128]))
                dve.tensor_scalar(s_nac, s_ac, -1.0, None, ALU.mult).then_inc(SEM["s_nac"], 1)
                rest_of_rows(1, SH)
                for g in range(SG):
                    dve.wait_ge(SEM["s_cbps"], g + 1)
                    for st in range(NT):
                        v = PS[6 + g % 2][:, st * T + st * P:st * T + (st + 1) * P]
                        w = PS[6 + g % 2][:, st * T + (1 - st) * P:st * T + (2 - st) * P]
                        dve.tensor_tensor(s_CB[:, g, st, 0, :], v, upper, ALU.mult)
                        dve.tensor_tensor(s_CB[:, g, st, 1, :], v, lower, ALU.mult)
                        last = dve.tensor_copy(s_CB[:, g, st, 2, :], w)
                    last.then_inc(SEM["s_cb"], 1)
                dve.wait_ge(SEM["s_cb"], SG)

                def decay(h):
                    dve.wait_ge(SEM["s_bc"], h + 1)
                    if h >= 2:
                        dve.wait_ge(SEM["s_mv"], h - 1)
                    for st in range(NT):
                        for d in range(2):
                            last = dve.tensor_scalar(s_E[:, h % 2, st, d, :], PS[h % 2][:, d * T + st * P:d * T + (st + 1) * P],
                                                     s_ac[:, st, d * SH + h:d * SH + h + 1], 0.0, ALU.subtract, ALU.min)
                    last.then_inc(SEM["s_d"], 1)

                def weigh(h):
                    g = h // SR
                    dve.wait_ge(SEM["s_e"], h + 1)
                    if h >= 2:
                        dve.wait_ge(SEM["s_yps"], h - 1)
                    for st in range(NT):
                        for d in range(2):
                            last = dve.scalar_tensor_tensor(
                                s_M[:, h % 2, st, d, :], s_CB[:, g, st, d, :], s_dt[:, st, d * SH + h:d * SH + h + 1],
                                s_E[:, h % 2, st, d, :], ALU.mult, ALU.mult)
                    last.then_inc(SEM["s_mv"], 1)

                def group_out(g):
                    for lt in range(NT):
                        dve.wait_ge(SEM["s_yps"], SR * (g + 1))
                        v = slice(g * 512, (g + 1) * 512)
                        if lt == 0:
                            dve.wait_ge(SEM["s_skip"], SR * (g + 1))
                        dve.tensor_tensor(s_y[:, lt, v], PS[2 + 2 * (g % 2) + lt][:, :], s_skip[:, lt, v], ALU.add).then_inc(SEM["s_y"], 1)

                def gate_rest(h):
                    rest_of_half(at[("sz", 0, 0)] + h // 2 + 2, h % 2)

                dve.wait_ge(lo_ready, 2 * at[("sz", 0, 2)])
                for h in range(SH):
                    decay(h)
                    if h:
                        gate_rest(h - 1)
                        weigh(h - 1)
                    if h > SR and h % SR == 3:
                        group_out(h // SR - 1)
                weigh(SH - 1)
                gate_rest(SH - 1)
                group_out(SG - 1)
                for t in range(NT):
                    v = s_y[:, t, (SG - 1) * 512:]
                    dve.wait_ge(SEM["s_y"], NT * (SG - 1) + t + 1)
                    dve.wait_ge(SEM["s_zs"], NT * (SG - 1) + t + 1)
                    dve.tensor_tensor(v, v, s_siluz[:, t, (SG - 1) * 512:], ALU.mult).then_inc(SEM["s_yg"], 1)
                dve.wait_ge(SEM["s_ss"], NT * SG)
                dve.tensor_scalar(s_ms, s_ss, 1.0 / 512, EPS, ALU.mult, ALU.add).then_inc(SEM["s_mean"], 1)
                dve.wait_ge(SEM["s_root"], 1)
                polish(s_ms, s_root, s_inv, s_new, s_rstd)
                dve.wait_ge(gain_loaded, 16)
                for g in range(SG):
                    for t in range(NT):
                        v = s_y[:, t, g * 512:(g + 1) * 512]
                        dve.scalar_tensor_tensor(v, v, s_rstd[:, t, g:g + 1], s_gain[:, g * 512:(g + 1) * 512],
                                                 ALU.mult, ALU.mult).then_inc(o_ready, 1)
                for gi in range(SX // 2):
                    rest_of_oT(4, gi)
                residual(at[("so", SX - 1)])

            def top16(rows4):
                def all_four(op):
                    for values, top, idx in rows4:
                        last = op(values, top, idx)
                    return last

                link(all_four(lambda v, top, idx: dve.max(top[:, 0:8], v)))
                all_four(lambda v, top, idx: dve.max_index(idx[:, 0:8], top[:, 0:8], v))
                link(all_four(lambda v, top, idx: dve.match_replace(v, top[:, 0:8], v, NEG)))
                link(all_four(lambda v, top, idx: dve.max(top[:, 8:16], v)))
                return all_four(lambda v, top, idx: dve.max_index(idx[:, 8:16], top[:, 8:16], v))

            def route(lyr):
                for g in range(8):
                    t, first_head = g // 2 % 2, 8 * (g // 4) + 4 * (g % 2)
                    dve.wait_ge(SEM["p_s"], 8 * lyr + g + 1)
                    last = top16([(p_s[:, t, hp, :], p_top[:, t, hp, :], p_idx[:, t, hp, :])
                                  for hp in range(first_head, first_head + 4)])
                link(last)
                link(dve.tensor_copy(flat(p_idxf, "t h k"), flat(p_idx, "t h k")))
                halves = p_top.rearrange("p t (h e) k -> p (t h) e k", e=2)
                first = halves[:, :, 0, :].rearrange("p h (k o) -> p h k o", o=1)
                second = halves[:, :, 1, :].rearrange("p h (o k) -> p h o k", o=1)
                grid = [P, PH, TOPK, TOPK]
                for t in range(NT):
                    hs = slice(t * PH, (t + 1) * PH)
                    link(dve.tensor_tensor(p_cand[:, hs, :].rearrange("p h (a b) -> p h a b", a=TOPK),
                                           first[:, hs].to_broadcast(grid), second[:, hs].to_broadcast(grid), ALU.add))
                for r0 in range(0, NT * PH, 4):
                    last = top16([(p_cand[:, r, :], p_best[:, r, :], p_pos[:, r, :]) for r in range(r0, r0 + 4)])
                link(last)
                dve.tensor_tensor(p_gate, p_best, p_best[:, :, 0:1].to_broadcast([P, NT * PH, TOPK]),
                                  ALU.subtract).then_inc(SEM["p_ex"], 1)
                link(dve.tensor_scalar(p_ab[:, 0], p_pos, 4, None, ALU.logical_shift_right))
                link(dve.tensor_scalar(p_ab[:, 1], p_pos, 15, None, ALU.bitwise_and))
                link(dve.tensor_copy(flat(p_abf, "e h k"), flat(p_ab, "e h k")))
                hot = p_hot.rearrange("p h (k a) -> p h k a", a=TOPK)
                idx = p_idxf.rearrange("p t (h e) k -> p (t h) e k", e=2)
                full = [P, NT * PH, TOPK, TOPK]
                lane = const[:, C_IOTA, 0:TOPK].rearrange("p (o q k) -> p o q k", o=1, q=1)
                for e in range(2):
                    place = p_abf[:, e].rearrange("p h (k o) -> p h k o", o=1)
                    link(dve.tensor_tensor(hot, place.to_broadcast(full), lane.to_broadcast(full), ALU.is_equal))
                    names = idx[:, :, e, :].rearrange("p h (o k) -> p h o k", o=1)
                    link(dve.tensor_tensor(hot, hot, names.to_broadcast(full), ALU.mult))
                    link(dve.tensor_reduce(p_key[:, e], hot, AX.X, ALU.add))
                dve.wait_ge(SEM["p_exd"], lyr + 1)
                link(dve.tensor_reduce(p_sum, p_gate, AX.X, ALU.add))
                link(dve.reciprocal(p_rsum, p_sum))
                dve.tensor_tensor(p_gate, p_gate, wide(p_rsum, TOPK), ALU.mult).then_inc(SEM["p_key"], 1)
                dve.wait_ge(SEM["p_Tps"], lyr + 1)
                dve.tensor_copy(flat(p_T[:, 0:2], "e t"), PS[6][:, :])
                dve.tensor_copy(p_T[:, 2], PS[7][:, 0:T])
                dve.tensor_scalar(p_minus, PS[7][:, 0:T], -1.0, None, ALU.mult).then_inc(SEM["p_Tsb"], 1)
                dve.wait_ge(SEM["p_Tsb"], lyr + 1)

                def one_hots(it, q, first):
                    if not first or q >= 2:
                        dve.wait_ge(SEM["p_mapps"], it * 16 + (T * lyr + 4 * q - 4))
                    keys = p_T[:, 1, bass.ds(it * 16 + 4 * q, 4)].rearrange("p (t o) -> p t o", o=1).to_broadcast([P, 4, P])
                    dve.tensor_tensor(p_B[q % 2], rows(iota, 4), keys, ALU.is_equal).then_inc(SEM["p_hotB"], 1)
                    for e in range(2):
                        tok = bass.ds(it * 16 + (4 * q + e), 1)
                        dve.tensor_scalar(p_A[:, 4 * (q % 2) + e, :], iota, p_T[:, 0, tok], p_T[:, 2, tok],
                                          ALU.is_equal, ALU.mult).then_inc(SEM["p_hot"], 1)

                def gate_early(it, q):
                    dve.wait_ge(SEM["p_map"], it * 4 + (64 * lyr + q + 1))
                    v = p_map[:, 0:EARLY, bass.ds(it * 16 + 4 * q, 4)]
                    dve.tensor_tensor(v, PS[q % 4][:, :].rearrange("p (t i) -> p i t", t=4)[:, 0:EARLY, :], v,
                                      ALU.mult).then_inc(SEM["p_mul"], 1)

                def tokens16(it, first=False):
                    for q in range(4):
                        one_hots(it, q, first)
                        if not first or q >= 2:
                            gate_early(it, q - 2)

                dve.wait_ge(SEM["p_gelu"], P * lyr + EARLY)
                tokens16(0, True)
                with dve.Fori(1, T // 16) as it:
                    tokens16(it)
                gate_early(T // 16, -2)
                gate_early(T // 16, -1)

            def experts(lyr):
                n0 = tables[lyr]
                n1, n2, n3 = n0 + EARLY, n0 + 2 * EARLY, n0 + 2 * P
                i0 = EARLY

                def parts(i, v, it=0, tiles=0):
                    link_in_loop(dve.tensor_copy(p_ag[0][:, i % 2, :], v), it, tiles, P * lyr + i)
                    dve.tensor_tensor(p_ag[1][:, i % 2, :], v, p_ag[0][:, i % 2, :].bitcast(F32),
                                      ALU.subtract).then_inc(SEM["p_ag"], 1)

                def link_in_loop(ins, it, tiles, count):
                    ins.then_inc(SEM["p_ag_hi"], 1)
                    dve.wait_ge(SEM["p_ag_hi"], it * tiles + (count + 1))

                def early(i, it=0, tiles=0):
                    if tiles or i >= 2:
                        dve.wait_ge(half_used, it * 8 + 2 * (n1 + i - 1))
                    row = flat(p_map[:, bass.ds(it * tiles + i, 1), :], "i t") if tiles else p_map[:, i, :]
                    parts(i, row, it, tiles)

                def late(i, it=0, tiles=0):
                    dve.wait_ge(SEM["p_gelu"], it * tiles + (P * lyr + i + 1))
                    row = flat(p_map[:, bass.ds(it * tiles + i, 1), :], "i t") if tiles else p_map[:, i, :]
                    v = p_act[:, i % 2, :]
                    dve.tensor_tensor(v, v, row, ALU.mult).then_inc(SEM["p_gated"], 1)
                    dve.wait_ge(SEM["p_gated"], it * tiles + ((P - EARLY) * lyr + i - EARLY + 1))
                    parts(i, v, it, tiles)

                dve.wait_ge(SEM["p_mul"], 64 * (lyr + 1))
                early(0)
                early(1)
                dve.wait_ge(lo_ready, 2 * (n1 + 2))
                with dve.Fori(0, EARLY // 4 - 1) as it:
                    for i in range(4):
                        rest_of_unit(n1 + i + 2, it, 8)
                        early(i + 2, it, 4)
                for i in range(EARLY - 4, EARLY):
                    rest_of_unit(n1 + i + 2)
                    if i + 2 < EARLY:
                        early(i + 2)
                rest_of_unit(n2 + 2)
                late(i0)
                rest_of_unit(n2 + 3)
                late(i0 + 1)
                rest_of_unit(n2 + 4)
                with dve.Fori(0, (P - EARLY) // 2 - 2) as it:
                    for e in range(2):
                        rest_of_unit(n2 + 5 + 2 * e, it, 8)
                        late(i0 + 2 + e, it, 2)
                        rest_of_unit(n2 + 6 + 2 * e, it, 8)
                rest_of_unit(n3 - 3)
                late(P - 2)
                rest_of_unit(n3 - 2)
                rest_of_unit(n3 - 1)
                late(P - 1)
                residual(n3 - 1)

            dve.wait_ge(x_loaded, 16)
            norm(0)
            gdn()
            norm(1)
            route(0)
            experts(0)
            norm(2)
            ssd()
            norm(3)
            route(1)
            experts(1)
            norm_stats(4)
            dve.wait_ge(last_gain_loaded, 16)
            for t in range(NT):
                ins = dve.scalar_tensor_tensor(x_sb[:, t, :], x_sb[:, t, :], n_rstd[:, t:t + 1], last_gain, ALU.mult, ALU.mult)
            ins.then_inc(SEM["finished"], 1)

        @block.scalar
        def _(act):
            def copy(o, i, scale=1.0):
                return act.activation(o, i, ACT.Copy, scale=scale)

            def split_half(n, hf, it=0, step=0):
                if n >= len(order):
                    return
                if hf == 0:
                    act.wait_ge(landed[n % RING], it * (step * 16 // (2 * RING)) + 16 * (n // RING + 1))
                if 2 * n + hf >= SPLIT:
                    act.wait_ge(half_used, it * step + (2 * n + hf + 1 - SPLIT))
                copy(w_part[0][:, (2 * n + hf) % SPLIT, :], ring[:, n % RING, hf * 512:(hf + 1) * 512]).then_inc(hi_ready, 1)

            def split(n, it=0, step=0):
                for hf in range(2):
                    split_half(n, hf, it, step)

            def norm_squares(i):
                if i:
                    act.activation(n_idle, n_root, ACT.Sqrt)
                for t in range(NT):
                    if i:
                        act.wait_ge(x_added, 4 * i - 2 + 2 * t)
                    act.activation(h_junk, x_sb[:, t, :], ACT.Square, accum_out=n_ss[:, t:t + 1]).then_inc(n_sq, 1)
                    act.wait_ge(n_sq, 2 * i + t + 1)
                act.wait_ge(n_mean, i + 1)
                act.activation(n_root, n_ms, ACT.Sqrt).then_inc(n_rooted, 1)

            def norm(i):
                if i == 0:
                    act.wait_ge(x_loaded, 16)
                norm_squares(i)
                if i == 0:
                    split(0)
                    split(1)
                    act.wait_ge(const_loaded, 32)
                for k in range(KD):
                    act.wait_ge(n_hTps, 4 * i + k // 2 + 1)
                    copy(hT[0][:, k, :], PS[k // 2][:, (k % 2) * T:(k % 2 + 1) * T], norm_w[:, i, k:k + 1]).then_inc(n_hT, 1)

            def rows_out(heads):
                copy(row[0][0:heads, :], PS[2][0:heads, :]).then_inc(row_hi, 1)
                copy(pick, const[0:SH, C_EYE, 0:SH]).then_inc(picks, 1)

            def softplus_tail(ab, exps, n):
                act.activation(ab, ab, ACT.Exp).then_inc(exps, 1)
                act.wait_ge(exps, n)
                return act.activation(ab, ab, ACT.Ln, bias=1.0)

            def gdn():
                for hf in range(2):
                    for q in range(KD // 2):
                        split(at[("gz", hf, q)] + 2)
                    act.wait_ge(half_used, 2 * (at[("gz", hf, 3)] + 1))
                    for t in range(NT):
                        act.activation(g_siluz[:, t, hf * 512:(hf + 1) * 512], PS[4 + 2 * hf + t][:, :], ACT.Silu).then_inc(SEM["g_zs"], 1)
                act.wait_ge(small_loaded, 16 * N_SMALL)
                act.wait_ge(SEM["g_gateb"], 1)
                act.activation(g_beta, PS[2][:, 0:64].rearrange("p (t c) -> p t c", t=NT)[:, :, 16:32], ACT.Sigmoid).then_inc(SEM["g_betas"], 1)
                act.activation(g_nega, g_alog, ACT.Exp)
                softplus_tail(g_ab, SEM["g_gexp"], 1).then_inc(SEM["g_gact"], 1)

                def silu(m):
                    act.wait_ge(SEM["g_conved"], m + 1)
                    act.activation(g_feat[:, m, :], g_acc[:, m % 4, :], ACT.Silu).then_inc(SEM["g_silued"], 1)

                act.wait_ge(SEM["g_pads"], 1)
                for m in range(GC):
                    split_half(at[("gq", m)] + 2, 0)
                    act.wait_ge(half_used, 2 * (at[("gq", m)] + 1))
                    if m >= 4:
                        act.wait_ge(SEM["g_conved"], m - 3)
                    copy(g_pad[:, m % 4, 2:2 + T], PS[m % 2][:, 0:T]).then_inc(SEM["g_padded"], 1)
                    split_half(at[("gq", m)] + 2, 1)
                    if m:
                        silu(m - 1)
                    if m >= 7 and m % 2 and (m - 7) // 2 < GH:
                        gi = (m - 7) // 2
                        act.wait_ge(SEM["g_toksb"], gi + 1)
                        if gi:
                            act.wait_ge(SEM["g_sqsum"], gi)
                        for t in range(NT):
                            for e in range(2):
                                last = act.activation(h_junk[:, (2 * t + e) * P:(2 * t + e + 1) * P], g_tok[:, t, 2 * gi + e, :],
                                                      ACT.Square, accum_out=g_ss[:, t, 2 * gi + e:2 * gi + e + 1])
                        last.then_inc(SEM["g_sqsum"], 1)
                silu(GC - 1)
                act.wait_ge(SEM["g_cumsb"], 1)
                act.activation(g_eg, g_gc, ACT.Exp).then_inc(SEM["g_exps"], 1)
                act.activation(g_wx, g_gt, ACT.Exp).then_inc(SEM["g_exps"], 1)
                rows_out(GH)
                act.wait_ge(SEM["g_mean"], 1)
                act.activation(g_root, g_ms, ACT.Sqrt).then_inc(SEM["g_root"], 1)
                for gi in range(GH):
                    act.wait_ge(SEM["g_backps"], gi + 1)
                    copy(g_feat[:, 2 * gi:2 * gi + 2, :], PS[4 + gi % 4][:, :].rearrange("p (e t) -> p e t", e=2)).then_inc(SEM["g_backsb"], 1)
                for h in range(GH):
                    act.wait_ge(SEM["g_logE"], h + 1)
                    act.activation(g_E[:, h, :], g_E[:, h, :], ACT.Exp).then_inc(SEM["g_E"], 1)
                def T_out(n):
                    act.wait_ge(SEM["g_Tps"], n + 1)
                    t = 4 * (n % GB)
                    copy(g_T[:, t:t + 4, :], PS[4 + n % 2][:, :].rearrange("p (s d) -> p s d", s=4)).then_inc(SEM["g_T"], 1)

                for n in range(3, LEVELS * GB):
                    b = n % GB
                    if n >= GB:
                        act.wait_ge(SEM["g_Yps"], n - GB + 1)
                        copy(g_Y[:, 4 * b:4 * b + 4, :], PS[n % 2][:, :].rearrange("p (s d) -> p s d", s=4)).then_inc(SEM["g_Y"], 1)
                    if n - 3 < (LEVELS - 1) * GB:
                        T_out(n - 3)
                for q4 in range(4):
                    act.wait_ge(SEM["g_S1ps"], q4 + 1)
                    copy(g_S[:, 4 * q4:4 * q4 + 4, :], PS[4 + q4][:, :].rearrange("p (s d) -> p s d", s=4)).then_inc(SEM["g_S1"], 1)
                for t in range(NT):
                    for s in range(t * GH, (t + 1) * GH):
                        if s % 4 == 0:
                            act.wait_ge(SEM["g_O"], s // 4 + 1)
                        last = act.activation(g_sq[:, s, :], g_o[:, s, :], ACT.Square, accum_out=g_ss[:, 0, s:s + 1])
                    last.then_inc(SEM["g_osum"], 1)
                    act.wait_ge(SEM["g_omean"], t + 1)
                    s = slice(t * GH, (t + 1) * GH)
                    act.activation(g_root[:, 0, s], g_ms[:, 0, s], ACT.Sqrt).then_inc(SEM["g_oroot"], 1)
                for b in range(4):
                    act.wait_ge(oT_psum, b + 1)
                    copy(hT[0][:, 2 * b:2 * b + 2, :], PS[b][:, :].rearrange("p (e t) -> p e t", e=2)).then_inc(oT_ready, 1)
                for k in range(GH):
                    split(at[("go", k)] + 2)

            def ssd():
                act.activation(s_nega, s_alog, ACT.Exp)
                act.wait_ge(SEM["s_gateb"], 1)
                softplus_tail(s_ab, SEM["s_gexp"], 1).then_inc(SEM["s_gact"], 1)

                def silu(m):
                    act.wait_ge(SEM["s_conved"], m + 1)
                    act.activation(s_feat[:, m, :], s_acc[:, m % 4, :], ACT.Silu, bias=s_cbias[:, m:m + 1]).then_inc(SEM["s_silued"], 1)

                act.wait_ge(SEM["s_pads"], 1)
                for m in range(SC):
                    split_half(at[("sx", m)] + 2, 0)
                    act.wait_ge(half_used, 2 * (at[("sx", m)] + 1))
                    if m >= 4:
                        act.wait_ge(SEM["s_conved"], m - 3)
                    copy(s_pad[:, m % 4, 2:2 + T], PS[m % 2][:, 0:T]).then_inc(SEM["s_padded"], 1)
                    split_half(at[("sx", m)] + 2, 1)
                    if m:
                        silu(m - 1)
                silu(SC - 1)
                act.wait_ge(SEM["s_cum"], 1)
                rows_out(SH)
                act.wait_ge(SEM["s_nac"], 1)
                act.wait_ge(SEM["s_toksb"], SX // 2)

                def group_gate(g):
                    act.wait_ge(half_used, 2 * (at[("sz", g, 3)] + 1))
                    for t in range(NT):
                        act.activation(s_siluz[:, t, g * 512:(g + 1) * 512], PS[6 + t][:, :], ACT.Silu).then_inc(SEM["s_zs"], 1)

                def group_squares(g):
                    for t in range(NT):
                        act.wait_ge(SEM["s_yg"], 2 * g + t + 1)
                        act.activation(s_junk, s_y[:, t, g * 512:(g + 1) * 512], ACT.Square,
                                       accum_out=s_ss[:, t, g:g + 1]).then_inc(SEM["s_ss"], 1)
                        act.wait_ge(SEM["s_ss"], 2 * g + t + 1)

                for h in range(SH):
                    act.wait_ge(SEM["s_bc"], h + 1)
                    if h >= 2:
                        act.wait_ge(SEM["s_m"], h - 1)
                    act.wait_ge(SEM["s_d"], h + 1)
                    act.activation(s_E[:, h % 2, 0, 2, :], PS[h % 2][:, P:2 * P], ACT.Exp, bias=s_nac[:, 0, h:h + 1])
                    act.activation(s_E[:, h % 2, 1, 2, :], PS[h % 2][:, T:T + P], ACT.Exp, bias=s_nac[:, 1, SH + h:SH + h + 1])
                    v = s_E[:, h % 2, :, 0:2, :].rearrange("p t e d -> p t (e d)")
                    act.activation(v, v, ACT.Exp).then_inc(SEM["s_e"], 1)
                    o = slice(h * SP_, (h + 1) * SP_)
                    copy(s_skip[:, :, o], s_tok[:, :, o], s_D[:, h:h + 1]).then_inc(SEM["s_skip"], 1)
                    split_half(at[("sz", 0, 0)] + h // 2 + 2, h % 2)
                    if h % SR == SR - 1:
                        group_gate(h // SR)
                    if h > SR and h % SR == 5:
                        group_squares(h // SR - 1)
                act.activation(n_idle, n_root, ACT.Sqrt)
                group_squares(SG - 1)
                act.wait_ge(SEM["s_mean"], 1)
                act.activation(s_root, s_ms, ACT.Sqrt).then_inc(SEM["s_root"], 1)
                def y_out(gi):
                    act.wait_ge(oT_psum, 4 + gi + 1)
                    b = gi % 4
                    copy(hT[0][:, 2 * b:2 * b + 2, :], PS[b][:, :].rearrange("p (e t) -> p e t", e=2)).then_inc(oT_ready, 1)

                for gi in range(4):
                    y_out(gi)
                for k in range(SX):
                    split(at[("so", k)] + 2)
                    if k % 2 and k // 2 + 4 < SX // 2:
                        y_out(k // 2 + 4)

            def route(lyr):
                for m in range(HP):
                    split_half(at[("pq", lyr, m)] + 2, 0)
                    act.wait_ge(half_used, 2 * (at[("pq", lyr, m)] + 1))
                    copy(p_qT[:, m, :], PS[4 + m % 2][:, 0:T]).then_inc(SEM["p_q"], 1)
                    split_half(at[("pq", lyr, m)] + 2, 1)
                for g in range(8):
                    t, first_head = g // 2 % 2, 8 * (g // 4) + 4 * (g % 2)
                    act.wait_ge(SEM["p_sps"], 8 * lyr + g + 1)
                    copy(p_s[:, t, first_head:first_head + 4, :], PS[2 + g % 4][:, :].rearrange("p (e k) -> p e k", e=4)).then_inc(SEM["p_s"], 1)

            def experts(lyr):
                n0 = tables[lyr]
                n1, n2, n3 = n0 + EARLY, n0 + 2 * EARLY, n0 + 2 * P
                i0 = EARLY

                def early(i, it=0, tiles=0):
                    split_half(n0 + i + 2, 0, it, 8)
                    act.wait_ge(half_used, it * 8 + 2 * (n0 + i + 1))
                    o = flat(p_map[:, bass.ds(it * tiles + i, 1), :], "i t") if tiles else p_map[:, i, :]
                    act.activation(o, PS[i % 2][:, 0:T], ACT.Gelu).then_inc(SEM["p_gelu"], 1)
                    split_half(n0 + i + 2, 1, it, 8)

                def late(i, n, it=0, tiles=0):
                    split_half(n + 2, 0, it, 8)
                    act.wait_ge(half_used, it * 8 + 2 * (n + 1))
                    if tiles or i >= i0 + 2:
                        act.wait_ge(SEM["p_ag"], it * tiles + (P * lyr + i - 1))
                    act.activation(p_act[:, i % 2, :], PS[i % 2][:, 0:T], ACT.Gelu).then_inc(SEM["p_gelu"], 1)
                    split_half(n + 2, 1, it, 8)

                for i in range(4):
                    early(i)
                with act.Fori(0, EARLY // 4 - 2) as it:
                    for i in range(4, 8):
                        early(i, it, 4)
                act.wait_ge(SEM["p_ex"], lyr + 1)
                act.activation(p_gate, p_gate, ACT.Exp).then_inc(SEM["p_exd"], 1)
                for i in range(EARLY - 4, EARLY):
                    early(i)

                def weighed_rows(it, q, first):
                    for e in range(2):
                        tok = bass.ds(it * 16 + (4 * q + 2 + e), 1)
                        act.wait_ge(SEM["p_sq"], it * 4 + (64 * lyr + q + 1))
                        act.activation(p_A[:, 4 * (q % 2) + 2 + e, :], p_sq[:, 2 * (q % 2) + e, :], ACT.Relu,
                                       bias=p_T[:, 2, tok], scale=p_minus[:, tok]).then_inc(SEM["p_hotS"], 1)

                def late_map(it, q):
                    act.wait_ge(SEM["p_mapps"], it * 16 + (T * lyr + 4 * q + 4))
                    copy(p_map[:, EARLY:P, bass.ds(it * 16 + 4 * q, 4)],
                         PS[q % 4][:, :].rearrange("p (t i) -> p i t", t=4)[:, EARLY:P, :]).then_inc(SEM["p_map"], 1)

                def maps16(it, first=False):
                    for q in range(4):
                        weighed_rows(it, q, first)
                        if not first or q:
                            late_map(it, q - 1)

                act.wait_ge(SEM["p_Tsb"], lyr + 1)
                maps16(0, True)
                with act.Fori(1, T // 16) as it:
                    maps16(it)
                late_map(T // 16, -1)
                with act.Fori(0, EARLY // 4) as it:
                    for i in range(4):
                        split(n1 + i + 2, it, 8)
                late(i0, n2)
                late(i0 + 1, n2 + 1)
                split(n2 + 4)
                with act.Fori(0, (P - EARLY) // 2 - 2) as it:
                    for e in range(2):
                        late(i0 + 2 + e, n2 + 3 + 2 * e, it, 2)
                        split(n2 + 6 + 2 * e, it, 8)
                late(P - 2, n3 - 5)
                split(n3 - 2)
                late(P - 1, n3 - 3)
                split(n3)
                split(n3 + 1)

            act.dma_start(const[:, :, :], a["const"]).then_inc(const_loaded, 16)
            act.dma_start(norm_w, a["norms"]).then_inc(const_loaded, 16)
            norm(0)
            gdn()
            norm(1)
            route(0)
            experts(0)
            norm(2)
            ssd()
            norm(3)
            route(1)
            experts(1)
            norm_squares(4)

        @block.gpsimd
        def _(pool):
            def rows(v, n):
                return v.rearrange("p (o c) -> p o c", o=1).to_broadcast([v.shape[0], n, v.shape[1]])

            def wide(v, n):
                return v.rearrange("p (a o) -> p a o", o=1).to_broadcast([v.shape[0], v.shape[1], n])

            loads = [(levels, a["levels"]), (g_conv, a["gdn_conv"]), (g_wg, a["gdn_gates"]),
                     (g_bias, a["gdn_dt_bias"].partition_broadcast(P)), (g_alog, a["gdn_a_log"].partition_broadcast(P)),
                     (g_gain[:, 0, :], a["gdn_norm"].partition_broadcast(P)),
                     (s_conv, a["ssd_conv"]), (s_cbias, a["ssd_conv_b"]),
                     (s_bias, a["ssd_dt_bias"].partition_broadcast(P)), (s_alog, a["ssd_a_log"].partition_broadcast(P)),
                     (s_D, a["ssd_d"].partition_broadcast(P))]
            assert len(loads) == N_SMALL
            for o, i in loads:
                pool.dma_start(o, i).then_inc(small_loaded, 16)

            def rest_of_unit(n, it=0, step=0):
                for hf in range(2):
                    pool.wait_ge(hi_ready, it * step + (2 * n + hf + 1))
                    s = (2 * n + hf) % SPLIT
                    pool.tensor_tensor(w_part[1][:, s, :], ring[:, n % RING, hf * 512:(hf + 1) * 512],
                                       w_part[0][:, s, :].bitcast(F32), ALU.subtract).then_inc(lo_ready, 1)

            def rest_of_units(first, end):
                for n in range(first, end):
                    rest_of_unit(n)

            def early_experts(lyr, start):
                rest_of_units(start, tables[lyr] + 2)
                with pool.Fori(0, EARLY // 4) as it:
                    for q in range(4):
                        rest_of_unit(tables[lyr] + 2 + q, it, 8)

                def squares(it, q, first):
                    if not first or q >= 2:
                        pool.wait_ge(SEM["p_mapps"], it * 16 + (T * lyr + 4 * q - 4))
                    key = p_T[:, 0, bass.ds(it * 16 + (4 * q + 2), 2)].rearrange("p (t o) -> p t o", o=1).to_broadcast([P, 2, P])
                    v = p_sq[:, 2 * (q % 2):2 * (q % 2) + 2, :]
                    pool.tensor_tensor(v, rows(iota, 2), key, ALU.subtract).then_inc(SEM["p_dist"], 1)
                    pool.wait_ge(SEM["p_dist"], it * 4 + (64 * lyr + q + 1))
                    pool.tensor_tensor(v, v, v, ALU.mult).then_inc(SEM["p_sq"], 1)

                pool.wait_ge(SEM["p_Tsb"], lyr + 1)
                for q in range(4):
                    squares(0, q, True)
                with pool.Fori(1, T // 16) as it:
                    for q in range(4):
                        squares(it, q, False)

            def load_keys(lyr):
                pool.wait_ge(x_added, 8 * lyr + 4)
                pool.dma_start(p_kT, a["peer_kT"][lyr]).then_inc(keys_loaded, 16)

            rest_of_units(0, at[("go", 2)])
            pool.wait_ge(small_loaded, 16 * N_SMALL)
            pool.wait_ge(SEM["g_zs"], 4)
            for t in range(NT):
                v = g_siluz[:, t, :].rearrange("p (h d) -> p h d", h=GH)
                pool.tensor_tensor(v, v, rows(g_gain[:, 0, :], GH), ALU.mult).then_inc(SEM["g_gz"], 1)
            for n in range(LEVELS * GB):
                level, b = divmod(n, GB)
                if n < GB:
                    pool.wait_ge(SEM["g_A"], 2 * (b % 4) + 2)
                if n - 2 >= GB:
                    pool.wait_ge(SEM["g_Yps"], n - 2 - GB + 1)
                elif n >= 2:
                    pool.wait_ge(SEM["g_TT"], n - 2 + 1)
                d = b // (GB // 2)
                pool.tensor_tensor(g_mask[:, 4 * (n % 2):4 * (n % 2) + 4, :], g_AT[:, 4 * b:4 * b + 4, :],
                                   rows(levels[:, d * LEVELS + level, :], 4), ALU.mult).then_inc(SEM["g_mask"], 1)
            pool.wait_ge(SEM["g_U0"], 1)
            for q4 in range(4):
                d, h0 = q4 // 2, 4 * (q4 % 2)
                pool.tensor_tensor(g_kS[:, 4 * q4:4 * q4 + 4, :], g_tok[:, d, GH + h0:GH + h0 + 4, :],
                                   wide(g_wx[:, d, d * GH + h0:d * GH + h0 + 4], P), ALU.mult).then_inc(SEM["g_kS"], 1)
            pool.wait_ge(SEM["g_QE"], GH)
            QE = g_E.rearrange("p h (c i) -> p h c i", c=NT)
            for c in range(NT):
                pool.tensor_tensor(g_tok[:, c, 0:GH, :], QE[:, :, c, :], rows(upper, GH), ALU.mult).then_inc(SEM["g_P"], 1)
                pool.tensor_tensor(g_PTb[:, :, c, :], QE[:, :, c, :], rows(lower, GH), ALU.mult).then_inc(SEM["g_P"], 1)
            rest_of_units(at[("go", 2)], at[("pq", 0, 0)])
            load_keys(0)
            early_experts(0, at[("pq", 0, 0)])
            pool.wait_ge(x_added, 8)
            pool.dma_start(s_wg, a["ssd_gates"]).then_inc(s_wg_loaded, 16)
            pool.wait_ge(lo_ready, 2 * at[("sx", 0)])
            rest_of_units(at[("sx", 0)], at[("sz", 0, 2)])
            pool.wait_ge(SEM["s_silued"], SC)
            pool.dma_start(s_gain, a["ssd_norm"].partition_broadcast(P)).then_inc(gain_loaded, 16)
            for h in range(SH):
                pool.wait_ge(SEM["s_e"], h + 1)
                if h >= 2:
                    pool.wait_ge(SEM["s_yps"], h - 1)
                off = s_M[:, h % 2, :, 2, :]
                pool.tensor_tensor(off, s_CB[:, h // SR, :, 2, :], s_E[:, h % 2, :, 2, :], ALU.mult).then_inc(SEM["s_off"], 1)
                pool.wait_ge(SEM["s_off"], h + 1)
                dt = flat(s_dt, "t c")[:, h:h + 3 * SH + 1:3 * SH]
                pool.tensor_tensor(off, off, wide(dt, P), ALU.mult)
                pool.wait_ge(SEM["s_mv"], h + 1)
                m = s_M[:, h % 2]
                pool.tensor_tensor(m[:, :, 0, :], m[:, :, 0, :], m[:, :, 1, :], ALU.add).then_inc(SEM["s_m"], 1)
                if h > SR and h % SR == 4:
                    g = h // SR - 1
                    for t in range(NT):
                        pool.wait_ge(SEM["s_zs"], 2 * g + t + 1)
                        pool.wait_ge(SEM["s_y"], 2 * g + t + 1)
                        v = s_y[:, t, g * 512:(g + 1) * 512]
                        pool.tensor_tensor(v, v, s_siluz[:, t, g * 512:(g + 1) * 512], ALU.mult).then_inc(SEM["s_yg"], 1)
            pool.wait_ge(lo_ready, 2 * at[("so", 2)])
            rest_of_units(at[("so", 2)], at[("pq", 1, 0)])
            load_keys(1)
            early_experts(1, at[("pq", 1, 0)])


def layout(i):
    c = np.ascontiguousarray

    def by_token(w):
        n = w.shape[1] // 512
        return c(w.reshape(KD // 2, 2, P, n, 512).transpose(3, 0, 2, 1, 4).reshape(n, KD // 2, P, D))

    def by_channel(w):
        n = w.shape[1] // P
        return c(w.reshape(KD, P, n, P).transpose(2, 1, 0, 3).reshape(n, P, D))

    def gates(w):
        return c(w.reshape(KD, P, -1).transpose(1, 0, 2))

    def taps(w):
        return c(w.reshape(TAPS, -1, P).transpose(2, 1, 0))

    masks, levels = host_constants()
    g, s = i["gdn_w_in"][0], i["ssd_w_in"][0]
    qkv, ch = GC * P, SC * P
    return {
        "x": c(i["x"][0].reshape(NT, P, D).transpose(1, 0, 2)),
        "const": masks, "levels": levels.astype(np.float16),
        "norms": c(np.stack([i["norm_mix"][0], i["norm_ffn"][0], i["norm_mix"][1], i["norm_ffn"][1]])
                   .reshape(4, KD, P).transpose(2, 0, 1)),
        "norm_final": i["norm_final"],
        "gdn_qkv": by_channel(g[:, :qkv]), "gdn_z": by_token(g[:, qkv:qkv + D]), "gdn_gates": gates(g[:, qkv + D:]),
        "gdn_conv": taps(i["gdn_conv"][0]), "gdn_a_log": c(i["gdn_a_log"][0].reshape(-1)),
        "gdn_dt_bias": c(i["gdn_dt_bias"][0].reshape(-1)), "gdn_norm": c(i["gdn_norm"][0]),
        "gdn_out": c(i["gdn_w_out"][0].reshape(GH, P, D)),
        "ssd_z": by_token(s[:, :SI]), "ssd_xbc": by_channel(s[:, SI:SI + ch]), "ssd_gates": gates(s[:, SI + ch:]),
        "ssd_conv": taps(i["ssd_conv"][0]), "ssd_conv_b": c(i["ssd_conv_b"][0].reshape(SC, P).T),
        "ssd_a_log": c(i["ssd_a_log"][0].reshape(-1)), "ssd_dt_bias": c(i["ssd_dt_bias"][0].reshape(-1)),
        "ssd_d": c(i["ssd_d"][0]), "ssd_norm": c(i["ssd_norm"][0]), "ssd_out": c(i["ssd_w_out"][0].reshape(SX, P, D)),
        "peer_wq": np.stack([by_channel(i["peer_w_q"][n]) for n in range(2)]),
        "peer_kT": c(i["peer_keys"].reshape(2, HP, P, P).transpose(0, 3, 1, 2)),
        "peer_u": c(i["peer_u"].reshape(2, P, P, KD, P).transpose(0, 1, 4, 3, 2).reshape(2, P, P, D)),
        "peer_v": c(i["peer_v"].reshape(2, P, P, D)),
    }


def kernel(**inputs):
    import concourse.bacc as _bacc
    from concourse.bass_utils import run_bass_kernel_spmd as _run

    arrays = layout({k: np.asarray(v) for k, v in inputs.items()})
    nc = _bacc.Bacc("TRN2", target_bir_lowering=False, num_devices=1)
    a = {k: nc.dram_tensor(f"in_{k}", v.shape, mybir.dt.from_np(v.dtype), kind="ExternalInput").ap()
         for k, v in arrays.items()}
    out = nc.dram_tensor("out", (P, NT, D), F32, kind="ExternalOutput").ap()
    hybrid_encoder(nc, a, out)
    r = _run(nc, [{f"in_{k}": v for k, v in arrays.items()}], core_ids=[0])
    got = r.results[0]["out"]
    return np.ascontiguousarray(got.transpose(1, 0, 2)).reshape(1, T, D)
```
